# Optimizing a Trainium2 kernel written in Bass

```python
import math
import jax, jax.numpy as jnp
from jax import lax
import numpy as np
import jax
import jax.numpy as jnp

D_MODEL = 1024
BATCH = 1
SEQ = 512
DEPTH = 1

N_MEM = 256
D_MIX = D_MODEL
D_MLSTM = D_MIX // 2
N_MLSTM_HEADS = 4
MLSTM_HEAD_DIM = D_MLSTM // N_MLSTM_HEADS
MLSTM_CHUNK = 128
CONV_WIDTH = 5
D_GMLP = D_MIX - D_MLSTM
N_GMLP_GROUPS = 4
GMLP_GROUP_DIM = D_GMLP // N_GMLP_GROUPS
GMLP_CHUNK = 128
N_GATES = 4 * N_MLSTM_HEADS
PROJ_COLS = 4 * D_MLSTM + N_GATES + 2 * D_GMLP
N_XATTN_HEADS = 4
XATTN_HEAD_DIM = D_MODEL // N_XATTN_HEADS
N_EXPERT_GROUPS = 4
EXPERTS_PER_GROUP = 8
N_EXPERTS = N_EXPERT_GROUPS * EXPERTS_PER_GROUP
TOP_K_IN_GROUP = 2
D_EXPERT = D_MODEL // 2
MOE_BLOCK = 128
RMS_EPS = 1e-6
LN_EPS = 1e-5
NEG_INIT = -1e30


def rms_norm(x, g):
    xf = x.astype(jnp.float32)
    y = xf * lax.rsqrt(jnp.mean(xf * xf, axis=-1, keepdims=True) + RMS_EPS)
    return (y * g.astype(jnp.float32)).astype(x.dtype)

def layer_norm(x, g, b):
    xf = x.astype(jnp.float32)
    mu = jnp.mean(xf, axis=-1, keepdims=True)
    xc = xf - mu
    y = xc * lax.rsqrt(jnp.mean(xc * xc, axis=-1, keepdims=True) + LN_EPS)
    return (y * g.astype(jnp.float32) + b.astype(jnp.float32)).astype(x.dtype)

def mlstm_chunkwise(q, k, v, i_pre, f_pre):
    Bq, H, S, dh = q.shape
    L = MLSTM_CHUNK
    NC = S // L
    q = q.reshape(Bq, H, NC, L, dh)
    k = k.reshape(Bq, H, NC, L, dh) * (dh ** -0.5)
    v = v.reshape(Bq, H, NC, L, dh)
    ig = i_pre.reshape(Bq, H, NC, L)
    b = jnp.cumsum(jax.nn.log_sigmoid(f_pre.reshape(Bq, H, NC, L)), axis=-1)
    F = b[..., -1]
    a = F[..., None] - b + ig
    m_loc = jnp.max(a, axis=-1)
    kw = k * jnp.exp(a - m_loc[..., None])[..., None]
    C_loc = jnp.einsum('bhcsd,bhcse->bhcde', kw, v)
    n_loc = jnp.sum(kw, axis=-2)

    def step(carry, inp):
        C, n, m = carry
        F_c, m_c, C_c, n_c = inp
        m_new = jnp.maximum(F_c + m, m_c)
        s_old = jnp.exp(F_c + m - m_new)
        s_new = jnp.exp(m_c - m_new)
        C_new = s_old[..., None, None] * C + s_new[..., None, None] * C_c
        n_new = s_old[..., None] * n + s_new[..., None] * n_c
        return (C_new, n_new, m_new), (C, n, m)

    init = (jnp.zeros((Bq, H, dh, dh), jnp.float32),
            jnp.zeros((Bq, H, dh), jnp.float32),
            jnp.full((Bq, H), NEG_INIT, jnp.float32))
    xs = (jnp.moveaxis(F, 2, 0), jnp.moveaxis(m_loc, 2, 0),
          jnp.moveaxis(C_loc, 2, 0), jnp.moveaxis(n_loc, 2, 0))
    _, (C_prev, n_prev, m_prev) = lax.scan(step, init, xs)
    C_prev = jnp.moveaxis(C_prev, 0, 2)
    n_prev = jnp.moveaxis(n_prev, 0, 2)
    m_prev = jnp.moveaxis(m_prev, 0, 2)

    mask = jnp.tril(jnp.ones((L, L), dtype=bool))
    Dm = jnp.where(mask, b[..., :, None] - b[..., None, :] + ig[..., None, :], -jnp.inf)
    inter = b + m_prev[..., None]
    m_t = jnp.maximum(inter, jnp.max(Dm, axis=-1))
    Wqk = jnp.exp(Dm - m_t[..., None]) * jnp.einsum('bhctd,bhcsd->bhcts', q, k)
    s_inter = jnp.exp(inter - m_t)
    num = (jnp.einsum('bhcts,bhcse->bhcte', Wqk, v)
           + s_inter[..., None] * jnp.einsum('bhctd,bhcde->bhcte', q, C_prev))
    den = jnp.sum(Wqk, axis=-1) + s_inter * jnp.einsum('bhctd,bhcd->bhct', q, n_prev)
    h = num / jnp.maximum(jnp.abs(den), jnp.exp(-m_t))[..., None]
    return h.reshape(Bq, H, S, dh)

def parallel_mixer(h, w_in, conv_w, conv_b, gate_b, g_head, ln_v_g, ln_v_b, w_s, b_s, w_out):
    Bq, S, _ = h.shape
    z = h @ w_in
    cuts = [D_MLSTM, 2 * D_MLSTM, 3 * D_MLSTM, 4 * D_MLSTM,
            4 * D_MLSTM + N_GATES, 4 * D_MLSTM + N_GATES + D_GMLP]
    q, k, v, o, gates, gu, gv = jnp.split(z, cuts, axis=-1)

    qk = lax.conv_general_dilated(jnp.concatenate([q, k], axis=-1), conv_w, (1,), 'SAME',
                                  dimension_numbers=('NWC', 'WIO', 'NWC'),
                                  feature_group_count=2 * D_MLSTM)
    qk = jax.nn.silu(qk + conv_b)
    q, k = qk[..., :D_MLSTM], qk[..., D_MLSTM:]

    def heads(t):
        return t.reshape(Bq, S, N_MLSTM_HEADS, MLSTM_HEAD_DIM).transpose(0, 2, 1, 3).astype(jnp.float32)

    qh, kh, vh = heads(q), heads(k), heads(v)
    g = (gates.astype(jnp.float32) + gate_b.astype(jnp.float32)).reshape(Bq, S, 4, N_MLSTM_HEADS)
    g = g.transpose(2, 0, 3, 1)
    i_f, f_f, i_b, f_b = g[0], g[1], g[2], g[3]

    def flip(t):
        return jnp.flip(t, axis=2)

    h_fwd = mlstm_chunkwise(qh, kh, vh, i_f, f_f)
    h_bwd = flip(mlstm_chunkwise(flip(qh), flip(kh), flip(vh), flip(i_b), flip(f_b)))
    hs = h_fwd + h_bwd
    gh = g_head.astype(jnp.float32).reshape(N_MLSTM_HEADS, 1, MLSTM_HEAD_DIM)
    hs = hs * lax.rsqrt(jnp.mean(hs * hs, axis=-1, keepdims=True) + RMS_EPS) * gh
    hs = hs.transpose(0, 2, 1, 3).reshape(Bq, S, D_MLSTM)
    y_mlstm = (jax.nn.sigmoid(o.astype(jnp.float32)) * hs).astype(h.dtype)

    gu = jax.nn.gelu(gu)
    gv = layer_norm(jax.nn.gelu(gv), ln_v_g, ln_v_b)
    NC = S // GMLP_CHUNK
    gv = gv.reshape(Bq, NC, GMLP_CHUNK, N_GMLP_GROUPS, GMLP_GROUP_DIM)
    sp = jnp.einsum('gts,bcsgd->bctgd', w_s, gv) + b_s.T[:, :, None]
    y_gmlp = gu * sp.reshape(Bq, S, D_GMLP)

    return jnp.concatenate([y_mlstm, y_gmlp], axis=-1) @ w_out

def memory_cross_attention(h, hm, w_q, w_kv, w_o):
    Bq, S, _ = h.shape
    M = hm.shape[1]
    q = (h @ w_q).reshape(Bq, S, N_XATTN_HEADS, XATTN_HEAD_DIM)
    kv = (hm @ w_kv).reshape(Bq, M, 2, N_XATTN_HEADS, XATTN_HEAD_DIM)
    k, v = kv[:, :, 0], kv[:, :, 1]
    s = jnp.einsum('bshd,bmhd->bhsm', q, k).astype(jnp.float32) * (XATTN_HEAD_DIM ** -0.5)
    p = jax.nn.softmax(s, axis=-1).astype(h.dtype)
    o = jnp.einsum('bhsm,bmhd->bshd', p, v).reshape(Bq, S, N_XATTN_HEADS * XATTN_HEAD_DIM)
    return o @ w_o

def hier_moe(h, w_rg, b_rg, w_re, b_re, w_gate, w_up, w_down):
    T, D = h.shape
    g_logits = (h @ w_rg).astype(jnp.float32) + b_rg.astype(jnp.float32)
    p_group = jax.nn.softmax(g_logits, axis=-1)
    p_top, g_idx = lax.top_k(p_group, 1)
    e_logits = ((h @ w_re).astype(jnp.float32) + b_re.astype(jnp.float32)).reshape(
        T, N_EXPERT_GROUPS, EXPERTS_PER_GROUP)
    e_logits = jnp.take_along_axis(e_logits, g_idx[:, :, None], axis=1)[:, 0]
    e_top, e_local = lax.top_k(e_logits, TOP_K_IN_GROUP)
    weights = p_top * jax.nn.softmax(e_top, axis=-1)
    expert_id = g_idx * EXPERTS_PER_GROUP + e_local

    A = T * TOP_K_IN_GROUP
    e_flat = expert_id.reshape(A)
    t_flat = jnp.repeat(jnp.arange(T), TOP_K_IN_GROUP)
    w_flat = weights.reshape(A)
    order = jnp.argsort(e_flat)
    e_sorted, t_sorted, w_sorted = e_flat[order], t_flat[order], w_flat[order]
    counts = jnp.bincount(e_flat, length=N_EXPERTS)
    padded = ((counts + MOE_BLOCK - 1) // MOE_BLOCK) * MOE_BLOCK
    start = jnp.cumsum(counts) - counts
    pend = jnp.cumsum(padded)
    pstart = pend - padded
    dest = pstart[e_sorted] + (jnp.arange(A) - start[e_sorted])
    NB = A // MOE_BLOCK + N_EXPERTS
    P = NB * MOE_BLOCK
    x_disp = jnp.zeros((P, D), h.dtype).at[dest].set(h[t_sorted])
    blk_e = jnp.clip(jnp.searchsorted(pend, jnp.arange(NB) * MOE_BLOCK, side='right'), 0, N_EXPERTS - 1)

    def expert_block(args):
        xb, e = args
        return (jax.nn.silu(xb @ w_gate[e]) * (xb @ w_up[e])) @ w_down[e]

    y_disp = lax.map(expert_block, (x_disp.reshape(NB, MOE_BLOCK, D), blk_e)).reshape(P, D)
    contrib = (w_sorted[:, None] * y_disp[dest].astype(jnp.float32))
    out = jnp.zeros((T, D), jnp.float32).at[t_sorted].add(contrib)
    return out.astype(h.dtype)

def first_inputs(seed: int = 0) -> dict:
    key = jax.random.key(seed)
    ks = jax.random.split(key, 32)

    def nrm(k, shape, scale):
        return jax.random.normal(k, shape, jnp.float32) * scale

    def gain(k, shape):
        return 1.0 + 0.1 * jax.random.normal(k, shape, jnp.float32)

    H = N_MLSTM_HEADS
    f_bias = jnp.linspace(3.0, 6.0, H, dtype=jnp.float32)
    gk = jax.random.split(ks[6], 4)
    gate_b = jnp.concatenate([
        nrm(gk[0], (DEPTH, H), 0.1),
        f_bias + nrm(gk[1], (DEPTH, H), 0.1),
        nrm(gk[2], (DEPTH, H), 0.1),
        f_bias + nrm(gk[3], (DEPTH, H), 0.1)], axis=-1)
    return {
        'x': nrm(ks[0], (BATCH, SEQ, D_MODEL), 1.0),
        'mem': nrm(ks[1], (BATCH, N_MEM, D_MODEL), 1.0),
        'g_mix': gain(ks[2], (DEPTH, D_MODEL)),
        'w_in': nrm(ks[3], (DEPTH, D_MODEL, PROJ_COLS), D_MODEL ** -0.5),
        'conv_w': nrm(ks[4], (DEPTH, CONV_WIDTH, 1, 2 * D_MLSTM), CONV_WIDTH ** -0.5),
        'conv_b': nrm(ks[5], (DEPTH, 2 * D_MLSTM), 0.01),
        'gate_b': gate_b,
        'g_head': gain(ks[7], (DEPTH, D_MLSTM)),
        'ln_v_g': gain(ks[8], (DEPTH, D_GMLP)),
        'ln_v_b': nrm(ks[9], (DEPTH, D_GMLP), 0.01),
        'w_s': nrm(ks[10], (DEPTH, N_GMLP_GROUPS, GMLP_CHUNK, GMLP_CHUNK), GMLP_CHUNK ** -0.5),
        'b_s': gain(ks[11], (DEPTH, N_GMLP_GROUPS, GMLP_CHUNK)),
        'w_out': nrm(ks[12], (DEPTH, D_MIX, D_MODEL), D_MIX ** -0.5),
        'g_xattn': gain(ks[13], (DEPTH, D_MODEL)),
        'g_mem': gain(ks[14], (DEPTH, D_MODEL)),
        'w_q_x': nrm(ks[15], (DEPTH, D_MODEL, N_XATTN_HEADS * XATTN_HEAD_DIM), D_MODEL ** -0.5),
        'w_kv_x': nrm(ks[16], (DEPTH, D_MODEL, 2 * N_XATTN_HEADS * XATTN_HEAD_DIM), D_MODEL ** -0.5),
        'w_o_x': nrm(ks[17], (DEPTH, N_XATTN_HEADS * XATTN_HEAD_DIM, D_MODEL), D_MODEL ** -0.5),
        'g_moe': gain(ks[18], (DEPTH, D_MODEL)),
        'w_rg': nrm(ks[19], (DEPTH, D_MODEL, N_EXPERT_GROUPS), D_MODEL ** -0.5),
        'b_rg': nrm(ks[20], (DEPTH, N_EXPERT_GROUPS), 0.01),
        'w_re': nrm(ks[21], (DEPTH, D_MODEL, N_EXPERTS), D_MODEL ** -0.5),
        'b_re': nrm(ks[22], (DEPTH, N_EXPERTS), 0.01),
        'w_gate': nrm(ks[23], (DEPTH, N_EXPERTS, D_MODEL, D_EXPERT), D_MODEL ** -0.5),
        'w_up': nrm(ks[24], (DEPTH, N_EXPERTS, D_MODEL, D_EXPERT), D_MODEL ** -0.5),
        'w_down': nrm(ks[25], (DEPTH, N_EXPERTS, D_EXPERT, D_MODEL), D_EXPERT ** -0.5),
        'g_final': gain(ks[26], (D_MODEL,)),
    }

def first_block(x, mem, g_mix, w_in, conv_w, conv_b, gate_b, g_head, ln_v_g, ln_v_b, w_s, b_s, w_out,
              g_xattn, g_mem, w_q_x, w_kv_x, w_o_x, g_moe, w_rg, b_rg, w_re, b_re,
              w_gate, w_up, w_down, g_final):
    Bq, S, D = x.shape
    for l in range(DEPTH):
        x = x + parallel_mixer(rms_norm(x, g_mix[l]), w_in[l], conv_w[l], conv_b[l], gate_b[l],
                               g_head[l], ln_v_g[l], ln_v_b[l], w_s[l], b_s[l], w_out[l])
        x = x + memory_cross_attention(rms_norm(x, g_xattn[l]), rms_norm(mem, g_mem[l]),
                                       w_q_x[l], w_kv_x[l], w_o_x[l])
        x = x + hier_moe(rms_norm(x, g_moe[l]).reshape(Bq * S, D), w_rg[l], b_rg[l], w_re[l], b_re[l],
                         w_gate[l], w_up[l], w_down[l]).reshape(Bq, S, D)
    return rms_norm(x, g_final)


DEPTH_2 = 2

N_BRANCH = 4
BRANCH_WIDTH = 256
HEAD_DIM = 64
N_HEADS = BRANCH_WIDTH // HEAD_DIM
MLA_Q_RANK = 256
MLA_KV_RANK = 128
MLA_NOPE_DIM = 64
MLA_ROPE_DIM = 32
MLA_V_DIM = BRANCH_WIDTH // N_HEADS
ROPE_BASE = 10000.0
CONV_CH = BRANCH_WIDTH
CONV_WIDTH_2 = 31
FORGET_BIAS_INIT = 3.0
Q_BLOCK = 128
N_GROUPS = 4
N_EXPERTS_2 = N_GROUPS * EXPERTS_PER_GROUP
TOP_K = 2
EXPERT_FF = 256
ROW_BLOCK = 128
NORM_EPS = 1e-5
IN_SPLITS = (MLA_Q_RANK, MLA_KV_RANK, MLA_ROPE_DIM, 3 * BRANCH_WIDTH, 2 * CONV_CH, 3 * BRANCH_WIDTH, N_HEADS, N_BRANCH * D_MODEL)
N_IN = sum(IN_SPLITS)


def _layernorm(x, g, b):
    xf = x.astype(jnp.float32)
    mu = jnp.mean(xf, axis=-1, keepdims=True)
    var = jnp.mean(jnp.square(xf - mu), axis=-1, keepdims=True)
    y = (xf - mu) * lax.rsqrt(var + NORM_EPS) * g.astype(jnp.float32) + b.astype(jnp.float32)
    return y.astype(x.dtype)

def _rmsnorm(x, g):
    xf = x.astype(jnp.float32)
    y = xf * lax.rsqrt(jnp.mean(xf * xf, axis=-1, keepdims=True) + NORM_EPS) * g.astype(jnp.float32)
    return y.astype(x.dtype)

def _rope(x, positions):
    half = x.shape[-1] // 2
    inv = ROPE_BASE ** (-jnp.arange(half, dtype=jnp.float32) / half)
    ang = (positions.astype(jnp.float32)[..., None] * inv)[:, :, None, :]
    cos, sin = jnp.cos(ang), jnp.sin(ang)
    x1 = x[..., :half].astype(jnp.float32)
    x2 = x[..., half:].astype(jnp.float32)
    out = jnp.concatenate([x1 * cos - x2 * sin, x2 * cos + x1 * sin], axis=-1)
    return out.astype(x.dtype)

def _split_cols(z):
    idx = [int(i) for i in np.cumsum(IN_SPLITS)[:-1]]
    return jnp.split(z, idx, axis=-1)

def _split_heads(qkv):
    b, s, _ = qkv.shape
    qkv = qkv.reshape(b, s, 3, N_HEADS, HEAD_DIM).transpose(2, 0, 3, 1, 4)
    return qkv[0], qkv[1], qkv[2]

def _merge_heads(o):
    b, h, s, d = o.shape
    return o.transpose(0, 2, 1, 3).reshape(b, s, h * d)

def _sweep_query_blocks(block_fn, q_side):
    b, h, s = q_side[0].shape[:3]
    nb = s // Q_BLOCK
    blocks = tuple(jnp.moveaxis(a.reshape((b, h, nb, Q_BLOCK) + a.shape[3:]), 2, 0) for a in q_side)
    t_pos = jnp.arange(s, dtype=jnp.int32).reshape(nb, Q_BLOCK)
    out = lax.map(lambda args: block_fn(*args), (t_pos,) + blocks)
    return jnp.moveaxis(out, 0, 2).reshape(b, h, s, out.shape[-1])

def _mla(c_q, c_kv, k_rope_raw, positions, q_norm, kv_norm, w_uq, w_ukv):
    b, s, _ = c_q.shape
    q = (_rmsnorm(c_q, q_norm) @ w_uq).reshape(b, s, N_HEADS, MLA_NOPE_DIM + MLA_ROPE_DIM)
    q_nope = q[..., :MLA_NOPE_DIM].transpose(0, 2, 1, 3)
    q_rope = _rope(q[..., MLA_NOPE_DIM:], positions).transpose(0, 2, 1, 3)
    kv = (_rmsnorm(c_kv, kv_norm) @ w_ukv).reshape(b, s, N_HEADS, MLA_NOPE_DIM + MLA_V_DIM)
    k_nope = kv[..., :MLA_NOPE_DIM].transpose(0, 2, 1, 3)
    v = kv[..., MLA_NOPE_DIM:].transpose(0, 2, 1, 3)
    k_rope = _rope(k_rope_raw[:, :, None, :], positions)[:, :, 0, :]
    scale = (MLA_NOPE_DIM + MLA_ROPE_DIM) ** -0.5
    key_pos = jnp.arange(s, dtype=jnp.int32)

    def block(t_pos, qn, qr):
        logits = jnp.einsum('bhqd,bhkd->bhqk', qn, k_nope) + jnp.einsum('bhqr,bkr->bhqk', qr, k_rope)
        logits = logits.astype(jnp.float32) * scale
        logits = jnp.where(key_pos[None, :] <= t_pos[:, None], logits, -jnp.inf)
        p = jax.nn.softmax(logits, axis=-1).astype(v.dtype)
        return jnp.einsum('bhqk,bhkd->bhqd', p, v)

    return _merge_heads(_sweep_query_blocks(block, (q_nope, q_rope)))

def _stick_breaking(q, k, v):
    s = k.shape[2]
    scale = HEAD_DIM ** -0.5
    key_pos = jnp.arange(s, dtype=jnp.int32)

    def block(t_pos, qb):
        z = jnp.einsum('bhqd,bhkd->bhqk', qb, k).astype(jnp.float32) * scale
        strict = key_pos[None, :] < t_pos[:, None]
        log_stay = jnp.where(strict, jax.nn.log_sigmoid(-z), 0.0)
        after = lax.cumsum(log_stay, axis=3, reverse=True) - log_stay
        a = jnp.where(strict, jnp.exp(jax.nn.log_sigmoid(z) + after), 0.0).astype(v.dtype)
        return jnp.einsum('bhqk,bhkd->bhqd', a, v)

    return _merge_heads(_sweep_query_blocks(block, (q,)))

def _conformer_conv(u, conv_w, conv_b, ln_g, ln_b):
    a, g = jnp.split(u, 2, axis=-1)
    h = a * jax.nn.sigmoid(g)
    hp = jnp.pad(h, ((0, 0), (CONV_WIDTH_2 - 1, 0), (0, 0)))
    y = lax.conv_general_dilated(hp, conv_w[:, None, :], window_strides=(1,), padding='VALID',
                                 dimension_numbers=('NWC', 'WIO', 'NWC'), feature_group_count=CONV_CH)
    y = _layernorm(y + conv_b, ln_g, ln_b)
    return jax.nn.silu(y)

def _forgetting_attention(q, k, v, forget_logit, b_forget):
    s = k.shape[2]
    scale = HEAD_DIM ** -0.5
    log_f = jax.nn.log_sigmoid((forget_logit + b_forget).astype(jnp.float32))
    c = jnp.cumsum(log_f, axis=1).transpose(0, 2, 1)
    key_pos = jnp.arange(s, dtype=jnp.int32)

    def block(t_pos, qb, cb):
        logits = jnp.einsum('bhqd,bhkd->bhqk', qb, k).astype(jnp.float32) * scale
        logits = logits + cb[..., None] - c[:, :, None, :]
        logits = jnp.where(key_pos[None, :] <= t_pos[:, None], logits, -jnp.inf)
        p = jax.nn.softmax(logits, axis=-1).astype(v.dtype)
        return jnp.einsum('bhqk,bhkd->bhqd', p, v)

    return _merge_heads(_sweep_query_blocks(block, (q, c)))

def _token_mixer(x, positions, w_in, b_gate, b_forget, mla_q_norm, mla_kv_norm, mla_w_uq, mla_w_ukv,
                 conv_w, conv_b, conv_ln_g, conv_ln_b, w_branch, w_o):
    b, s, d = x.shape
    z = x @ w_in
    c_q, c_kv, k_rope, sb_qkv, conv_in, fox_qkv, fox_f, gate_logits = _split_cols(z)
    y_a = _mla(c_q, c_kv, k_rope, positions, mla_q_norm, mla_kv_norm, mla_w_uq, mla_w_ukv)
    y_b = _stick_breaking(*_split_heads(sb_qkv))
    y_c = _conformer_conv(conv_in, conv_w, conv_b, conv_ln_g, conv_ln_b)
    y_d = _forgetting_attention(*_split_heads(fox_qkv), fox_f, b_forget)
    ys = jnp.stack([y_a, y_b, y_c, y_d], axis=2)
    gates = jax.nn.sigmoid(gate_logits + b_gate).reshape(b, s, N_BRANCH, d)
    proj = jnp.einsum('bsnc,ncd->bsnd', ys, w_branch)
    merged = jnp.sum(proj * gates, axis=2)
    return merged @ w_o

def _hier_moe(h, w_rg, b_rg, w_re, b_re, w_gate, w_up, w_down):
    b, s, d = h.shape
    xt = h.reshape(-1, d)
    n_tok = xt.shape[0]
    grp_prob = jax.nn.softmax((xt @ w_rg + b_rg).astype(jnp.float32), axis=-1)
    grp_p, grp_idx = lax.top_k(grp_prob, 1)
    exp_logits = (xt @ w_re + b_re).astype(jnp.float32).reshape(n_tok, N_GROUPS, EXPERTS_PER_GROUP)
    in_grp = jnp.take_along_axis(exp_logits, grp_idx[:, :, None], axis=1)[:, 0]
    top_p, top_i = lax.top_k(jax.nn.softmax(in_grp, axis=-1), TOP_K)
    weights = grp_p * top_p / jnp.sum(top_p, axis=-1, keepdims=True)
    expert_id = (grp_idx * EXPERTS_PER_GROUP + top_i).reshape(-1)
    n_assign = expert_id.shape[0]
    order = jnp.argsort(expert_id).astype(jnp.int32)
    sorted_e = expert_id[order]
    counts = jnp.bincount(expert_id, length=N_EXPERTS_2).astype(jnp.int32)
    padded = (counts + ROW_BLOCK - 1) // ROW_BLOCK * ROW_BLOCK
    pad_end = jnp.cumsum(padded)
    pad_start = pad_end - padded
    start = jnp.cumsum(counts) - counts
    slot = pad_start[sorted_e] + jnp.arange(n_assign, dtype=jnp.int32) - start[sorted_e]
    n_blocks = (n_assign + ROW_BLOCK - 1) // ROW_BLOCK + N_EXPERTS_2
    slot_token = jnp.full((n_blocks * ROW_BLOCK,), n_tok, dtype=jnp.int32).at[slot].set(order // TOP_K)
    block_start = jnp.arange(n_blocks, dtype=jnp.int32) * ROW_BLOCK
    block_expert = jnp.minimum(jnp.searchsorted(pad_end, block_start, side='right'), N_EXPERTS_2 - 1)
    x_pad = jnp.concatenate([xt, jnp.zeros((1, d), xt.dtype)], axis=0)
    xb = x_pad[slot_token].reshape(n_blocks, ROW_BLOCK, d)

    def expert_block(args):
        xe, e = args
        hid = jax.nn.silu(xe @ w_gate[e]) * (xe @ w_up[e])
        return hid @ w_down[e]

    yb = lax.map(expert_block, (xb, block_expert)).reshape(-1, d)
    y_assign = jnp.zeros((n_assign, d), yb.dtype).at[order].set(yb[slot])
    y = jnp.einsum('tkd,tk->td', y_assign.reshape(n_tok, TOP_K, d), weights.astype(yb.dtype))
    return y.reshape(b, s, d)

def second_inputs(seed: int = 0) -> dict:
    key = jax.random.key(seed)
    ks = jax.random.split(key, 28)
    L, D = DEPTH_2, D_MODEL
    beta = (8.0 * DEPTH_2) ** -0.25

    def nrm(k, shape, scale):
        return jax.random.normal(k, shape, jnp.float32) * scale

    def gain(k, shape):
        return 1.0 + 0.02 * jax.random.normal(k, shape, jnp.float32)

    offset = jax.random.randint(ks[1], (BATCH, 1), 0, 1024, dtype=jnp.int32)
    positions = offset + jnp.arange(SEQ, dtype=jnp.int32)[None, :]
    return {
        'x': nrm(ks[0], (BATCH, SEQ, D), 1.0),
        'positions': positions,
        'w_in': nrm(ks[2], (L, D, N_IN), D ** -0.5),
        'b_gate': nrm(ks[3], (L, N_BRANCH * D), 0.02),
        'b_forget': FORGET_BIAS_INIT + nrm(ks[4], (L, N_HEADS), 0.1),
        'mla_q_norm': gain(ks[5], (L, MLA_Q_RANK)),
        'mla_kv_norm': gain(ks[6], (L, MLA_KV_RANK)),
        'mla_w_uq': nrm(ks[7], (L, MLA_Q_RANK, N_HEADS * (MLA_NOPE_DIM + MLA_ROPE_DIM)), MLA_Q_RANK ** -0.5),
        'mla_w_ukv': nrm(ks[8], (L, MLA_KV_RANK, N_HEADS * (MLA_NOPE_DIM + MLA_V_DIM)), MLA_KV_RANK ** -0.5),
        'conv_w': nrm(ks[9], (L, CONV_WIDTH_2, CONV_CH), CONV_WIDTH_2 ** -0.5),
        'conv_b': nrm(ks[10], (L, CONV_CH), 0.02),
        'conv_ln_g': gain(ks[11], (L, CONV_CH)),
        'conv_ln_b': nrm(ks[12], (L, CONV_CH), 0.02),
        'w_branch': nrm(ks[13], (L, N_BRANCH, BRANCH_WIDTH, D), BRANCH_WIDTH ** -0.5),
        'w_o': nrm(ks[14], (L, D, D), beta * D ** -0.5),
        'ln1_g': gain(ks[15], (L, D)),
        'ln1_b': nrm(ks[16], (L, D), 0.02),
        'w_router_group': nrm(ks[17], (L, D, N_GROUPS), D ** -0.5),
        'b_router_group': nrm(ks[18], (L, N_GROUPS), 0.01),
        'w_router_expert': nrm(ks[19], (L, D, N_EXPERTS_2), D ** -0.5),
        'b_router_expert': nrm(ks[20], (L, N_EXPERTS_2), 0.01),
        'w_exp_gate': nrm(ks[21], (L, N_EXPERTS_2, D, EXPERT_FF), D ** -0.5),
        'w_exp_up': nrm(ks[22], (L, N_EXPERTS_2, D, EXPERT_FF), D ** -0.5),
        'w_exp_down': nrm(ks[23], (L, N_EXPERTS_2, EXPERT_FF, D), beta * EXPERT_FF ** -0.5),
        'ln2_g': gain(ks[24], (L, D)),
        'ln2_b': nrm(ks[25], (L, D), 0.02),
    }

def second_block(x, positions, w_in, b_gate, b_forget, mla_q_norm, mla_kv_norm, mla_w_uq, mla_w_ukv,
              conv_w, conv_b, conv_ln_g, conv_ln_b, w_branch, w_o, ln1_g, ln1_b,
              w_router_group, b_router_group, w_router_expert, b_router_expert,
              w_exp_gate, w_exp_up, w_exp_down, ln2_g, ln2_b):
    alpha = (2.0 * DEPTH_2) ** 0.25
    for l in range(DEPTH_2):
        mix = _token_mixer(x, positions, w_in[l], b_gate[l], b_forget[l], mla_q_norm[l], mla_kv_norm[l],
                           mla_w_uq[l], mla_w_ukv[l], conv_w[l], conv_b[l], conv_ln_g[l], conv_ln_b[l],
                           w_branch[l], w_o[l])
        x = _layernorm(alpha * x + mix, ln1_g[l], ln1_b[l])
        ffn = _hier_moe(x, w_router_group[l], b_router_group[l], w_router_expert[l], b_router_expert[l],
                        w_exp_gate[l], w_exp_up[l], w_exp_down[l])
        x = _layernorm(alpha * x + ffn, ln2_g[l], ln2_b[l])
    return x


def setup_inputs(seed=0):
    out = dict(first_inputs(seed))
    for name, value in second_inputs(seed + 1).items():
        if name != "x":
            out[name + "_2"] = value
    return out


def reference(
    x, mem, g_mix, w_in, conv_w, conv_b, gate_b, g_head, ln_v_g, ln_v_b, w_s, b_s, w_out,
    g_xattn, g_mem, w_q_x, w_kv_x, w_o_x, g_moe, w_rg, b_rg, w_re, b_re, w_gate, w_up, w_down,
    g_final, positions_2, w_in_2, b_gate_2, b_forget_2, mla_q_norm_2, mla_kv_norm_2, mla_w_uq_2,
    mla_w_ukv_2, conv_w_2, conv_b_2, conv_ln_g_2, conv_ln_b_2, w_branch_2, w_o_2, ln1_g_2,
    ln1_b_2, w_router_group_2, b_router_group_2, w_router_expert_2, b_router_expert_2,
    w_exp_gate_2, w_exp_up_2, w_exp_down_2, ln2_g_2, ln2_b_2,
):
    x = first_block(
        x, mem, g_mix, w_in, conv_w, conv_b, gate_b, g_head, ln_v_g, ln_v_b, w_s, b_s, w_out,
        g_xattn, g_mem, w_q_x, w_kv_x, w_o_x, g_moe, w_rg, b_rg, w_re, b_re, w_gate, w_up,
        w_down, g_final,
    )
    return second_block(
        x, positions_2, w_in_2, b_gate_2, b_forget_2, mla_q_norm_2, mla_kv_norm_2, mla_w_uq_2,
        mla_w_ukv_2, conv_w_2, conv_b_2, conv_ln_g_2, conv_ln_b_2, w_branch_2, w_o_2, ln1_g_2,
        ln1_b_2, w_router_group_2, b_router_group_2, w_router_expert_2, b_router_expert_2,
        w_exp_gate_2, w_exp_up_2, w_exp_down_2, ln2_g_2, ln2_b_2,
    )


_drawn_inputs = setup_inputs


def setup_inputs(seed=0):
    import zlib

    import numpy as np

    out = dict(_drawn_inputs(seed))
    spreads = {}
    factors = {'conv_b': 4.621,
     'ln_v_b': 3.822,
     'b_rg': 3.634,
     'b_re': 4.284,
     'b_gate_2': 8.0,
     'b_forget_2': 64.0,
     'mla_q_norm_2': 8.0,
     'mla_kv_norm_2': 8.0,
     'conv_b_2': 5.443,
     'conv_ln_g_2': 8.0,
     'conv_ln_b_2': 7.07,
     'b_router_group_2': 6.294,
     'b_router_expert_2': 5.291}
    for name, (base, spread) in spreads.items():
        noise = np.random.default_rng([zlib.crc32(name.encode()), seed]).standard_normal(out[name].shape)
        drawn = base * np.exp(spread * noise) if base else spread * noise
        out[name] = jnp.asarray(drawn.astype(out[name].dtype))
    for name, factor in factors.items():
        out[name] = (out[name] * factor).astype(out[name].dtype)
    return out
```

```python
from contextlib import ExitStack

import numpy as np

import concourse.bass as bass
from concourse import mybir
from concourse.alu_op_type import AluOpType as ALU

P = 128
F32 = mybir.dt.float32
I32 = mybir.dt.int32
U32 = mybir.dt.uint32
ACT = mybir.ActivationFunctionType
AX_X = mybir.AxisListType.X
BIG = 1e30
D = 1024
S = 512
DC = D // P
TT = S // P

NE = 32
NG = 4
EPG = NE // NG
SLOTS = 64
MAX_BLOCKS = NE + 2 * S // SLOTS
TABLE = MAX_BLOCKS + 2
ROWS = TABLE * SLOTS


class Stage:

    def __init__(self, nc, name):
        self.nc, self.name, self.stack, self.sems = nc, name, ExitStack(), []

    def __enter__(self):
        return self

    def sb(self, name, shape, dtype=F32):
        return self.stack.enter_context(self.nc.sbuf_tensor(f"{self.name}_{name}", shape, dtype))

    def sem(self, name):
        handle = self.nc.alloc_semaphore(f"{self.name}_{name}")
        self.sems.append(handle)
        return handle

    def __exit__(self, kind, value, trace):
        if kind is None:
            self.nc.clear_and_free_semaphores(self.sems)
            self.nc.all_engine_barrier()
        self.stack.close()
        return False


class Chain:

    def __init__(self, engine, semaphore):
        self.engine, self.semaphore, self.count = engine, semaphore, 0

    def __call__(self, instruction):
        self.count += 1
        instruction.then_inc(self.semaphore, 1)
        self.engine.wait_ge(self.semaphore, self.count)


def cols(ap, n):
    return ap.unsqueeze(len(ap.shape)).to_broadcast(list(ap.shape) + [n])


class Item:

    def __init__(self, chunk, operands, rows, n, engine, out):
        self.chunk, self.operands, self.rows, self.n, self.engine, self.out = chunk, operands, rows, n, engine, out


def dense(nc, name, k, chunks, items, ring=3):
    ps = k["ps"]
    widest = max(c.shape[2] for c in chunks)
    deepest = max(c.shape[1] for c in chunks)
    last_item = {it.chunk: i for i, it in enumerate(items)}
    nth, counts = [], {"act": 0, "dve": 0}
    for it in items:
        counts[it.engine] += 1
        nth.append(counts[it.engine])
    with Stage(nc, name) as st:
        w = st.sb("w", [P, ring, deepest, widest])
        landed = [st.sem(f"weights_landed{i}") for i in range(ring)]
        bank_full = st.sem("bank_full")
        emptied = {"act": st.sem("emptied_by_act"), "dve": st.sem("emptied_by_dve")}
        with nc.Block() as block:
            @block.sync
            def _(sp):
                for c, dram in enumerate(chunks):
                    if c >= ring:
                        sp.wait_ge(bank_full, last_item[c - ring] + 1)
                    sp.dma_start(w[:, c % ring, 0:dram.shape[1], 0:dram.shape[2]], dram).then_inc(landed[c % ring], 16)

            @block.tensor
            def _(pe):
                for i, it in enumerate(items):
                    pe.wait_ge(landed[it.chunk % ring], 16 * (it.chunk // ring + 1))
                    if i >= 8:
                        pe.wait_ge(emptied[items[i - 8].engine], nth[i - 8])
                    pairs = it.operands(w[:, it.chunk % ring])
                    for j, (stationary, moving) in enumerate(pairs):
                        last = nc.tensor.matmul(ps[0:it.rows, i % 8, 0:it.n], stationary, moving,
                                                start=j == 0, stop=j == len(pairs) - 1)
                    last.then_inc(bank_full, 1)

            @block.scalar
            def _(act):
                for i, it in enumerate(items):
                    if it.engine == "act":
                        act.wait_ge(bank_full, i + 1)
                        it.out(nc.scalar, ps[0:it.rows, i % 8, 0:it.n]).then_inc(emptied["act"], 1)

            @block.vector
            def _(dve):
                for i, it in enumerate(items):
                    if it.engine == "dve":
                        dve.wait_ge(bank_full, i + 1)
                        it.out(nc.vector, ps[0:it.rows, i % 8, 0:it.n]).then_inc(emptied["dve"], 1)


def chunk_of(w_dram, a, b):
    return w_dram.rearrange("(c p) n -> p c n", p=P)[:, :, a:b]


def by_token(chunk, hT, t, a, b, engine, out, kc=DC):
    return Item(chunk, lambda w: [(hT[:, c, t * P:(t + 1) * P], w[:, c, a:b]) for c in range(kc)], P, b - a, engine, out)


def by_feature(chunk, hT, a, engine, out, n=S, kc=DC):
    return Item(chunk, lambda w: [(w[:, c, a:a + P], hT[:, c, 0:n]) for c in range(kc)], P, n, engine, out)


def turn(nc, name, k, tiles, src, outs):
    ps = k["ps"]
    with Stage(nc, name) as st:
        full = st.sem("bank_full")
        emptied = [st.sem("emptied_by_act"), st.sem("emptied_by_dve")]
        with nc.Block() as block:
            @block.tensor
            def _(pe):
                for c in range(len(outs)):
                    if c >= 8:
                        pe.wait_ge(emptied[c % 2], (c - 8) // 2 + 1)
                    for t in range(tiles):
                        last = nc.tensor.transpose(ps[:, c % 8, t * P:(t + 1) * P], src(t, c), k["ident"][:])
                    last.then_inc(full, 1)

            @block.scalar
            def _(act):
                for c in range(0, len(outs), 2):
                    act.wait_ge(full, c + 1)
                    outs[c](nc.scalar, ps[:, c % 8, 0:tiles * P]).then_inc(emptied[0], 1)

            @block.vector
            def _(dve):
                for c in range(1, len(outs), 2):
                    dve.wait_ge(full, c + 1)
                    outs[c](nc.vector, ps[:, c % 8, 0:tiles * P]).then_inc(emptied[1], 1)


def plain(nc, out, gain=None):
    def f(eng, src):
        if eng is nc.scalar:
            return eng.activation(out, src, ACT.Identity, scale=1.0 if gain is None else gain)
        if gain is None:
            return eng.tensor_copy(out, src)
        return eng.tensor_scalar(out, src, gain, None, ALU.mult)
    return f


def rms_rows(nc, name, x, h, tiles, width, eps):
    with Stage(nc, name) as st:
        junk = st.sb("junk", [P, width])
        ss = st.sb("ss", [P, 4, tiles])
        squared, mean_ready, root_ready, chain = (st.sem(n) for n in ("squared", "mean_ready", "root_ready", "dve_chain"))
        act_chain = st.sem("act_chain")
        with nc.Block() as block:
            @block.scalar
            def _(act):
                link = Chain(act, act_chain)
                for t in range(tiles):
                    link(nc.scalar.activation(junk[:], x(t), ACT.Square, accum_out=ss[:, 0, t:t + 1]))
                act.sem_inc(squared, 1)
                act.wait_ge(mean_ready, 1)
                nc.scalar.activation(ss[:, 2], ss[:, 1], ACT.Sqrt).then_inc(root_ready, 1)

            @block.vector
            def _(dve):
                link = Chain(dve, chain)
                dve.wait_ge(squared, 1)
                nc.vector.tensor_scalar(ss[:, 1], ss[:, 0], 1.0 / width, eps, ALU.mult, ALU.add).then_inc(mean_ready, 1)
                dve.wait_ge(root_ready, 1)
                link(nc.vector.reciprocal(ss[:, 3], ss[:, 2]))
                for t in range(tiles):
                    nc.vector.tensor_scalar(h(t), x(t), ss[:, 3, t:t + 1], None, ALU.mult)


def ln_rows(nc, name, x, out, tiles, width, eps, rows=None):
    with Stage(nc, name) as st:
        stats = st.sb("stats", [P, tiles, width // 256, nc.vector.BN_STATS_DIM])
        mv = st.sb("mv", [P, tiles, nc.vector.BN_AGGR_DIM])
        r = st.sb("r", [P, 3, tiles])
        chain, mean_ready, root_ready = (st.sem(n) for n in ("dve_chain", "mean_ready", "root_ready"))
        with nc.Block() as block:
            @block.vector
            def _(dve):
                link = Chain(dve, chain)
                for t in range(tiles):
                    for q in range(width // 256):
                        last = nc.vector.bn_stats(stats[:, t, q, :], x(t)[:, q * 256:(q + 1) * 256])
                link(last)
                for t in range(tiles):
                    last = nc.vector.bn_aggr(mv[:, t, :], stats[:, t])
                link(last)
                nc.vector.tensor_scalar(r[:, 0], mv[:, :, 1], eps, None, ALU.add).then_inc(mean_ready, 1)
                dve.wait_ge(root_ready, 1)
                link(nc.vector.reciprocal(r[:, 2], r[:, 1]))
                for t in range(tiles):
                    last = nc.vector.tensor_scalar(out(t), x(t), mv[:, t, 0:1], r[:, 2, t:t + 1], ALU.subtract, ALU.mult)
                link(last)
                if rows is not None:
                    for t in range(tiles):
                        last = nc.vector.tensor_tensor(out(t), out(t), rows[:, 0], ALU.mult)
                    link(last)
                    for t in range(tiles):
                        last = nc.vector.tensor_tensor(out(t), out(t), rows[:, 1], ALU.add)
                    link(last)

            @block.scalar
            def _(act):
                act.wait_ge(mean_ready, 1)
                nc.scalar.activation(r[:, 1], r[:, 0], ACT.Sqrt).then_inc(root_ready, 1)


class Unit:

    def __init__(self, head, tile, lo, hi, column, mask=None, row=None, shift=None, add=False):
        self.head, self.tile, self.lo, self.hi = head, tile, lo, hi
        self.column, self.mask, self.row, self.shift, self.add = column, mask, row, shift, add


def causal_units(mask, row=None):
    units = []
    for h in range(4):
        for i in range(TT):
            hi = (i + 1) * P
            units.append(Unit(h, i, 0, hi, h * TT + i, mask[:, S - P - i * P:S - P - i * P + hi], row and row(h)[:, 0:hi]))
    return units


def attention(nc, name, k, kind, units, query, key, value, out, dv, scale):
    ps, ident, vec, sca = k["ps"], k["ident"], nc.vector, nc.scalar
    U = len(units)
    late = 1 if kind in ("stick", "mlstm") else 0
    with Stage(nc, name) as st:
        lg = st.sb("logits", [P, 2, S])
        tmp = st.sb("between", [P, 2, S])
        sp_ = st.sb("softplus", [P, 2, S])
        pr = st.sb("weights", [P, 2, S])
        prT = st.sb("weightsT", [P, 2, S])
        mx = st.sb("max", [P, U])
        nm = st.sb("minus_max", [P, U])
        den = st.sb("den", [P, U])
        low = st.sb("low", [P, 2, U])
        sc_full = st.sem("scores_ready")
        first = st.sem("logits_ready")
        mid = st.sem("between_ready")
        second = st.sem("second_ready")
        w_ready = st.sem("weights_ready")
        t_full = st.sem("turned")
        wt_ready = st.sem("turned_copied")
        o_full = st.sem("sum_ready")
        o_done = st.sem("sum_used")
        chain = st.sem("dve_chain")
        achain = st.sem("act_chain")

        def scores(n):
            u = units[n]
            return ps[:, n % 2, 0:u.hi - u.lo]

        def buf(b, n):
            u = units[n]
            return b[:, n % 2, 0:u.hi - u.lo]

        def wait(eng, sem, value):
            if value > 0:
                eng.wait_ge(sem, value)

        with nc.Block() as block:
            @block.tensor
            def _(pe):
                for n in range(U + 2 + late):
                    if n < U:
                        u = units[n]
                        wait(pe, w_ready, n - 1)
                        qs, ks = query(u.head, u.tile), key(u.head, u.lo, u.hi)
                        pairs = list(zip(qs, ks)) if isinstance(qs, list) else [(qs, ks)]
                        for j, (q, kk) in enumerate(pairs):
                            last = nc.tensor.matmul(scores(n), q, kk, start=j == 0, stop=j == len(pairs) - 1)
                        last.then_inc(sc_full, 1)
                    m = n - 1 - late
                    if 0 <= m < U:
                        u = units[m]
                        wait(pe, w_ready, m + 1)
                        wait(pe, wt_ready, m - 1)
                        for c in range((u.hi - u.lo) // P):
                            last = nc.tensor.transpose(ps[:, 2 + m % 2, c * P:(c + 1) * P], pr[:, m % 2, c * P:(c + 1) * P],
                                                       ident[:])
                        last.then_inc(t_full, 1)
                    m = n - 2 - late
                    if 0 <= m < U:
                        u = units[m]
                        wait(pe, wt_ready, m + 1)
                        wait(pe, o_done, m - 1)
                        nk = (u.hi - u.lo) // P
                        for c in range(nk):
                            last = nc.tensor.matmul(ps[:, 4 + m % 2, 0:dv], prT[:, m % 2, c * P:(c + 1) * P],
                                                    value(u.head, u.lo // P + c), start=c == 0, stop=c == nk - 1)
                        last.then_inc(o_full, 1)

            @block.scalar
            def _(act):
                link = Chain(act, achain)
                for n in range(U + 2 + late):
                    if n < U:
                        u = units[n]
                        c = u.column
                        wait(act, first, n + 1)
                        if kind in ("softmax", "decayed"):
                            wait(act, t_full, n - 1)
                            src = buf(lg, n) if u.mask is not None else scores(n)
                            sca.activation(buf(pr, n), src, ACT.Exp, bias=nm[:, n:n + 1],
                                           scale=scale if kind == "softmax" else 1.0,
                                           accum_out=den[:, n:n + 1]).then_inc(w_ready, 1)
                        elif kind == "mlstm":
                            wait(act, w_ready, n - 1)
                            sca.activation(buf(tmp, n), buf(lg, n), ACT.Exp, bias=nm[:, n:n + 1])
                            sca.activation(low[:, 1, n:n + 1], low[:, 0, n:n + 1], ACT.Exp).then_inc(mid, 1)
                        else:
                            wait(act, second, n - 1)
                            link(sca.activation(buf(tmp, n), buf(lg, n), ACT.Abs))
                            link(sca.activation(buf(tmp, n), buf(tmp, n), ACT.Exp, scale=-1.0))
                            sca.activation(buf(tmp, n), buf(tmp, n), ACT.Ln, bias=1.0).then_inc(mid, 1)
                    m = n - 1
                    if kind == "stick" and 0 <= m < U:
                        wait(act, second, m + 1)
                        wait(act, t_full, m - 1)
                        sca.activation(buf(pr, m), buf(lg, m), ACT.Exp).then_inc(w_ready, 1)
                    m = n - 1 - late
                    if kind != "stick" and 0 <= m < U:
                        wait(act, t_full, m + 1)
                        wait(act, o_full, m - 1)
                        w_ = units[m].hi - units[m].lo
                        sca.activation(prT[:, m % 2, 0:w_], ps[:, 2 + m % 2, 0:w_], ACT.Identity).then_inc(wt_ready, 1)

            @block.vector
            def _(dve):
                link = Chain(dve, chain)
                for n in range(U + 2 + late):
                    if n < U:
                        u = units[n]
                        w_ = u.hi - u.lo
                        one = slice(n, n + 1)
                        wait(dve, w_ready, n - 1)
                        if kind == "mlstm":
                            link(vec.tensor_tensor_reduce(buf(lg, n), u.row, u.mask, 1.0, -3e38, ALU.add, ALU.max, mx[:, one]))
                            vec.tensor_scalar(nm[:, one], mx[:, one], -1.0, None, ALU.mult)
                            vec.scalar_tensor_tensor(low[:, 0, one], mx[:, one], -1.0, u.shift, ALU.mult,
                                                     ALU.subtract).then_inc(first, 1)
                        elif kind == "stick":
                            wait(dve, sc_full, n + 1)
                            vec.tensor_tensor(buf(lg, n), scores(n), u.mask, ALU.add).then_inc(first, 1)
                        else:
                            wait(dve, sc_full, n + 1)
                            if kind == "decayed":
                                link(vec.scalar_tensor_tensor(buf(lg, n), scores(n), scale, u.row, ALU.mult, ALU.add))
                                link(vec.tensor_tensor_reduce(buf(lg, n), buf(lg, n), u.mask, 1.0, -3e38, ALU.add, ALU.max,
                                                              mx[:, one]))
                            elif u.mask is not None:
                                link(vec.tensor_tensor_reduce(buf(lg, n), scores(n), u.mask, 1.0, -3e38, ALU.add, ALU.max,
                                                              mx[:, one]))
                            else:
                                link(vec.tensor_reduce(mx[:, one], scores(n), AX_X, ALU.max))
                            vec.tensor_scalar(nm[:, one], mx[:, one], -scale if kind == "softmax" else -1.0, None,
                                              ALU.mult).then_inc(first, 1)
                    m = n - 1
                    if late and 0 <= m < U:
                        wait(dve, mid, m + 1)
                        if kind == "mlstm":
                            wait(dve, sc_full, m + 1)
                            wait(dve, t_full, m - 1)
                            vec.scalar_tensor_tensor(buf(pr, m), scores(m), scale, buf(tmp, m), ALU.mult, ALU.mult,
                                                     accum_out=den[:, m:m + 1]).then_inc(w_ready, 1)
                        else:
                            link(vec.scalar_tensor_tensor(buf(sp_, m), buf(lg, m), 0.0, buf(tmp, m), ALU.max, ALU.add))
                            w_ = units[m].hi
                            s = sp_[:, m % 2, 0:w_]
                            link(vec.tensor_tensor_scan(s[:, ::-1], s[:, ::-1], s[:, ::-1], 0.0, ALU.add, ALU.bypass))
                            vec.tensor_tensor(buf(lg, m), buf(lg, m), s, ALU.subtract).then_inc(second, 1)
                    m = n - 1 - late
                    if kind == "stick" and 0 <= m < U:
                        wait(dve, t_full, m + 1)
                        wait(dve, o_full, m - 1)
                        w_ = units[m].hi
                        vec.tensor_copy(prT[:, m % 2, 0:w_], ps[:, 2 + m % 2, 0:w_]).then_inc(wt_ready, 1)
                    m = n - 2 - late
                    if 0 <= m < U:
                        u = units[m]
                        one = slice(m, m + 1)
                        o = ps[:, 4 + m % 2, 0:dv]
                        wait(dve, o_full, m + 1)
                        if kind == "stick":
                            vec.tensor_copy(out(u.head, u.tile), o).then_inc(o_done, 1)
                            continue
                        if kind == "mlstm":
                            link(vec.scalar_tensor_tensor(mx[:, one], den[:, one], -1.0, den[:, one], ALU.mult, ALU.max))
                            link(vec.tensor_tensor(den[:, one], mx[:, one], low[:, 1, one], ALU.max))
                        link(vec.reciprocal(mx[:, one], den[:, one]))
                        dst = out(u.head, u.tile)
                        if u.add:
                            wait(dve, o_done, m)
                            vec.scalar_tensor_tensor(dst, o, mx[:, one], dst, ALU.mult, ALU.add).then_inc(o_done, 1)
                        else:
                            vec.tensor_scalar(dst, o, mx[:, one], None, ALU.mult).then_inc(o_done, 1)


def constants(nc, st, ps):
    k = {"ps": ps}
    for n, shape, dt in (("ident", [P, P], F32), ("ones", [P, P], F32), ("before", [P, P], F32), ("upto", [P, P], F32),
                         ("after", [P, P], F32), ("mask_le", [P, 2 * S - P], F32), ("mask_lt", [P, 2 * S - P], F32),
                         ("mask_ge", [P, 2 * S - P], F32),
                         ("iota_e", [P, NE], F32), ("group_of", [P, NE], F32), ("choice", [P, 2, TT], F32), ("second", [P, 1], F32)):
        k[n] = st.sb(n, shape, dt)
    made = st.sem("const_made")
    with nc.Block() as block:
        @block.gpsimd
        def _(pool):
            g = nc.gpsimd
            for n in ("ones", "before", "upto", "after"):
                g.memset(k[n][:], 1.0)
            for n in ("ident", "mask_le", "mask_lt", "mask_ge", "second"):
                g.memset(k[n][:], 0.0)
            g.iota(k["iota_e"][:], [[1, NE]], 0, 0, allow_small_or_imprecise_dtypes=True)
            g.iota(k["group_of"][:].rearrange("p (g e) -> p g e", g=NG), [[1, NG], [0, EPG]], 0, 0,
                   allow_small_or_imprecise_dtypes=True)
            g.iota(k["choice"][:], [[S, 2], [P, TT]], 0, 1, allow_small_or_imprecise_dtypes=True).then_inc(made, 1)
            pool.wait_ge(made, 1)
            g.affine_select(k["second"][:], k["second"][:], [[0, 1]], ALU.is_ge, 1.0, SLOTS - 1, -1)
            g.affine_select(k["ident"][:], k["ident"][:], [[-1, P]], ALU.not_equal, 1.0, 0, 1)
            g.affine_select(k["before"][:], k["before"][:], [[1, P]], ALU.is_gt, 0.0, 0, -1)
            g.affine_select(k["upto"][:], k["upto"][:], [[1, P]], ALU.is_ge, 0.0, 0, -1)
            g.affine_select(k["after"][:], k["after"][:], [[-1, P]], ALU.is_ge, 0.0, 0, 1)
            n, off = 2 * S - P, S - P
            g.affine_select(k["mask_le"][:], k["mask_le"][:], [[-1, n]], ALU.is_ge, -BIG, off, 1)
            g.affine_select(k["mask_lt"][:], k["mask_lt"][:], [[-1, n]], ALU.is_gt, -BIG, off, 1)
            g.affine_select(k["mask_ge"][:], k["mask_ge"][:], [[1, n]], ALU.is_ge, -BIG, -off, -1).then_inc(made, 1)
    return k


def moe(nc, name, k, x, hT, h_rows, gain, w_rg, b_rg, w_re, b_re, w_gate, w_up, w_down, alpha=1.0):
    FF = w_gate.shape[2]
    NF = FF // P
    RING = 2 * 512 // FF
    HALF = FF // 2
    HF = HALF // P
    ident, ps = k["ident"], k["ps"]
    rows_dram = nc.dram_tensor(f"{name}_dram_rows", [S, D], F32).ap()
    y_dram = nc.dram_tensor(f"{name}_dram_y", [4 * S, D // 2], F32).ap()
    spare_dram = nc.dram_tensor(f"{name}_dram_spare", [1, SLOTS], F32).ap()
    token_dram = nc.dram_tensor(f"{name}_dram_token", [ROWS, 1], F32).ap()

    with Stage(nc, name) as st:
        wg = st.sb("wg", [P, RING, DC, FF])
        wu = st.sb("wu", [P, RING, DC, FF])
        wd = st.sb("wd", [P, RING, NF, D])
        router = st.sb("router", [P, DC, NG + NE])
        bias = st.sb("bias", [P, NG + NE])
        logits = st.sb("logits", [P, TT, NG + NE])
        gpad = st.sb("gpad", [P, TT, 8])
        gmax = st.sb("gmax", [P, TT, 8])
        gidx = st.sb("gidx", [P, TT, 8], U32)
        gidxf = st.sb("gidxf", [P, TT, 1])
        gmask = st.sb("gmask", [P, TT, NE])
        away = st.sb("away", [P, TT, NE])
        masked = st.sb("masked", [P, TT, NE])
        emax = st.sb("emax", [P, TT, 8])
        eidx = st.sb("eidx", [P, TT, 8], U32)
        eidxf = st.sb("eidxf", [P, TT, 2])
        hot = st.sb("hot", [P, 2, TT, NE])
        both = st.sb("both", [P, TT, NE])
        diff = st.sb("diff", [P, 5 * TT])
        expd = st.sb("expd", [P, 5 * TT])
        gsum = st.sb("gsum", [P, TT])
        weight = st.sb("weight", [P, 2, TT])
        nblk = st.sb("nblk", [P, 8, NE])
        ends = st.sb("ends", [P, 3, NE])
        slot = st.sb("slot", [P, TT, NE])
        picked = st.sb("picked", [P, 2, TT, NE])
        slotf = st.sb("slotf", [P, 2, TT])
        sloti = st.sb("sloti", [P, 2, TT], U32)
        table = st.sb("table", [1, 2, NE], I32)
        zero = st.sb("zero", [1, ROWS])
        tokrow = st.sb("tokrow", [TABLE, 2, SLOTS])
        part = st.sb("part", [P, 3, TABLE])
        tokcol = st.sb("tokcol", [SLOTS, TABLE], U32)
        choicecol = st.sb("choicecol", [P, TABLE], U32)
        choicecur = st.sb("choicecur", [P, 1], U32)
        tokcur = st.sb("tokcur", [SLOTS, 1], U32)
        gathered = st.sb("gathered", [SLOTS, D])
        xT = st.sb("xT", [P, DC, SLOTS])
        silu = st.sb("silu", [P, 2, HALF])
        hid = st.sb("hid", [P, 2, HALF])
        hidT = st.sb("hidT", [P, NF, SLOTS])
        y = st.sb("y", [P, D // 2])
        aside = st.sb("aside", [1, 1])

        w_sem = [[st.sem(f"{m}_landed{s}") for m in ("gate", "up", "down")] for s in range(RING)]
        router_landed = st.sem("router_landed")
        rows_stored = st.sem("rows_stored")
        zero_ready = st.sem("zero_ready")
        zero_stored = st.sem("zero_stored")
        logits_ready = st.sem("logits_ready")
        chain = st.sem("dve_chain")
        diff_ready = st.sem("diff_ready")
        exp_ready = st.sem("exp_ready")
        hot_ready = st.sem("hot_ready")
        rank_ready = st.sem("rank_ready")
        table_ready = st.sem("table_ready")
        token_scattered = st.sem("token_scattered")
        tokrow_landed = st.sem("tokrow_landed")
        tokT_ready = st.sem("tokT_ready")
        tokcol_ready = st.sem("tokcol_ready")
        tokcur_ready = st.sem("tokcur_ready")
        choicecur_ready = st.sem("choicecur_ready")
        rows_gathered = st.sem("rows_gathered")
        turned = st.sem("turned")
        xT_ready = st.sem("xT_ready")
        gu_ready = st.sem("gate_up_ready")
        silu_ready = st.sem("silu_ready")
        hid_ready = st.sem("hid_ready")
        hid_turned = st.sem("hid_turned")
        hidT_ready = st.sem("hidT_ready")
        y_ready = st.sem("y_ready")
        y_copied = st.sem("y_copied")
        y_stored = st.sem("y_stored")
        back_landed = st.sem("back_landed")
        back_used = st.sem("back_used")

        wg_dram = w_gate.rearrange("e (c p) f -> e p c f", p=P)
        wu_dram = w_up.rearrange("e (c p) f -> e p c f", p=P)
        wd_dram = w_down.rearrange("e (c p) d -> e p c d", p=P)
        ps_turn = ps[:, 0, :]
        ps_gu = [ps[:, 1 + q, 0:HALF] for q in range(2)]
        ps_hid = [ps[:, 3 + q, 0:HF * SLOTS] for q in range(2)]
        ps_y = ps[:, 5, :]
        ps_tok = ps[:, 6, 0:TABLE]

        def back(j):
            return wg[:, j * RING // 2:(j + 1) * RING // 2].rearrange("p r c f -> p (r c f)").rearrange("p (t d) -> p t d", t=TT)

        def blocks_of(eng, e):
            return eng.value_load(table[0:1, 0, bass.ds(e, 1)], min_val=1, max_val=S // SLOTS)

        with nc.Block() as block:
            @block.sync
            def _(sp):
                def load(e, s, m):
                    w, dram = ((wg, wg_dram), (wu, wu_dram), (wd, wd_dram))[m]
                    sp.dma_start(w[:, s], dram[bass.ds(e, 1)].rearrange("e p c f -> p (e c) f")).then_inc(w_sem[s][m], 16)

                sp.dma_start(router[:, :, 0:NG], w_rg.rearrange("(c p) n -> p c n", p=P)).then_inc(router_landed, 16)
                sp.dma_start(router[:, :, NG:], w_re.rearrange("(c p) n -> p c n", p=P)).then_inc(router_landed, 16)
                sp.dma_start(bias[:, 0:NG], b_rg.partition_broadcast(P)).then_inc(router_landed, 16)
                sp.dma_start(bias[:, NG:], b_re.partition_broadcast(P)).then_inc(router_landed, 16)
                sp.wait_ge(zero_ready, 1)
                sp.dma_start(token_dram.rearrange("n one -> one n"), zero[:]).then_inc(zero_stored, 16)
                sp.dma_start(rows_dram.rearrange("(t p) d -> p t d", p=P), h_rows).then_inc(rows_stored, 16)
                for s in range(RING):
                    for m in range(3):
                        load(s, s, m)
                sp.wait_ge(token_scattered, 16 * 2 * TT)
                for q in range(2):
                    sp.dma_start(tokrow[:, q], token_dram.rearrange("(b s) one -> b (s one)", s=SLOTS)).then_inc(tokrow_landed, 16)
                sp.wait_ge(table_ready, 2)
                with sp.Fori(0, NE // RING - 1) as turn_:
                    for s in range(RING):
                        e = turn_ * RING + s
                        end = sp.value_load(table[0:1, 1, bass.ds(e, 1)], min_val=1, max_val=MAX_BLOCKS)
                        prev, landed = (s - 1) % RING, (turn_ + (1 if s == 0 else 2)) * 16
                        sp.wait_ge(gu_ready, end * 2)
                        sp.wait_ge(w_sem[prev][0 if FF < 512 else 1], landed)
                        load(e + RING, s, 0)
                        sp.wait_ge(w_sem[prev][1 if FF < 512 else 2], landed)
                        load(e + RING, s, 1)
                        sp.wait_ge(y_ready, end)
                        if FF < 512:
                            sp.wait_ge(w_sem[prev][2], landed)
                        else:
                            sp.wait_ge(w_sem[s][0], (turn_ + 2) * 16)
                        load(e + RING, s, 2)
                total = sp.value_load(table[0:1, 1, NE - 1:NE], min_val=1, max_val=MAX_BLOCKS)
                sp.wait_ge(y_stored, total * 16 + 16)
                for j in range(2):
                    sp.dma_start(back(j), y_dram[2 * S * j:2 * S * (j + 1)].rearrange("(t p h) d -> p t (h d)", t=TT, p=P)
                                 ).then_inc(back_landed, 16)

            @block.tensor
            def _(pe):
                pe.wait_ge(router_landed, 64)
                for t in range(TT):
                    for c in range(DC):
                        last = nc.tensor.matmul(ps[:, t, 0:NG + NE], hT[:, c, t * P:(t + 1) * P], router[:, c, :],
                                                start=c == 0, stop=c == DC - 1)
                last.then_inc(logits_ready, 1)
                pe.wait_ge(hot_ready, 1)
                for t in range(TT):
                    for u in range(t + 1):
                        nc.tensor.matmul(ps[:, t, 64:64 + NE], k["ones"][:] if u < t else k["before"][:], both[:, u, :],
                                         start=u == 0, stop=u == t)
                for t in range(TT):
                    last = nc.tensor.matmul(ps[:, 4, 0:NE], k["ones"][:], both[:, t, :], start=t == 0, stop=t == TT - 1)
                last.then_inc(rank_ready, 1)
                pe.wait_ge(tokrow_landed, 32)
                nb = TABLE
                nc.tensor.transpose(ps_tok, tokrow[:].rearrange("b q s -> b (q s)"), ident[0:nb, 0:nb]).then_inc(tokT_ready, 1)
                pe.wait_ge(table_ready, 2)

                def turn():
                    nc.tensor.matmul(ps_turn[:, 0:SLOTS], gathered[:, 0:P], ident[0:SLOTS, 0:SLOTS], start=True, stop=True)
                    for c in range(1, DC):
                        last = nc.tensor.transpose(ps_turn[:, c * SLOTS:(c + 1) * SLOTS], gathered[:, c * P:(c + 1) * P],
                                                   ident[0:SLOTS, 0:SLOTS])
                    last.then_inc(turned, 1)

                pe.wait_ge(rows_gathered, 16)
                turn()
                done = pe.alloc_register(f"{name}_done")
                pe.reg_mov(done, 0)
                with pe.Fori(0, NE // RING) as turn_:
                    for s in range(RING):
                        for m in range(3):
                            pe.wait_ge(w_sem[s][m], (turn_ + 1) * 16)
                        with pe.Fori(0, blocks_of(pe, turn_ * RING + s)):
                            g = pe.snap(done)
                            pe.wait_ge(xT_ready, g + 1)
                            for q in range(2):
                                span = slice(q * HALF, (q + 1) * HALF)
                                for c in range(DC):
                                    nc.tensor.matmul(ps_gu[q][0:SLOTS], xT[:, c, :], wg[:, s, c, span],
                                                     start=c == 0, stop=c == DC - 1)
                                    last = nc.tensor.matmul(ps_gu[q][SLOTS:P], xT[:, c, :], wu[:, s, c, span],
                                                            start=c == 0, stop=c == DC - 1)
                                last.then_inc(gu_ready, 1)
                            pe.wait_ge(rows_gathered, (g + 2) * 16)
                            turn()
                            for q in range(2):
                                pe.wait_ge(hid_ready, g * 2 + (q + 1))
                                for f in range(HF):
                                    last = nc.tensor.matmul(ps_hid[q][:, f * SLOTS:(f + 1) * SLOTS],
                                                            hid[SLOTS:P, q, f * P:(f + 1) * P], ident[SLOTS:P, SLOTS:P],
                                                            start=True, stop=True)
                                last.then_inc(hid_turned, 1)
                            pe.wait_ge(y_copied, g + 1)
                            for f in range(NF):
                                if f % HF == 0:
                                    pe.wait_ge(hidT_ready, g * 2 + (f // HF + 1))
                                for h in range(2):
                                    last = nc.tensor.matmul(ps_y[h * SLOTS:(h + 1) * SLOTS], hidT[:, f, :],
                                                            wd[:, s, f, h * 512:(h + 1) * 512],
                                                            start=f == 0, stop=f == NF - 1)
                            last.then_inc(y_ready, 1)
                            pe.reg_add(done, done, 1)

            @block.scalar
            def _(act):
                act.sem_inc(y_copied, 1)
                act.wait_ge(diff_ready, 1)
                nc.scalar.activation(expd[:], diff[:], ACT.Exp).then_inc(exp_ready, 1)
                act.wait_ge(table_ready, 2)
                done = act.alloc_register(f"{name}_done")
                act.reg_mov(done, 0)
                with act.Fori(0, NE) as e:
                    with act.Fori(0, blocks_of(act, e)):
                        g = act.snap(done)
                        for q in range(2):
                            act.wait_ge(gu_ready, g * 2 + (q + 1))
                            nc.scalar.activation(silu[SLOTS:P, q], ps_gu[q][0:SLOTS], ACT.Silu).then_inc(silu_ready, 1)
                        for q in range(2):
                            act.wait_ge(hid_turned, g * 2 + (q + 1))
                            nc.scalar.copy(hidT[:, q * HF:(q + 1) * HF].rearrange("p f s -> p (f s)"), ps_hid[q]
                                           ).then_inc(hidT_ready, 1)
                        act.wait_ge(y_ready, g + 1)
                        act.wait_ge(y_stored, (g + 1) * 16)
                        nc.scalar.copy(y[:], ps_y).then_inc(y_copied, 1)
                        act.reg_add(done, done, 1)

            @block.vector
            def _(dve):
                link = Chain(dve, chain)
                vec = nc.vector
                vec.memset(zero[:], float(2 * S)).then_inc(zero_ready, 1)
                link(vec.memset(gpad[:], -BIG * 1e8))
                dve.wait_ge(router_landed, 64)
                dve.wait_ge(logits_ready, 1)
                link(vec.tensor_tensor(logits[:], ps[:, 0:TT, 0:NG + NE],
                                       bias[:].unsqueeze(1).to_broadcast([P, TT, NG + NE]), ALU.add))
                link(vec.tensor_copy(gpad[:, :, 0:NG], logits[:, :, 0:NG]))
                for t in range(TT):
                    link(vec.max(gmax[:, t, :], gpad[:, t, :]))
                    link(vec.max_index(gidx[:, t, :], gmax[:, t, :], gpad[:, t, :]))
                link(vec.tensor_copy(gidxf[:], gidx[:, :, 0:1]))
                link(vec.tensor_tensor(gmask[:], k["group_of"][:].unsqueeze(1).to_broadcast([P, TT, NE]),
                                       gidxf[:].to_broadcast([P, TT, NE]), ALU.is_equal))
                link(vec.tensor_scalar(away[:], gmask[:], -1.0, BIG, ALU.add, ALU.mult))
                link(vec.tensor_tensor(masked[:], logits[:, :, NG:], gmask[:], ALU.mult))
                link(vec.tensor_tensor(masked[:], masked[:], away[:], ALU.add))
                for t in range(TT):
                    link(vec.max(emax[:, t, :], masked[:, t, :]))
                    link(vec.max_index(eidx[:, t, :], emax[:, t, :], masked[:, t, :]))
                link(vec.tensor_copy(eidxf[:], eidx[:, :, 0:2]))
                for j in range(2):
                    link(vec.tensor_tensor(hot[:, j], k["iota_e"][:].unsqueeze(1).to_broadcast([P, TT, NE]),
                                           eidxf[:, :, j:j + 1].to_broadcast([P, TT, NE]), ALU.is_equal))
                vec.tensor_tensor(both[:], hot[:, 0], hot[:, 1], ALU.add).then_inc(hot_ready, 1)
                vec.tensor_tensor(diff[:, 0:TT * NG].rearrange("p (t g) -> p t g", t=TT), logits[:, :, 0:NG],
                                  gmax[:, :, 0:1].to_broadcast([P, TT, NG]), ALU.subtract)
                link(vec.tensor_tensor(diff[:, TT * NG:], emax[:, :, 1], emax[:, :, 0], ALU.subtract))
                vec.tensor_copy(gpad[:, 0, 0:1], diff[:, 0:1]).then_inc(diff_ready, 1)
                dve.wait_ge(exp_ready, 1)
                link(vec.tensor_reduce(gsum[:], expd[:, 0:TT * NG].rearrange("p (t g) -> p t g", t=TT), AX_X, ALU.add))
                link(vec.scalar_tensor_tensor(gsum[:], expd[:, TT * NG:], 1.0, gsum[:], ALU.add, ALU.mult))
                link(vec.reciprocal(weight[:, 0], gsum[:]))
                link(vec.tensor_tensor(weight[:, 1], weight[:, 0], expd[:, TT * NG:], ALU.mult))
                dve.wait_ge(rank_ready, 1)
                counts = ps[:, 4, 0:NE]
                link(vec.tensor_scalar(nblk[:, 0], counts, float(SLOTS), 1.0, ALU.is_gt, ALU.add))
                for j in range(2, S // SLOTS):
                    link(vec.scalar_tensor_tensor(nblk[:, j - 1], counts, float(SLOTS * j), nblk[:, j - 2], ALU.is_gt, ALU.add))
                blocks = nblk[:, S // SLOTS - 2]
                link(vec.tensor_tensor_scan(ends[:, 0], blocks, blocks, 0.0, ALU.add, ALU.bypass))
                vec.tensor_copy(table[0:1, 0], blocks[0:1]).then_inc(table_ready, 1)
                vec.tensor_copy(table[0:1, 1], ends[0:1, 0]).then_inc(table_ready, 1)
                link(vec.tensor_tensor(ends[:, 1], ends[:, 0], blocks, ALU.subtract))
                link(vec.tensor_scalar(ends[:, 2], ends[:, 1], float(SLOTS), None, ALU.mult))
                link(vec.tensor_tensor(slot[:], ps[:, 0:TT, 64:64 + NE],
                                       ends[:, 2:3].to_broadcast([P, TT, NE]), ALU.add))
                for j in range(2):
                    link(vec.tensor_tensor(picked[:, j], slot[:], hot[:, j], ALU.mult))
                for j in range(2):
                    link(vec.tensor_reduce(slotf[:, j], picked[:, j], AX_X, ALU.add))
                vec.tensor_copy(sloti[:], slotf[:]).then_inc(table_ready, 1)
                dve.wait_ge(tokT_ready, 1)
                link(vec.tensor_scalar(part[:, 0], ps_tok, 1.0, None, ALU.mult))
                link(vec.tensor_scalar(part[:, 1], part[:, 0], float(S), float(-S), ALU.is_ge, ALU.mult))
                link(vec.tensor_tensor(part[:, 2], part[:, 0], part[:, 1], ALU.add))
                vec.tensor_scalar(choicecol[:], part[:, 0], 2.0, k["second"][:], ALU.mult, ALU.add).then_inc(tokcol_ready, 1)
                vec.tensor_scalar(tokcol[:], part[0:SLOTS, 2], float(S - 1), None, ALU.min).then_inc(tokcol_ready, 1)

                def turn_copy(n):
                    dve.wait_ge(turned, n)
                    view = ps_turn.rearrange("p (c s) -> p c s", c=DC)
                    if gain is None:
                        vec.tensor_copy(xT[:], view).then_inc(xT_ready, 1)
                    else:
                        vec.tensor_tensor(xT[:], view, cols(gain, SLOTS), ALU.mult).then_inc(xT_ready, 1)

                turn_copy(1)
                done = dve.alloc_register(f"{name}_done")
                dve.reg_mov(done, 0)
                with dve.Fori(0, NE) as e:
                    with dve.Fori(0, blocks_of(dve, e)):
                        g = dve.snap(done)
                        for q in range(2):
                            dve.wait_ge(silu_ready, g * 2 + (q + 1))
                            vec.tensor_tensor(hid[SLOTS:P, q], silu[SLOTS:P, q], ps_gu[q][SLOTS:P], ALU.mult).then_inc(hid_ready, 1)
                        turn_copy(g + 2)
                        dve.reg_add(done, done, 1)
                dve.wait_ge(rows_stored, 16)
                if alpha != 1.0:
                    link(vec.tensor_scalar(x[:], x[:], alpha, None, ALU.mult))
                dve.wait_ge(back_landed, 32)
                for j in range(2):
                    for t in range(TT):
                        if j:
                            dve.wait_ge(back_used, t + 1)
                        vec.scalar_tensor_tensor(x[:, t, :], back(j)[:, t, :], weight[:, j, t:t + 1], x[:, t, :],
                                                 ALU.mult, ALU.add).then_inc(back_used, 1)

            @block.gpsimd
            def _(pool):
                def step_aside():
                    nc.gpsimd.tensor_tensor(aside[:], ident[0:1, 0:1], ident[0:1, 0:1], ALU.mult)

                pool.wait_ge(zero_stored, 16)
                pool.wait_ge(rows_stored, 16)
                pool.wait_ge(table_ready, 3)
                for t in range(TT):
                    for j in range(2):
                        nc.gpsimd.indirect_dma_start(token_dram, bass.IndirectOffsetOnAxis(sloti[:, j, t:t + 1], 0),
                                                     k["choice"][:, j, t:t + 1], None).then_inc(token_scattered, 16)
                pool.wait_ge(tokcol_ready, 2)

                def gather(n):
                    nc.gpsimd.tensor_copy(tokcur[:], tokcol[:, bass.ds(n, 1)]).then_inc(tokcur_ready, 1)
                    pool.wait_ge(tokcur_ready, n + 1)
                    step_aside()
                    nc.gpsimd.indirect_dma_start(gathered[:], None, rows_dram,
                                                 bass.IndirectOffsetOnAxis(tokcur[:], 0)).then_inc(rows_gathered, 16)

                nc.gpsimd.dma_start(spare_dram, ident[0:1, 0:SLOTS]).then_inc(y_stored, 16)
                gather(0)
                pool.wait_ge(turned, 1)
                gather(1)
                done = pool.alloc_register(f"{name}_done")
                pool.reg_mov(done, 0)
                with pool.Fori(0, NE) as e:
                    with pool.Fori(0, blocks_of(pool, e)):
                        g = pool.snap(done)
                        pool.wait_ge(turned, g + 2)
                        gather(g + 2)
                        pool.wait_ge(y_copied, g + 2)
                        nc.gpsimd.tensor_copy(choicecur[:], choicecol[:, bass.ds(g, 1)]).then_inc(choicecur_ready, 1)
                        pool.wait_ge(choicecur_ready, g + 1)
                        step_aside()
                        nc.gpsimd.indirect_dma_start(y_dram, bass.IndirectOffsetOnAxis(choicecur[:], 0), y[:], None,
                                                     bounds_check=4 * S - 1, oob_is_err=False).then_inc(y_stored, 16)
                        pool.reg_add(done, done, 1)


class Columns:

    def __init__(self, sizes):
        self.at, n = {}, 0
        for name, width in sizes:
            self.at[name] = (n, n + width)
            n += width
        self.width = n


COLS = Columns([("g_mix", 8), ("g_xattn", 8), ("g_mem", 8), ("g_moe", 8), ("conv_w", 40), ("conv_b", 8), ("b_s", 4)]
               + [(f"{n}{l}", w) for l in range(2) for n, w in (("b_gate", 32), ("q_norm", 2), ("kv_norm", 1), ("conv_w2", 62),
                                                               ("conv_b2", 2), ("ln_g2", 2), ("ln_b2", 2))])
ROWS_ = Columns([("gate_b", 16), ("g_head", 512), ("ln_v_g", 512), ("ln_v_b", 512), ("g_final", 1024), ("inv_freq", 16)]
                + [(f"{n}{l}", w) for l in range(2) for n, w in (("b_forget", 4), ("ln1_g", 1024), ("ln1_b", 1024),
                                                                ("ln2_g", 1024), ("ln2_b", 1024))])


def load(nc, name, pairs):
    with Stage(nc, name) as st:
        landed = st.sem("landed")
        with nc.Block() as block:
            @block.sync
            def _(sp):
                for dst, src in pairs:
                    sp.dma_start(dst, src).then_inc(landed, 16)
                sp.wait_ge(landed, 16 * len(pairs))


def running_log_sigmoid(nc, name, k, f, nf, after_from, b):
    ps = k["ps"]
    with Stage(nc, name) as st:
        a = st.sb("abs", [P, TT, nf])
        e = st.sb("exp", [P, TT, nf])
        l1 = st.sb("ln", [P, TT, nf])
        ls = st.sb("ls", [P, TT, nf])
        achain, ln_ready, ls_ready, summed = (st.sem(n) for n in ("act_chain", "ln_ready", "ls_ready", "summed"))
        with nc.Block() as block:
            @block.scalar
            def _(act):
                link = Chain(act, achain)
                link(nc.scalar.activation(a[:], f, ACT.Abs))
                link(nc.scalar.activation(e[:], a[:], ACT.Exp, scale=-1.0))
                nc.scalar.activation(l1[:], e[:], ACT.Ln, bias=1.0).then_inc(ln_ready, 1)

            @block.vector
            def _(dve):
                dve.wait_ge(ln_ready, 1)
                nc.vector.scalar_tensor_tensor(ls[:], f, 0.0, l1[:], ALU.min, ALU.subtract).then_inc(ls_ready, 1)
                dve.wait_ge(summed, 1)
                nc.vector.tensor_copy(b, ps[:, 0:TT, 0:nf])

            @block.tensor
            def _(pe):
                pe.wait_ge(ls_ready, 1)
                for t in range(TT):
                    for u in range(t + 1):
                        last = nc.tensor.matmul(ps[:, t, 0:after_from], (k["ones"] if u < t else k["upto"])[:],
                                                ls[:, u, 0:after_from], start=u == 0, stop=u == t)
                    if after_from < nf:
                        for u in range(t, TT):
                            last = nc.tensor.matmul(ps[:, t, after_from:nf], (k["ones"] if u > t else k["after"])[:],
                                                    ls[:, u, after_from:nf], start=u == t, stop=u == TT - 1)
                last.then_inc(summed, 1)


def spread_rows(nc, name, k, r, n, rows):
    ps = k["ps"]
    with Stage(nc, name) as st:
        full = st.sem("bank_full")
        emptied = [st.sem("emptied_by_act"), st.sem("emptied_by_dve")]
        with nc.Block() as block:
            @block.tensor
            def _(pe):
                for j in range(n):
                    for t in range(TT):
                        last = nc.tensor.matmul(ps[:, j, t * P:(t + 1) * P], r[:, t, j:j + 1].to_broadcast([P, P]),
                                                k["ident"][:], start=True, stop=True)
                    last.then_inc(full, 1)

            @block.scalar
            def _(act):
                for j in range(0, n, 2):
                    act.wait_ge(full, j + 1)
                    nc.scalar.activation(rows[:, j, :], ps[:, j, :], ACT.Identity)

            @block.vector
            def _(dve):
                for j in range(1, n, 2):
                    dve.wait_ge(full, j + 1)
                    nc.vector.tensor_copy(rows[:, j, :], ps[:, j, :])


def mixer_one(nc, k, x, hT, col, i):
    ps, vec, sca = k["ps"], nc.vector, nc.scalar
    H, DH = 4, P
    with Stage(nc, "mix") as sx:
        o = sx.sb("o", [P, TT, 512])
        gu = sx.sb("gu", [P, TT, 512])
        gv = sx.sb("gv", [P, TT, 512])
        y = sx.sb("y", [P, TT, D])
        with Stage(nc, "mixa") as sa:
            raw = sa.sb("raw", [P, 8, S + 4])
            qk = sa.sb("qk", [P, 8, S])
            v = sa.sb("v", [P, TT, 512])
            gates = sa.sb("gates", [P, TT, 16])
            rms_rows(nc, "mixn", lambda t: x[:, t, :], lambda t: y[:, t, :], TT, D, 1e-6)
            turn(nc, "mixt", k, TT, lambda t, c: y[:, t, c * P:(c + 1) * P],
                 [plain(nc, hT[:, c, :], col("g_mix")[:, c:c + 1]) for c in range(DC)])
            w = i["w_in"][0]
            chunks = [chunk_of(w, a, b) for a, b in ((0, 512), (512, 1024), (1024, 1536), (1536, 2048), (2048, 2064),
                                                     (2064, 2576), (2576, 3088))]
            items = []
            for c in range(2):
                for j in range(4):
                    items.append(by_feature(c, hT, j * P, "act" if j % 2 else "dve", plain(nc, raw[:, 4 * c + j, 2:2 + S])))
            func = lambda out, f: lambda eng, src: eng.activation(out, src, f)
            for t in range(TT):
                items.append(by_token(2, hT, t, 0, 512, "dve", plain(nc, v[:, t, :])))
            for t in range(TT):
                items.append(by_token(3, hT, t, 0, 512, "act", func(o[:, t, :], ACT.Sigmoid)))
            for t in range(TT):
                items.append(by_token(4, hT, t, 0, 16, "dve", lambda eng, src, t=t: eng.tensor_tensor(
                    gates[:, t, :], src, k["rows"]["gate_b"], ALU.add)))
            for t in range(TT):
                items.append(by_token(5, hT, t, 0, 512, "act", func(gu[:, t, :], ACT.Gelu_apprx_tanh)))
            for t in range(TT):
                items.append(by_token(6, hT, t, 0, 512, "act", func(gv[:, t, :], ACT.Gelu_apprx_tanh)))
            dense(nc, "mixw", k, chunks, items)
            with Stage(nc, "mixc") as st:
                acc = st.sb("acc", [P, 8, S])
                padded, tapped, done = st.sem("padded"), st.sem("tapped"), st.sem("done")
                with nc.Block() as block:
                    @block.vector
                    def _(dve):
                        vec.memset(raw[:, :, 0:2], 0.0)
                        vec.memset(raw[:, :, 2 + S:], 0.0).then_inc(padded, 1)
                        dve.wait_ge(padded, 1)
                        for j in range(5):
                            for c in range(8):
                                wj = col("conv_w")[:, 8 * j + c:8 * j + c + 1]
                                src = raw[:, c, j:j + S]
                                if j == 0:
                                    vec.tensor_scalar(acc[:, c, :], src, wj, None, ALU.mult).then_inc(tapped, 1)
                                else:
                                    dve.wait_ge(tapped, 8 * (j - 1) + c + 1)
                                    vec.scalar_tensor_tensor(acc[:, c, :], src, wj, acc[:, c, :], ALU.mult,
                                                             ALU.add).then_inc(tapped, 1)

                    @block.scalar
                    def _(act):
                        for c in range(8):
                            act.wait_ge(tapped, 32 + c + 1)
                            sca.activation(qk[:, c, :], acc[:, c, :], ACT.Silu, bias=col("conv_b")[:, c:c + 1])
            hs = raw[:, 0:4, 0:512]
            with Stage(nc, "mixm") as sm:
                f = sm.sb("f", [P, TT, 8])
                b = sm.sb("b", [P, TT, 8])
                r = sm.sb("r", [P, TT, 8])
                rows = sm.sb("rows", [P, 8, S])
                copied = sm.sem("copied")
                with nc.Block() as block:
                    @block.vector
                    def _(dve):
                        g4 = gates[:].rearrange("p t (q h) -> p t q h", h=4)
                        vec.tensor_copy(f[:].rearrange("p t (q h) -> p t q h", h=4), g4[:, :, 1::2, :]).then_inc(copied, 1)
                        dve.wait_ge(copied, 1)
                running_log_sigmoid(nc, "mixs", k, f[:], 8, 4, b[:])
                with nc.Block() as block:
                    @block.vector
                    def _(dve):
                        g4 = gates[:].rearrange("p t (q h) -> p t q h", h=4)
                        vec.tensor_tensor(r[:].rearrange("p t (q h) -> p t q h", h=4), g4[:, :, 0::2, :],
                                          b[:].rearrange("p t (q h) -> p t q h", h=4), ALU.subtract)
                spread_rows(nc, "mixr", k, r, 8, rows)
                units = []
                for h in range(H):
                    for t in range(TT):
                        n = (h * TT + t) * 2
                        hi = (t + 1) * P
                        off = S - P - t * P
                        units.append(Unit(h, t, 0, hi, n, k["mask_le"][:, off:off + hi], rows[:, h, 0:hi], b[:, t, h:h + 1]))
                        lo = t * P
                        units.append(Unit(h, t, lo, S, n + 1, k["mask_ge"][:, S - P:S - P + S - lo], rows[:, 4 + h, lo:],
                                          b[:, t, 4 + h:5 + h], add=True))
                attention(nc, "mixh", k, "mlstm", units, lambda h, t: qk[:, h, t * P:(t + 1) * P],
                          lambda h, lo, hi: qk[:, 4 + h, lo:hi], lambda h, c: v[:, c, h * P:(h + 1) * P],
                          lambda h, t: hs[:, t, h * P:(h + 1) * P], P, DH ** -0.5)
            with Stage(nc, "mixg") as st:
                junk = st.sb("junk", [P, P])
                ss = st.sb("ss", [P, 4, TT, H])
                squared, mean_ready, root_ready, chain, act_chain = (
                    st.sem(n) for n in ("squared", "mean_ready", "root_ready", "dve_chain", "act_chain"))
                with nc.Block() as block:
                    @block.scalar
                    def _(act):
                        link = Chain(act, act_chain)
                        for t in range(TT):
                            for h in range(H):
                                link(sca.activation(junk[:], hs[:, t, h * P:(h + 1) * P], ACT.Square,
                                                    accum_out=ss[:, 0, t, h:h + 1]))
                        act.sem_inc(squared, 1)
                        act.wait_ge(mean_ready, 1)
                        sca.activation(ss[:, 2], ss[:, 1], ACT.Sqrt).then_inc(root_ready, 1)

                    @block.vector
                    def _(dve):
                        link = Chain(dve, chain)
                        for t in range(TT):
                            last = vec.tensor_tensor(o[:, t, :], o[:, t, :], k["rows"]["g_head"], ALU.mult)
                        link(last)
                        dve.wait_ge(squared, 1)
                        vec.tensor_scalar(ss[:, 1], ss[:, 0], 1.0 / P, 1e-6, ALU.mult, ALU.add).then_inc(mean_ready, 1)
                        dve.wait_ge(root_ready, 1)
                        link(vec.reciprocal(ss[:, 3], ss[:, 2]))
                        for t in range(TT):
                            for h in range(H):
                                cs = slice(h * P, (h + 1) * P)
                                vec.scalar_tensor_tensor(y[:, t, cs], hs[:, t, cs], ss[:, 3, t, h:h + 1], o[:, t, cs],
                                                         ALU.mult, ALU.mult)
        ln_rows(nc, "mixl", lambda t: gv[:, t, :], lambda t: gv[:, t, :], TT, 512, 1e-5,
                k["ln_v"])
        with Stage(nc, "mixp") as st:
            full = st.sem("bank_full")
            with nc.Block() as block:
                @block.tensor
                def _(pe):
                    for t in range(TT):
                        for g in range(4):
                            last = nc.tensor.matmul(ps[:, t, g * P:(g + 1) * P], k["w_sT"][:, g, :],
                                                    gv[:, t, g * P:(g + 1) * P], start=True, stop=True)
                        last.then_inc(full, 1)

                @block.vector
                def _(dve):
                    for t in range(TT):
                        dve.wait_ge(full, t + 1)
                        for g in range(4):
                            cs = slice(g * P, (g + 1) * P)
                            vec.scalar_tensor_tensor(y[:, t, 512 + g * P:512 + (g + 1) * P], ps[:, t, cs],
                                                     col("b_s")[:, g:g + 1], gu[:, t, cs], ALU.add, ALU.mult)
        turn(nc, "mixu", k, TT, lambda t, c: y[:, t, c * P:(c + 1) * P], [plain(nc, hT[:, c, :]) for c in range(DC)])
    project_onto(nc, "mixo", k, hT, i["w_out"][0], x, 1.0)


def project_onto(nc, name, k, hT, w, x, alpha):
    chunks = [chunk_of(w, a, a + 512) for a in (0, 512)]
    items = []
    for c in range(2):
        for t in range(TT):
            xs = x[:, t, c * 512:(c + 1) * 512]
            items.append(by_token(c, hT, t, 0, 512, "dve", lambda eng, src, xs=xs: eng.scalar_tensor_tensor(
                xs, xs, alpha, src, ALU.mult, ALU.add)))
    dense(nc, name, k, chunks, items, ring=2)


def cross_attention(nc, k, x, hT, col, i):
    MT = i["mem"].shape[1] // P
    M = MT * P
    with Stage(nc, "xa") as sx:
        h = sx.sb("h", [P, TT, D])
        qT = sx.sb("qT", [P, DC, S])
        kT = sx.sb("kT", [P, DC, M])
        v = sx.sb("v", [P, MT, D])
        mT = sx.sb("mT", [P, DC, M])
        m = sx.sb("m", [P, MT, D])
        load(nc, "xal", [(m[:], i["mem"][0].rearrange("(t p) d -> p t d", p=P))])
        rms_rows(nc, "xam", lambda t: m[:, t, :], lambda t: m[:, t, :], MT, D, 1e-6)
        turn(nc, "xat", k, MT, lambda t, c: m[:, t, c * P:(c + 1) * P],
             [plain(nc, mT[:, c, :], col("g_mem")[:, c:c + 1]) for c in range(DC)])
        rms_rows(nc, "xan", lambda t: x[:, t, :], lambda t: h[:, t, :], TT, D, 1e-6)
        turn(nc, "xau", k, TT, lambda t, c: h[:, t, c * P:(c + 1) * P],
             [plain(nc, hT[:, c, :], col("g_xattn")[:, c:c + 1]) for c in range(DC)])
        wq, wkv = i["w_q_x"][0], i["w_kv_x"][0]
        chunks = [chunk_of(wq, a, a + 512) for a in (0, 512)] + [chunk_of(wkv, a, a + 512) for a in range(0, 2048, 512)]
        items = []
        eng = lambda n: "act" if n % 2 else "dve"
        for c in range(2):
            for j in range(4):
                items.append(by_feature(c, hT, j * P, eng(j), plain(nc, qT[:, 4 * c + j, :])))
        for c in range(2):
            for j in range(4):
                items.append(by_feature(2 + c, mT, j * P, eng(j), plain(nc, kT[:, 4 * c + j, :]), n=M))
        for c in range(2):
            for t in range(MT):
                items.append(by_token(4 + c, mT, t, 0, 512, eng(t), plain(nc, v[:, t, c * 512:(c + 1) * 512])))
        dense(nc, "xaw", k, chunks, items)
        units = [Unit(hd, t, 0, M, hd * TT + t) for hd in range(4) for t in range(TT)]
        attention(nc, "xaa", k, "softmax", units,
                  lambda hd, t: [qT[:, 2 * hd + j, t * P:(t + 1) * P] for j in range(2)],
                  lambda hd, lo, hi: [kT[:, 2 * hd + j, lo:hi] for j in range(2)],
                  lambda hd, c: v[:, c, hd * 256:(hd + 1) * 256], lambda hd, t: h[:, t, hd * 256:(hd + 1) * 256],
                  256, 256 ** -0.5)
        turn(nc, "xav", k, TT, lambda t, c: h[:, t, c * P:(c + 1) * P], [plain(nc, hT[:, c, :]) for c in range(DC)])
    project_onto(nc, "xao", k, hT, i["w_o_x"][0], x, 1.0)


def rope_tables(nc, k, positions, cs):
    vec, sca = nc.vector, nc.scalar
    two_pi = 2 * np.pi
    c1 = float(np.float32(round(two_pi * 256) / 256))
    c2 = float(np.float32(round((two_pi - c1) * 2 ** 20) / 2 ** 20))
    c3 = float(np.float32(two_pi - c1 - c2))
    shift = 12582912.0
    with Stage(nc, "rope") as st:
        pi = st.sb("pi", [P, TT], I32)
        pf = st.sb("pf", [P, TT])
        ang = st.sb("ang", [P, 4, TT, 16])
        landed, chain, ready, sined = (st.sem(n) for n in ("landed", "dve_chain", "ready", "sined"))
        with nc.Block() as block:
            @block.sync
            def _(sp):
                sp.dma_start(pi[:], positions).then_inc(landed, 16)

            @block.vector
            def _(dve):
                link = Chain(dve, chain)
                dve.wait_ge(landed, 16)
                link(vec.tensor_copy(pf[:], pi[:]))
                link(vec.tensor_tensor(ang[:, 0], pf[:].unsqueeze(2).to_broadcast([P, TT, 16]),
                                       k["rows"]["inv_freq"].unsqueeze(1).to_broadcast([P, TT, 16]), ALU.mult))
                link(vec.tensor_scalar(ang[:, 1], ang[:, 0], float(1 / two_pi), shift, ALU.mult, ALU.add))
                link(vec.tensor_scalar(ang[:, 1], ang[:, 1], -shift, None, ALU.add))
                for c in (c1, c2, c3):
                    link(vec.scalar_tensor_tensor(ang[:, 0], ang[:, 1], -c, ang[:, 0], ALU.mult, ALU.add))
                link(vec.tensor_scalar(ang[:, 0], ang[:, 0], float(np.float32(3.141592)), float(np.float32(-3.141592)),
                                       ALU.min, ALU.max))
                link(vec.scalar_tensor_tensor(ang[:, 2], ang[:, 0], -1.0, ang[:, 0], ALU.mult, ALU.min))
                vec.tensor_scalar(ang[:, 3], ang[:, 2], float(np.pi / 2), None, ALU.add).then_inc(ready, 1)

            @block.scalar
            def _(act):
                act.wait_ge(ready, 1)
                sca.activation(cs[:, 0], ang[:, 3], ACT.Sin)
                sca.activation(cs[:, 1], ang[:, 0], ACT.Sin)


def token_mixer(nc, name, k, x, hT, col, i, l):
    ps, vec, sca = k["ps"], nc.vector, nc.scalar
    alpha = (2.0 * 2) ** 0.25
    H = 4
    with Stage(nc, name) as sx:
        ys = sx.sb("ys", [P, TT, D])
        turn(nc, name + "t", k, TT, lambda t, c: x[:, t, c * P:(c + 1) * P], [plain(nc, hT[:, c, :]) for c in range(DC)])
        with Stage(nc, name + "a") as sa:
            za = sa.sb("za", [P, TT, 416])
            sbqk = sa.sb("sbqk", [P, 4, S])
            sbv = sa.sb("sbv", [P, TT, 256])
            fxqk = sa.sb("fxqk", [P, 4, S])
            fxv = sa.sb("fxv", [P, TT, 256])
            fxf = sa.sb("fxf", [P, TT, 4])
            ca = sa.sb("ca", [P, 2, S + 30])
            cg = sa.sb("cg", [P, 2, S])
            w = i["w_in_2"][l]
            spans = ((0, 416), (416, 928), (928, 1184), (1184, 1696), (1696, 2208), (2208, 2468))
            chunks = [chunk_of(w, a, b) for a, b in spans]
            eng = lambda n: "act" if n % 2 else "dve"
            items = []
            for t in range(TT):
                items.append(by_token(0, hT, t, 0, 416, eng(t), plain(nc, za[:, t, :])))
            for j in range(4):
                items.append(by_feature(1, hT, j * P, eng(j), (lambda e, src, j=j: e.tensor_scalar(
                    sbqk[:, j, :], src, 64 ** -0.5, None, ALU.mult) if e is nc.vector else e.activation(
                    sbqk[:, j, :], src, ACT.Identity, scale=64 ** -0.5)) if j < 2 else plain(nc, sbqk[:, j, :])))
            for t in range(TT):
                items.append(by_token(2, hT, t, 0, 256, eng(t), plain(nc, sbv[:, t, :])))
            for j in range(4):
                items.append(by_feature(3, hT, j * P, "dve", plain(nc, ca[:, j, 30:])) if j < 2 else
                             by_feature(3, hT, j * P, "act", lambda e, src, j=j: e.activation(cg[:, j - 2, :], src, ACT.Sigmoid)))
            for j in range(4):
                items.append(by_feature(4, hT, j * P, eng(j), plain(nc, fxqk[:, j, :])))
            for t in range(TT):
                items.append(by_token(5, hT, t, 0, 256, eng(t), plain(nc, fxv[:, t, :])))
            for t in range(TT):
                items.append(by_token(5, hT, t, 256, 260, "dve", lambda e, src, t=t: e.tensor_tensor(
                    fxf[:, t, :], src, k["rows"][f"b_forget{l}"], ALU.add)))
            dense(nc, name + "w", k, chunks, items)

            with Stage(nc, name + "m") as sm:
                cT = sm.sb("cT", [P, 3, S])
                wuq = sm.sb("wuq", [P, 2, 384])
                wukv = sm.sb("wukv", [P, 512])
                qf = sm.sb("qf", [P, TT, H, 96])
                kf = sm.sb("kf", [P, TT, H, 96])
                v = sm.sb("v", [P, TT, H, 64])
                rot = sm.sb("rot", [P, 4, TT, H, 16])
                qkT = sm.sb("qkT", [96, 2 * H, S])
                load(nc, name + "ml", [(wuq[:], i["mla_w_uq_2"][l].rearrange("(c p) n -> p c n", p=P)),
                                       (wukv[:], i["mla_w_ukv_2"][l])])
                rms_rows(nc, name + "mq", lambda t: za[:, t, 0:256], lambda t: za[:, t, 0:256], TT, 256, 1e-5)
                rms_rows(nc, name + "mk", lambda t: za[:, t, 256:384], lambda t: za[:, t, 256:384], TT, 128, 1e-5)
                turn(nc, name + "mt", k, TT, lambda t, c: za[:, t, c * P:(c + 1) * P],
                     [plain(nc, cT[:, c, :], (col(f"q_norm{l}")[:, c:c + 1] if c < 2 else col(f"kv_norm{l}"))) for c in range(3)])
                with Stage(nc, name + "mu") as st:
                    full, q_out, chain = st.sem("bank_full"), st.sem("q_out"), st.sem("dve_chain")
                    with nc.Block() as block:
                        @block.tensor
                        def _(pe):
                            for t in range(TT):
                                for c in range(2):
                                    last = nc.tensor.matmul(ps[:, t, 0:384], cT[:, c, t * P:(t + 1) * P], wuq[:, c, :],
                                                            start=c == 0, stop=c == 1)
                                last.then_inc(full, 1)
                            for t in range(TT):
                                nc.tensor.matmul(ps[:, 4 + t, :], cT[:, 2, t * P:(t + 1) * P], wukv[:],
                                                 start=True, stop=True).then_inc(full, 1)

                        @block.scalar
                        def _(act):
                            act.wait_ge(full, TT)
                            for t in range(TT):
                                last = sca.activation(qf[:, t], ps[:, t, 0:384].rearrange("p (h d) -> p h d", h=H), ACT.Identity)
                            last.then_inc(q_out, 1)
                            for t in range(TT):
                                act.wait_ge(full, TT + t + 1)
                                kv = ps[:, 4 + t, :].rearrange("p (h d) -> p h d", h=H)
                                sca.activation(kf[:, t, :, 0:64], kv[:, :, 0:64], ACT.Identity)
                                sca.activation(v[:, t], kv[:, :, 64:], ACT.Identity)

                        @block.vector
                        def _(dve):
                            link = Chain(dve, chain)

                            def rotate(src, heads, write):
                                x1, x2 = src(0), src(16)
                                cs = [k["cs"][:, j].unsqueeze(2).to_broadcast([P, TT, heads, 16]) if heads > 1 else k["cs"][:, j]
                                      for j in range(2)]
                                r = [rot[:, j] if heads > 1 else rot[:, j, :, 0, :] for j in range(4)]
                                vec.tensor_tensor(r[0], x1, cs[0], ALU.mult)
                                vec.tensor_tensor(r[1], x2, cs[1], ALU.mult)
                                vec.tensor_tensor(r[2], x2, cs[0], ALU.mult)
                                link(vec.tensor_tensor(r[3], x1, cs[1], ALU.mult))
                                write(r)

                            def write_k(r):
                                for h in range(H):
                                    vec.tensor_tensor(kf[:, :, h, 64:80], r[0], r[1], ALU.subtract)
                                    last = vec.tensor_tensor(kf[:, :, h, 80:96], r[2], r[3], ALU.add)
                                link(last)

                            def write_q(r):
                                vec.tensor_tensor(qf[:, :, :, 64:80], r[0], r[1], ALU.subtract)
                                vec.tensor_tensor(qf[:, :, :, 80:96], r[2], r[3], ALU.add)

                            rotate(lambda a: za[:, :, 384 + a:400 + a], 1, write_k)
                            dve.wait_ge(q_out, 1)
                            rotate(lambda a: qf[:, :, :, 64 + a:80 + a], H, write_q)
                with Stage(nc, name + "mv") as st:
                    full = st.sem("bank_full")
                    with nc.Block() as block:
                        @block.tensor
                        def _(pe):
                            for j in range(2 * H):
                                src = (qf if j < H else kf)
                                for t in range(TT):
                                    last = nc.tensor.transpose(ps[0:96, j, t * P:(t + 1) * P], src[:, t, j % H, :], k["ident"][:])
                                last.then_inc(full, 1)

                        @block.scalar
                        def _(act):
                            for j in range(0, 2 * H, 2):
                                act.wait_ge(full, j + 1)
                                sca.activation(qkT[:, j, :], ps[0:96, j, :], ACT.Identity)

                        @block.vector
                        def _(dve):
                            for j in range(1, 2 * H, 2):
                                dve.wait_ge(full, j + 1)
                                vec.tensor_copy(qkT[:, j, :], ps[0:96, j, :])
                attention(nc, name + "ma", k, "softmax", causal_units(k["mask_le"]),
                          lambda h, t: qkT[:, h, t * P:(t + 1) * P], lambda h, lo, hi: qkT[:, H + h, lo:hi],
                          lambda h, c: v[:, c, h, :], lambda h, t: ys[:, t, h * 64:(h + 1) * 64], 64, 96 ** -0.5)

            def half(buf, j0):
                return lambda h, lo, hi: buf[64 * (h % 2):64 * (h % 2) + 64, j0 + h // 2, lo:hi]

            attention(nc, name + "sa", k, "stick", causal_units(k["mask_lt"]),
                      lambda h, t: half(sbqk, 0)(h, t * P, (t + 1) * P), half(sbqk, 2),
                      lambda h, c: sbv[:, c, h * 64:(h + 1) * 64], lambda h, t: ys[:, t, 256 + h * 64:256 + (h + 1) * 64],
                      64, 1.0)
            with Stage(nc, name + "f") as sf:
                b = sf.sb("b", [P, TT, 4])
                r = sf.sb("r", [P, TT, 4])
                rows = sf.sb("rows", [P, 4, S])
                running_log_sigmoid(nc, name + "fs", k, fxf[:], 4, 4, b[:])
                with nc.Block() as block:
                    @block.vector
                    def _(dve):
                        vec.tensor_scalar(r[:], b[:], -1.0, None, ALU.mult)
                spread_rows(nc, name + "fr", k, r, 4, rows)
                attention(nc, name + "fa", k, "decayed", causal_units(k["mask_le"], lambda h: rows[:, h, :]),
                          lambda h, t: half(fxqk, 0)(h, t * P, (t + 1) * P), half(fxqk, 2),
                          lambda h, c: fxv[:, c, h * 64:(h + 1) * 64], lambda h, t: ys[:, t, 768 + h * 64:768 + (h + 1) * 64],
                          64, 64 ** -0.5)
            with Stage(nc, name + "c") as st:
                acc = st.sb("acc", [P, 2, S])
                cn = st.sb("cn", [P, TT, 256])
                ready, tapped, full = st.sem("ready"), st.sem("tapped"), st.sem("bank_full")
                with nc.Block() as block:
                    @block.vector
                    def _(dve):
                        vec.memset(ca[:, :, 0:30], 0.0)
                        vec.tensor_tensor(ca[:, :, 30:], ca[:, :, 30:], cg[:], ALU.mult).then_inc(ready, 1)
                        dve.wait_ge(ready, 1)
                        for j in range(31):
                            for c in range(2):
                                wj = col(f"conv_w2{l}")[:, 2 * j + c:2 * j + c + 1]
                                src = ca[:, c, j:j + S]
                                if j == 0:
                                    vec.tensor_scalar(acc[:, c, :], src, wj, col(f"conv_b2{l}")[:, c:c + 1], ALU.mult,
                                                      ALU.add).then_inc(tapped, 1)
                                else:
                                    dve.wait_ge(tapped, 2 * (j - 1) + c + 1)
                                    vec.scalar_tensor_tensor(acc[:, c, :], src, wj, acc[:, c, :], ALU.mult,
                                                             ALU.add).then_inc(tapped, 1)
                        dve.wait_ge(full, 1)
                        vec.tensor_copy(cn[:], ps[:, 0:TT, 0:256])

                    @block.tensor
                    def _(pe):
                        pe.wait_ge(tapped, 62)
                        for t in range(TT):
                            for c in range(2):
                                last = nc.tensor.transpose(ps[:, t, c * P:(c + 1) * P], acc[:, c, t * P:(t + 1) * P], k["ident"][:])
                        last.then_inc(full, 1)
                ln_rows(nc, name + "cl", lambda t: cn[:, t, :], lambda t: ys[:, t, 512:768], TT, 256, 1e-5)
        with Stage(nc, name + "p") as sp_:
            ysT = sp_.sb("ysT", [P, DC, S])
            merged = sp_.sb("merged", [P, DC, S])

            def out_of(c):
                if c in (4, 5):
                    j = c - 4
                    return lambda e, src: e.activation(ysT[:, c, :], src, ACT.Silu, scale=col(f"ln_g2{l}")[:, j:j + 1],
                                                       bias=col(f"ln_b2{l}")[:, j:j + 1])
                return plain(nc, ysT[:, c, :])

            order = [4, 0, 5, 1, 2, 3, 6, 7]
            turn(nc, name + "pt", k, TT, lambda t, n: ys[:, t, order[n] * P:(order[n] + 1) * P], [out_of(c) for c in order])
            gated_projection(nc, name + "g", k, hT, ysT, merged, i["w_in_2"][l][:, 2468:], i["w_branch_2"][l],
                             col(f"b_gate{l}"))
            project_onto(nc, name + "o", k, merged, i["w_o_2"][l], x, alpha)


def gated_projection(nc, name, k, hT, ysT, merged, w_gates, w_branch, b_gate):
    ps, vec, sca = k["ps"], nc.vector, nc.scalar
    RING = 3
    order = [(n, half) for half in range(2) for n in range(4)]
    with Stage(nc, name) as st:
        w = st.sb("w", [P, RING, DC, 512])
        wb = st.sb("wb", [P, 4, 2, D])
        sg = st.sb("sg", [P, 2, S])
        gp = st.sb("gp", [P, 2, S])
        landed = [st.sem(f"weights_landed{n}") for n in range(RING)]
        branch_landed, gate_full, proj_full, sig_ready, prod_ready, merged_ready = (
            st.sem(n) for n in ("branch_landed", "gate_full", "proj_full", "sig_ready", "prod_ready", "merged_ready"))
        N = 4 * len(order)
        with nc.Block() as block:
            @block.sync
            def _(sp):
                for c, (n, half) in enumerate(order):
                    if c >= RING:
                        sp.wait_ge(gate_full, 4 * (c - RING) + 4)
                    a = n * D + half * 512
                    sp.dma_start(w[:, c % RING], chunk_of(w_gates, a, a + 512)).then_inc(landed[c % RING], 16)
                    if c == 0:
                        sp.dma_start(wb[:], w_branch.rearrange("n (c p) d -> p n c d", p=P)).then_inc(branch_landed, 16)

            @block.tensor
            def _(pe):
                for u in range(N):
                    c, j = u // 4, u % 4
                    n, half = order[c]
                    if j == 0:
                        pe.wait_ge(landed[c % RING], 16 * (c // RING + 1))
                    if u >= 4:
                        pe.wait_ge(sig_ready, u - 3)
                    for q in range(DC):
                        last = nc.tensor.matmul(ps[:, u % 4, :], w[:, c % RING, q, j * P:(j + 1) * P], hT[:, q, :],
                                                start=q == 0, stop=q == DC - 1)
                    last.then_inc(gate_full, 1)
                    if u == 0:
                        pe.wait_ge(branch_landed, 16)
                    if u >= 4:
                        pe.wait_ge(prod_ready, u - 3)
                    d = half * 512 + j * P
                    for q in range(2):
                        last = nc.tensor.matmul(ps[:, 4 + u % 4, :], wb[:, n, q, d:d + P], ysT[:, 2 * n + q, :],
                                                start=q == 0, stop=q == 1)
                    last.then_inc(proj_full, 1)

            @block.scalar
            def _(act):
                for u in range(N):
                    n, half = order[u // 4]
                    g = n * DC + half * 4 + u % 4
                    act.wait_ge(gate_full, u + 1)
                    if u >= 2:
                        act.wait_ge(prod_ready, u - 1)
                    sca.activation(sg[:, u % 2, :], ps[:, u % 4, :], ACT.Sigmoid, bias=b_gate[:, g:g + 1]).then_inc(sig_ready, 1)

            @block.vector
            def _(dve):
                for u in range(N):
                    n, half = order[u // 4]
                    dst = merged[:, half * 4 + u % 4, :]
                    dve.wait_ge(proj_full, u + 1)
                    dve.wait_ge(sig_ready, u + 1)
                    out = dst if n == 0 else gp[:, u % 2, :]
                    if u >= 2:
                        dve.wait_ge(merged_ready, u - 1)
                    vec.tensor_tensor(out, ps[:, 4 + u % 4, :], sg[:, u % 2, :], ALU.mult).then_inc(prod_ready, 1)
                    dve.wait_ge(prod_ready, u + 1)
                    if n:
                        vec.tensor_tensor(dst, dst, out, ALU.add).then_inc(merged_ready, 1)
                    else:
                        dve.sem_inc(merged_ready, 1)


def program(nc, i, out, dump=None):
    with ExitStack() as ctx:
        ps = ctx.enter_context(nc.psum_tensor("ps", [P, 8, 512], F32))
        with Stage(nc, "all") as st:
            x = st.sb("x", [P, TT, D])
            hT = st.sb("hT", [P, DC, S])
            k = constants(nc, st, ps)
            columns = st.sb("columns", [P, COLS.width])
            small = st.sb("small", [P, 16 + 16 + 8])
            cs = st.sb("cs", [P, 2, TT, 16])
            k["cs"] = cs
            k["rows"] = {"gate_b": small[:, 0:16], "inv_freq": small[:, 16:32], "b_forget0": small[:, 32:36],
                         "b_forget1": small[:, 36:40]}
            col = lambda n: columns[:, COLS.at[n][0]:COLS.at[n][1]]

            def row(n):
                a, b = ROWS_.at[n]
                return i["rows"][a:b].partition_broadcast(P)

            load(nc, "ld", [(x[:], i["x"][0].rearrange("(t p) d -> p t d", p=P)), (columns[:], i["columns"])]
                 + [(k["rows"][n], row(n)) for n in k["rows"]])
            rope_tables(nc, k, i["positions"], cs)
            with Stage(nc, "m1") as s1:
                w_sT = s1.sb("w_sT", [P, 4, P])
                g_head = s1.sb("g_head", [P, 512])
                ln_v = s1.sb("ln_v", [P, 2, 512])
                load(nc, "ld1", [(w_sT[:], i["w_sT"]), (g_head[:], row("g_head")), (ln_v[:, 0], row("ln_v_g")),
                                 (ln_v[:, 1], row("ln_v_b"))])
                k["w_sT"], k["ln_v"] = w_sT, ln_v
                k["rows"]["g_head"] = g_head[:]
                mixer_one(nc, k, x, hT, col, i)
            dump and dump("mix", x)
            cross_attention(nc, k, x, hT, col, i)
            dump and dump("xa", x)
            with Stage(nc, "m3") as s3:
                h = s3.sb("h", [P, TT, D])
                rms_rows(nc, "m3n", lambda t: x[:, t, :], lambda t: h[:, t, :], TT, D, 1e-6)
                turn(nc, "m3t", k, TT, lambda t, c: h[:, t, c * P:(c + 1) * P],
                     [plain(nc, hT[:, c, :], col("g_moe")[:, c:c + 1]) for c in range(DC)])
                moe(nc, "e0", k, x, hT, h[:], col("g_moe"), i["w_rg"][0], i["b_rg"][0], i["w_re"][0], i["b_re"][0],
                    i["w_gate"][0], i["w_up"][0], i["w_down"][0])
            with Stage(nc, "m4") as s4:
                g = s4.sb("g", [P, D])
                load(nc, "ld4", [(g[:], row("g_final"))])
                rms_rows(nc, "m4n", lambda t: x[:, t, :], lambda t: x[:, t, :], TT, D, 1e-6)
                with nc.Block() as block:
                    @block.vector
                    def _(dve):
                        for t in range(TT):
                            nc.vector.tensor_tensor(x[:, t, :], x[:, t, :], g[:], ALU.mult)
            dump and dump("first", x)
            for l in range(2):
                token_mixer(nc, f"t{l}", k, x, hT, col, i, l)
                dump and dump(f"tm{l}", x)
                for j in (1, 2):
                    if j == 2:
                        turn(nc, f"r{l}t", k, TT, lambda t, c: x[:, t, c * P:(c + 1) * P],
                             [plain(nc, hT[:, c, :]) for c in range(DC)])
                        alpha = (2.0 * 2) ** 0.25
                        moe(nc, f"e{l + 1}", k, x, hT, x[:], None, i["w_router_group_2"][l], i["b_router_group_2"][l],
                            i["w_router_expert_2"][l], i["b_router_expert_2"][l], i["w_exp_gate_2"][l], i["w_exp_up_2"][l],
                            i["w_exp_down_2"][l], alpha)
                    with Stage(nc, f"l{l}{j}") as sl:
                        rows = sl.sb("rows", [P, 2, D])
                        load(nc, f"ll{l}{j}", [(rows[:, 0], row(f"ln{j}_g{l}")), (rows[:, 1], row(f"ln{j}_b{l}"))])
                        ln_rows(nc, f"ln{l}{j}", lambda t: x[:, t, :], lambda t: x[:, t, :], TT, D, 1e-5, rows)
                    dump and dump(f"ln{l}{j}", x)
            with Stage(nc, "end") as se:
                stored = se.sem("stored")
                with nc.Block() as block:
                    @block.sync
                    def _(sp):
                        sp.dma_start(out[0].rearrange("(t p) d -> p t d", p=P), x[:]).then_inc(stored, 16)
                        sp.wait_ge(stored, 16)


def columns_of(inputs):
    def cols_(v):
        return v.reshape(-1, P).T

    parts = {"g_mix": cols_(inputs["g_mix"]), "g_xattn": cols_(inputs["g_xattn"]), "g_mem": cols_(inputs["g_mem"]),
             "g_moe": cols_(inputs["g_moe"]), "conv_w": cols_(inputs["conv_w"]), "conv_b": cols_(inputs["conv_b"]),
             "b_s": inputs["b_s"][0].T}
    for l in range(2):
        for n, src in (("b_gate", "b_gate_2"), ("q_norm", "mla_q_norm_2"), ("kv_norm", "mla_kv_norm_2"),
                       ("conv_w2", "conv_w_2"), ("conv_b2", "conv_b_2"), ("ln_g2", "conv_ln_g_2"), ("ln_b2", "conv_ln_b_2")):
            parts[f"{n}{l}"] = cols_(inputs[src][l])
    return np.ascontiguousarray(np.concatenate([parts[n] for n in COLS.at], axis=1))


def rows_of(inputs):
    parts = {"gate_b": inputs["gate_b"][0], "g_head": inputs["g_head"][0], "ln_v_g": inputs["ln_v_g"][0],
             "ln_v_b": inputs["ln_v_b"][0], "g_final": inputs["g_final"],
             "inv_freq": (np.float32(10000.0) ** (-np.arange(16, dtype=np.float32) / np.float32(16))).astype(np.float32)}
    for l in range(2):
        for n, src in (("b_forget", "b_forget_2"), ("ln1_g", "ln1_g_2"), ("ln1_b", "ln1_b_2"), ("ln2_g", "ln2_g_2"),
                       ("ln2_b", "ln2_b_2")):
            parts[f"{n}{l}"] = inputs[src][l]
    return np.ascontiguousarray(np.concatenate([parts[n] for n in ROWS_.at]))


_DIRECT = ["x", "mem", "w_in", "w_out", "w_q_x", "w_kv_x", "w_o_x", "w_rg", "b_rg", "w_re", "b_re", "w_gate", "w_up",
           "w_down", "w_in_2", "mla_w_uq_2", "mla_w_ukv_2", "w_branch_2", "w_o_2", "w_router_group_2", "b_router_group_2",
           "w_router_expert_2", "b_router_expert_2", "w_exp_gate_2", "w_exp_up_2", "w_exp_down_2"]


def laid_out(inputs):
    arrays = {n: np.ascontiguousarray(inputs[n]) for n in _DIRECT}
    arrays["columns"] = columns_of(inputs)
    arrays["rows"] = rows_of(inputs)
    arrays["w_sT"] = np.ascontiguousarray(inputs["w_s"][0].transpose(2, 0, 1))
    arrays["positions"] = np.ascontiguousarray(inputs["positions_2"].reshape(TT, P).T)
    return arrays


def kernel(**inputs):
    from concourse import bacc
    from concourse.bass_utils import run_bass_kernel_spmd

    nc = bacc.Bacc("TRN2", target_bir_lowering=False, num_devices=1)
    inputs = {n: np.asarray(a) for n, a in inputs.items()}
    arrays, aps = {}, {}
    for n, a in laid_out(inputs).items():
        arrays[f"in_{n}"] = a
        aps[n] = nc.dram_tensor(f"in_{n}", a.shape, mybir.dt.from_np(a.dtype), kind="ExternalInput").ap()
    out = nc.dram_tensor("out_0", (1, S, D), F32, kind="ExternalOutput").ap()
    program(nc, aps, out)
    return run_bass_kernel_spmd(nc, [arrays], core_ids=[0]).results[0]["out_0"]
```

```python
from contextlib import ExitStack

import numpy as np

import concourse.bass as bass
from concourse import mybir
from concourse.alu_op_type import AluOpType as ALU

P = 128
F32 = mybir.dt.float32
F32R = mybir.dt.float32r
HI, LO = 0, 1
I32 = mybir.dt.int32
U32 = mybir.dt.uint32
ACT = mybir.ActivationFunctionType
AX_X = mybir.AxisListType.X
BIG = 1e30
D = 1024
S = 512
DC = D // P
TT = S // P

NE = 32
NG = 4
EPG = NE // NG
SLOTS = 64
MAX_BLOCKS = NE + 2 * S // SLOTS
TABLE = MAX_BLOCKS + 2
ROWS = TABLE * SLOTS


class Stage:

    def __init__(self, nc, name):
        self.nc, self.name, self.stack, self.sems = nc, name, ExitStack(), []

    def __enter__(self):
        return self

    def sb(self, name, shape, dtype=F32):
        return self.stack.enter_context(self.nc.sbuf_tensor(f"{self.name}_{name}", shape, dtype))

    def sem(self, name):
        handle = self.nc.alloc_semaphore(f"{self.name}_{name}")
        self.sems.append(handle)
        return handle

    def __exit__(self, kind, value, trace):
        if kind is None:
            self.nc.clear_and_free_semaphores(self.sems)
            self.nc.all_engine_barrier()
        self.stack.close()
        return False


class Chain:

    def __init__(self, engine, semaphore):
        self.engine, self.semaphore, self.count = engine, semaphore, 0

    def __call__(self, instruction):
        self.count += 1
        instruction.then_inc(self.semaphore, 1)
        self.engine.wait_ge(self.semaphore, self.count)


def cols(ap, n):
    return ap.unsqueeze(len(ap.shape)).to_broadcast(list(ap.shape) + [n])


class Item:

    def __init__(self, chunk, operands, rows, n, engine, out):
        self.chunk, self.operands, self.rows, self.n, self.engine, self.out = chunk, operands, rows, n, engine, out


WIDTH = 256


def dense(nc, name, k, chunks, items, raw_ring=3, side=None, before=None):
    ps = k["ps"]
    widest = max(c.shape[2] for c in chunks)
    deepest = max(c.shape[1] for c in chunks)
    last_item = {it.chunk: i for i, it in enumerate(items)}
    nth, counts = [], {"act": 0, "dve": 0}
    for it in items:
        counts[it.engine] += 1
        nth.append(counts[it.engine])
    with Stage(nc, name) as st:
        raw = st.sb("raw", [P, raw_ring, deepest, widest])
        w = st.sb("w", [P, 2, 2, deepest, widest], F32R)
        landed = [st.sem(f"weights_landed{i}") for i in range(raw_ring)]
        high_ready = st.sem("high_ready")
        low_ready = st.sem("low_ready")
        bank_full = st.sem("bank_full")
        emptied = {"act": st.sem("emptied_by_act"), "dve": st.sem("emptied_by_dve")}

        def raw_of(c):
            return raw[:, c % raw_ring, 0:chunks[c].shape[1], 0:chunks[c].shape[2]]

        def part_of(c, part):
            return w[:, c % 2, part, 0:chunks[c].shape[1], 0:chunks[c].shape[2]]

        if before is not None:
            before.begin(st)

        with nc.Block() as block:
            @block.sync
            def _(sp):
                for c, dram in enumerate(chunks):
                    if c >= raw_ring:
                        sp.wait_ge(low_ready, c - raw_ring + 1)
                    sp.dma_start(raw_of(c), dram).then_inc(landed[c % raw_ring], 16)

            @block.tensor
            def _(pe):
                if before is not None:
                    before.pe(pe)
                    pe.wait_ge(before.low_ready, before.n)
                for i, it in enumerate(items):
                    pe.wait_ge(low_ready, it.chunk + 1)
                    if i >= 8:
                        pe.wait_ge(emptied[items[i - 8].engine], nth[i - 8])
                    pairs = it.operands(w[:, it.chunk % 2])
                    for j, (stationary, moving) in enumerate(pairs):
                        last = nc.tensor.matmul(ps[0:it.rows, i % 8, 0:it.n], stationary, moving,
                                                start=j == 0, stop=j == len(pairs) - 1)
                    last.then_inc(bank_full, 1)

            @block.scalar
            def _(act):
                def high(c):
                    act.wait_ge(landed[c % raw_ring], 16 * (c // raw_ring + 1))
                    if c >= 2:
                        act.wait_ge(bank_full, last_item[c - 2] + 1)
                    nc.scalar.copy(part_of(c, HI), raw_of(c)).then_inc(high_ready, 1)

                if before is not None:
                    before.act(act)
                high(0)
                for c in range(len(chunks)):
                    if c + 1 < len(chunks):
                        high(c + 1)
                    for i, it in enumerate(items):
                        if it.chunk == c and it.engine == "act":
                            act.wait_ge(bank_full, i + 1)
                            it.out(nc.scalar, ps[0:it.rows, i % 8, 0:it.n]).then_inc(emptied["act"], 1)

            @block.vector
            def _(dve):
                def low(c):
                    dve.wait_ge(high_ready, c + 1)
                    nc.vector.tensor_tensor(part_of(c, LO), raw_of(c), part_of(c, HI), ALU.subtract).then_inc(low_ready, 1)

                if before is not None:
                    before.dve(dve)
                low(0)
                for c in range(len(chunks)):
                    if c + 1 < len(chunks):
                        low(c + 1)
                    for i, it in enumerate(items):
                        if it.chunk == c and it.engine == "dve":
                            dve.wait_ge(bank_full, i + 1)
                            it.out(nc.vector, ps[0:it.rows, i % 8, 0:it.n]).then_inc(emptied["dve"], 1)
                    if side is not None:
                        side(dve, c, emptied)


def chunk_of(w_dram, a, b):
    return w_dram.rearrange("(c p) n -> p c n", p=P)[:, :, a:b]


PARTS = ((HI, HI), (HI, LO), (LO, HI))


def by_token(chunk, hT, t, a, b, engine, out, kc=DC):
    return Item(chunk, lambda w: [(hT[:, p, c, t * P:(t + 1) * P], w[:, q, c, a:b]) for c in range(kc) for p, q in PARTS],
                P, b - a, engine, out)


def by_feature(chunk, hT, a, engine, out, n=S, kc=DC):
    return Item(chunk, lambda w: [(w[:, p, c, a:a + P], hT[:, q, c, 0:n]) for c in range(kc) for p, q in PARTS],
                P, n, engine, out)


def turn(nc, name, k, tiles, src, outs):
    ps = k["ps"]
    with Stage(nc, name) as st:
        full = st.sem("bank_full")
        emptied = [st.sem("emptied_by_act"), st.sem("emptied_by_dve")]
        with nc.Block() as block:
            @block.tensor
            def _(pe):
                for c in range(len(outs)):
                    if c >= 8:
                        pe.wait_ge(emptied[c % 2], (c - 8) // 2 + 1)
                    for t in range(tiles):
                        last = nc.tensor.transpose(ps[:, c % 8, t * P:(t + 1) * P], src(t, c), k["ident"][:])
                    last.then_inc(full, 1)

            @block.scalar
            def _(act):
                for c in range(0, len(outs), 2):
                    act.wait_ge(full, c + 1)
                    outs[c](nc.scalar, ps[:, c % 8, 0:tiles * P]).then_inc(emptied[0], 1)

            @block.vector
            def _(dve):
                for c in range(1, len(outs), 2):
                    dve.wait_ge(full, c + 1)
                    outs[c](nc.vector, ps[:, c % 8, 0:tiles * P]).then_inc(emptied[1], 1)


class TurnSplit:

    def __init__(self, nc, k, tiles, src, dst, n, factor=None):
        self.nc, self.k, self.tiles, self.src, self.dst, self.n, self.factor = nc, k, tiles, src, dst, n, factor

    def begin(self, st):
        self.full, self.high_ready, self.low_ready = (st.sem(n) for n in ("turn_full", "turn_high_ready", "turn_low_ready"))

    def bank(self, c):
        return self.k["ps"][:, c, 0:self.tiles * P]

    def pe(self, pe):
        for c in range(self.n):
            for t in range(self.tiles):
                last = self.nc.tensor.transpose(self.bank(c)[:, t * P:(t + 1) * P], self.src(t, c), self.k["ident"][:])
            last.then_inc(self.full, 1)

    def act(self, act):
        for c in range(self.n):
            act.wait_ge(self.full, c + 1)
            scale = 1.0 if self.factor is None else self.factor[:, c:c + 1]
            self.nc.scalar.activation(self.dst[:, HI, c, :], self.bank(c), ACT.Identity, scale=scale).then_inc(self.high_ready, 1)

    def dve(self, dve):
        vec = self.nc.vector
        for c in range(self.n):
            dve.wait_ge(self.high_ready, c + 1)
            low, high = self.dst[:, LO, c, :], self.dst[:, HI, c, :]
            if self.factor is None:
                vec.tensor_tensor(low, self.bank(c), high, ALU.subtract).then_inc(self.low_ready, 1)
            else:
                vec.scalar_tensor_tensor(low, self.bank(c), self.factor[:, c:c + 1], high, ALU.mult,
                                         ALU.subtract).then_inc(self.low_ready, 1)


class Split:

    def __init__(self, nc, src, dst, factor):
        self.nc, self.src, self.dst, self.factor, self.n = nc, src, dst, factor, src.shape[1]

    def begin(self, st):
        self.high_ready, self.low_ready = st.sem("split_high_ready"), st.sem("split_low_ready")

    def pe(self, pe):
        pass

    def act(self, act):
        for c in range(self.n):
            self.nc.scalar.activation(self.dst[:, HI, c, :], self.src[:, c, :], ACT.Identity,
                                      scale=self.factor).then_inc(self.high_ready, 1)

    def dve(self, dve):
        for c in range(self.n):
            dve.wait_ge(self.high_ready, c + 1)
            self.nc.vector.scalar_tensor_tensor(self.dst[:, LO, c, :], self.src[:, c, :], self.factor,
                                                self.dst[:, HI, c, :], ALU.mult, ALU.subtract).then_inc(self.low_ready, 1)


def turn_split(nc, name, k, tiles, src, dst, n, factor=None):
    turned = TurnSplit(nc, k, tiles, src, dst, n, factor)
    with Stage(nc, name) as st:
        turned.begin(st)
        with nc.Block() as block:
            @block.tensor
            def _(pe):
                turned.pe(pe)

            @block.scalar
            def _(act):
                turned.act(act)

            @block.vector
            def _(dve):
                turned.dve(dve)


def plain(nc, out, gain=None):
    def f(eng, src):
        if eng is nc.scalar:
            return eng.activation(out, src, ACT.Identity, scale=1.0 if gain is None else gain)
        if gain is None:
            return eng.tensor_copy(out, src)
        return eng.tensor_scalar(out, src, gain, None, ALU.mult)
    return f


def rms_rows(nc, name, parts, eps, loads=()):
    with Stage(nc, name) as st:
        junk = st.sb("junk", [P, max(width for _, _, _, width in parts)])
        ss = [st.sb(f"ss{n}", [P, 4, tiles]) for n, (_, _, tiles, _) in enumerate(parts)]
        squared, mean_ready, root_ready, chain = (st.sem(n) for n in ("squared", "mean_ready", "root_ready", "dve_chain"))
        act_chain, landed = st.sem("act_chain"), st.sem("landed")
        with nc.Block() as block:
            @block.sync
            def _(sp):
                for dst, src in loads:
                    sp.dma_start(dst, src).then_inc(landed, 16)
                if loads:
                    sp.wait_ge(landed, 16 * len(loads))

            @block.scalar
            def _(act):
                link = Chain(act, act_chain)
                for n, (x, h, tiles, width) in enumerate(parts):
                    for t in range(tiles):
                        link(nc.scalar.activation(junk[:, 0:width], x(t), ACT.Square, accum_out=ss[n][:, 0, t:t + 1]))
                act.sem_inc(squared, 1)
                act.wait_ge(mean_ready, 1)
                for n in range(len(parts)):
                    last = nc.scalar.activation(ss[n][:, 2], ss[n][:, 1], ACT.Sqrt)
                last.then_inc(root_ready, 1)

            @block.vector
            def _(dve):
                link = Chain(dve, chain)
                dve.wait_ge(squared, 1)
                for n, (x, h, tiles, width) in enumerate(parts):
                    last = nc.vector.tensor_scalar(ss[n][:, 1], ss[n][:, 0], 1.0 / width, eps, ALU.mult, ALU.add)
                last.then_inc(mean_ready, 1)
                dve.wait_ge(root_ready, 1)
                for n in range(len(parts)):
                    last = nc.vector.reciprocal(ss[n][:, 3], ss[n][:, 2])
                link(last)
                for n, (x, h, tiles, width) in enumerate(parts):
                    for t in range(tiles):
                        nc.vector.tensor_scalar(h(t), x(t), ss[n][:, 3, t:t + 1], None, ALU.mult)


def ln_rows(nc, name, x, out, tiles, width, eps, rows=None):
    with Stage(nc, name) as st:
        stats = st.sb("stats", [P, tiles, width // 256, nc.vector.BN_STATS_DIM])
        mv = st.sb("mv", [P, tiles, nc.vector.BN_AGGR_DIM])
        r = st.sb("r", [P, 3, tiles])
        chain, mean_ready, root_ready = (st.sem(n) for n in ("dve_chain", "mean_ready", "root_ready"))
        with nc.Block() as block:
            @block.vector
            def _(dve):
                link = Chain(dve, chain)
                for t in range(tiles):
                    for q in range(width // 256):
                        last = nc.vector.bn_stats(stats[:, t, q, :], x(t)[:, q * 256:(q + 1) * 256])
                link(last)
                for t in range(tiles):
                    last = nc.vector.bn_aggr(mv[:, t, :], stats[:, t])
                link(last)
                nc.vector.tensor_scalar(r[:, 0], mv[:, :, 1], eps, None, ALU.add).then_inc(mean_ready, 1)
                dve.wait_ge(root_ready, 1)
                link(nc.vector.reciprocal(r[:, 2], r[:, 1]))
                for t in range(tiles):
                    last = nc.vector.tensor_scalar(out(t), x(t), mv[:, t, 0:1], r[:, 2, t:t + 1], ALU.subtract, ALU.mult)
                link(last)
                if rows is not None:
                    for t in range(tiles):
                        last = nc.vector.tensor_tensor(out(t), out(t), rows[:, 0], ALU.mult)
                    link(last)
                    for t in range(tiles):
                        last = nc.vector.tensor_tensor(out(t), out(t), rows[:, 1], ALU.add)
                    link(last)

            @block.scalar
            def _(act):
                act.wait_ge(mean_ready, 1)
                nc.scalar.activation(r[:, 1], r[:, 0], ACT.Sqrt).then_inc(root_ready, 1)


def post_norm(nc, name, k, x, row_g, row_b, eps, hT=None):
    ps, vec, sca = k["ps"], nc.vector, nc.scalar
    with Stage(nc, name) as st:
        rows = st.sb("rows", [P, 2, D])
        stats = st.sb("stats", [P, TT, D // 256, vec.BN_STATS_DIM])
        mv = st.sb("mv", [P, TT, vec.BN_AGGR_DIM])
        r = st.sb("r", [P, 4, TT])
        (gain_landed, bias_landed, chain, mean_ready, root_ready, factors_ready, normed, scaled, shifted, full, out) = (
            st.sem(n) for n in ("gain_landed", "bias_landed", "dve_chain", "mean_ready", "root_ready", "factors_ready",
                                "normed", "scaled", "shifted", "bank_full", "turned_out"))
        with nc.Block() as block:
            @block.sync
            def _(sp):
                sp.dma_start(rows[:, 0], row_g.partition_broadcast(P)).then_inc(gain_landed, 16)
                sp.dma_start(rows[:, 1], row_b.partition_broadcast(P)).then_inc(bias_landed, 16)

            @block.vector
            def _(dve):
                link = Chain(dve, chain)
                for t in range(TT):
                    for q in range(D // 256):
                        last = vec.bn_stats(stats[:, t, q, :], x[:, t, q * 256:(q + 1) * 256])
                link(last)
                for t in range(TT):
                    last = vec.bn_aggr(mv[:, t, :], stats[:, t])
                link(last)
                vec.tensor_scalar(r[:, 0], mv[:, :, 1], eps, None, ALU.add).then_inc(mean_ready, 1)
                dve.wait_ge(root_ready, 1)
                link(vec.reciprocal(r[:, 2], r[:, 1]))
                vec.scalar_tensor_tensor(r[:, 3], mv[:, :, 0], -1.0, r[:, 2], ALU.mult, ALU.mult).then_inc(factors_ready, 1)
                dve.wait_ge(gain_landed, 16)
                for t in range(TT):
                    dve.wait_ge(normed, t + 1)
                    vec.tensor_tensor(x[:, t, :], x[:, t, :], rows[:, 0], ALU.mult).then_inc(scaled, 1)

            @block.gpsimd
            def _(pool):
                pool.wait_ge(bias_landed, 16)
                for t in range(TT):
                    pool.wait_ge(scaled, t + 1)
                    nc.gpsimd.tensor_tensor(x[:, t, :], x[:, t, :], rows[:, 1], ALU.add).then_inc(shifted, 1)

            if hT is not None:
                @block.tensor
                def _(pe):
                    for t in range(TT):
                        pe.wait_ge(shifted, t + 1)
                        for c in range(DC):
                            last = nc.tensor.transpose(ps[:, 2 * t + c // 4, c % 4 * P:(c % 4 + 1) * P],
                                                       x[:, t, c * P:(c + 1) * P], k["ident"][:])
                        last.then_inc(full, 1)

            @block.scalar
            def _(act):
                act.wait_ge(mean_ready, 1)
                sca.activation(r[:, 1], r[:, 0], ACT.Sqrt).then_inc(root_ready, 1)
                act.wait_ge(factors_ready, 1)
                for t in range(TT):
                    sca.activation(x[:, t, :], x[:, t, :], ACT.Identity, scale=r[:, 2, t:t + 1],
                                   bias=r[:, 3, t:t + 1]).then_inc(normed, 1)
                if hT is not None:
                    for t in range(TT):
                        act.wait_ge(full, t + 1)
                        sca.copy(hT[:, :, t * P:(t + 1) * P].rearrange("p (b c) s -> p b c s", b=2),
                                 ps[:, 2 * t:2 * t + 2, :].rearrange("p b (c s) -> p b c s", s=P)).then_inc(out, 1)


def final_norm(nc, name, x, row_g, eps):
    vec, sca = nc.vector, nc.scalar
    with Stage(nc, name) as st:
        row = st.sb("row", [P, D])
        junk = st.sb("junk", [P, D])
        ss = st.sb("ss", [P, 4, TT])
        landed, squared, mean_ready, root_ready, chain, act_chain = (
            st.sem(n) for n in ("gain_landed", "squared", "mean_ready", "root_ready", "dve_chain", "act_chain"))
        with nc.Block() as block:
            @block.sync
            def _(sp):
                sp.dma_start(row[:], row_g.partition_broadcast(P)).then_inc(landed, 16)

            @block.scalar
            def _(act):
                link = Chain(act, act_chain)
                for t in range(TT):
                    link(sca.activation(junk[:], x[:, t, :], ACT.Square, accum_out=ss[:, 0, t:t + 1]))
                act.sem_inc(squared, 1)
                act.wait_ge(mean_ready, 1)
                sca.activation(ss[:, 2], ss[:, 1], ACT.Sqrt).then_inc(root_ready, 1)

            @block.vector
            def _(dve):
                link = Chain(dve, chain)
                dve.wait_ge(squared, 1)
                vec.tensor_scalar(ss[:, 1], ss[:, 0], 1.0 / D, eps, ALU.mult, ALU.add).then_inc(mean_ready, 1)
                dve.wait_ge(root_ready, 1)
                link(vec.reciprocal(ss[:, 3], ss[:, 2]))
                dve.wait_ge(landed, 16)
                for t in range(TT):
                    vec.scalar_tensor_tensor(x[:, t, :], x[:, t, :], ss[:, 3, t:t + 1], row[:], ALU.mult, ALU.mult)


class Unit:

    def __init__(self, head, tile, lo, hi, column, mask=None, row=None, shift=None, add=False):
        self.head, self.tile, self.lo, self.hi = head, tile, lo, hi
        self.column, self.mask, self.row, self.shift, self.add = column, mask, row, shift, add


def causal_units(mask, row=None):
    units = []
    for h in range(4):
        for i in range(TT):
            hi = (i + 1) * P
            units.append(Unit(h, i, 0, hi, h * TT + i, mask[:, S - P - i * P:S - P - i * P + hi], row and row(h)[:, 0:hi]))
    return units


def attention(nc, name, k, kind, units, query, key, value, out, dv, scale, branches=None):
    ps, ident, vec, sca = k["ps"], k["ident"], nc.vector, nc.scalar
    U = len(units)
    late = 1 if kind in ("stick", "mlstm") else 0
    with Stage(nc, name) as st:
        lg = st.sb("logits", [P, 3, S])
        tmp = st.sb("between", [P, 2, S])
        sp_ = st.sb("softplus", [P, 2, S])
        pr = st.sb("weights", [P, 2, S])
        prT = st.sb("weightsT", [P, 2, S])
        mx = st.sb("max", [P, U])
        nm = st.sb("minus_max", [P, U])
        den = st.sb("den", [P, U])
        low = st.sb("low", [P, 2, U])
        sc_full = st.sem("scores_ready")
        first = st.sem("logits_ready")
        mid = st.sem("between_ready")
        second = st.sem("second_ready")
        w_ready = st.sem("weights_ready")
        t_full = st.sem("turned")
        wt_ready = st.sem("turned_copied")
        o_full = st.sem("sum_ready")
        o_done = st.sem("sum_used")
        chain = st.sem("dve_chain")
        achain = st.sem("act_chain")

        def scores(n):
            u = units[n]
            return ps[:, n % 2, 0:u.hi - u.lo]

        def buf(b, n):
            u = units[n]
            return b[:, n % (3 if b is lg else 2), 0:u.hi - u.lo]

        def wait(eng, sem, value):
            if value > 0:
                eng.wait_ge(sem, value)

        steps = U + 2 + late
        if branches is not None:
            branches.begin()

        with nc.Block() as block:
            if branches is not None:
                @block.sync
                def _(sp):
                    branches.load_on(sp)

            @block.tensor
            def _(pe):
                for n in range(steps):
                    if n < U:
                        u = units[n]
                        wait(pe, first if kind != "mlstm" and u.mask is not None else w_ready, n - 1)
                        qs, ks = query(u.head, u.tile), key(u.head, u.lo, u.hi)
                        pairs = list(zip(qs, ks)) if isinstance(qs, list) else [(qs, ks)]
                        for j, (q, kk) in enumerate(pairs):
                            last = nc.tensor.matmul(scores(n), q, kk, start=j == 0, stop=j == len(pairs) - 1)
                        last.then_inc(sc_full, 1)
                    if branches is not None:
                        branches.pe_steps(pe, branches.share(n - 0.5, steps))
                    m = n - 1 - late
                    if 0 <= m < U:
                        u = units[m]
                        wait(pe, w_ready, m + 1)
                        wait(pe, wt_ready, m - 1)
                        for c in range((u.hi - u.lo) // P):
                            last = nc.tensor.transpose(ps[:, 2 + m % 2, c * P:(c + 1) * P], pr[:, m % 2, c * P:(c + 1) * P],
                                                       ident[:])
                        last.then_inc(t_full, 1)
                    m = n - 2 - late
                    if 0 <= m < U:
                        u = units[m]
                        wait(pe, wt_ready, m + 1)
                        wait(pe, o_done, m - 1)
                        nk = (u.hi - u.lo) // P
                        for c in range(nk):
                            last = nc.tensor.matmul(ps[:, 4 + m % 2, 0:dv], prT[:, m % 2, c * P:(c + 1) * P],
                                                    value(u.head, u.lo // P + c), start=c == 0, stop=c == nk - 1)
                        last.then_inc(o_full, 1)
                    if branches is not None:
                        branches.pe_steps(pe, branches.share(n, steps))

            @block.scalar
            def _(act):
                link = Chain(act, achain)
                if kind == "stick":
                    act.preload_act_table_set("natural_log_exp_and_others")
                for n in range(steps):
                    if branches is not None:
                        branches.act_steps(act, branches.share(n - 1, steps))
                        branches.splits(act, "high", branches.share(n - 1, steps))
                    if n < U:
                        u = units[n]
                        c = u.column
                        wait(act, first, n + 1)
                        if kind in ("softmax", "decayed"):
                            wait(act, t_full, n - 1)
                            src = buf(lg, n) if u.mask is not None else scores(n)
                            sca.activation(buf(pr, n), src, ACT.Exp, bias=nm[:, n:n + 1],
                                           scale=scale if kind == "softmax" else 1.0,
                                           accum_out=den[:, n:n + 1]).then_inc(w_ready, 1)
                        elif kind == "mlstm":
                            wait(act, w_ready, n - 1)
                            sca.activation(buf(tmp, n), buf(lg, n), ACT.Exp, bias=nm[:, n:n + 1])
                            sca.activation(low[:, 1, n:n + 1], low[:, 0, n:n + 1], ACT.Exp).then_inc(mid, 1)
                        else:
                            wait(act, second, n - 1)
                            link(sca.activation(buf(tmp, n), buf(lg, n), ACT.Abs))
                            link(sca.activation(buf(tmp, n), buf(tmp, n), ACT.Exp, scale=-1.0))
                            sca.activation(buf(tmp, n), buf(tmp, n), ACT.Ln, bias=1.0).then_inc(mid, 1)
                    m = n - 1
                    if kind == "stick" and 0 <= m < U:
                        wait(act, second, m + 1)
                        wait(act, t_full, m - 1)
                        sca.activation(buf(pr, m), buf(lg, m), ACT.Exp).then_inc(w_ready, 1)
                    m = n - 1 - late
                    if kind != "stick" and 0 <= m < U:
                        wait(act, t_full, m + 1)
                        wait(act, o_full, m - 1)
                        w_ = units[m].hi - units[m].lo
                        sca.activation(prT[:, m % 2, 0:w_], ps[:, 2 + m % 2, 0:w_], ACT.Identity).then_inc(wt_ready, 1)
                if branches is not None:
                    branches.act_steps(act, branches.share(steps, steps))

            @block.vector
            def _(dve):
                link = Chain(dve, chain)
                for n in range(steps):
                    if branches is not None:
                        branches.dve_steps(dve, branches.share(n - 1, steps))
                        branches.splits(dve, "low", branches.share(n - 1, steps))
                    if n < U:
                        u = units[n]
                        w_ = u.hi - u.lo
                        one = slice(n, n + 1)
                        wait(dve, w_ready, n - 2)
                        if kind == "mlstm":
                            link(vec.tensor_tensor_reduce(buf(lg, n), u.row, u.mask, 1.0, -3e38, ALU.add, ALU.max, mx[:, one]))
                            vec.tensor_scalar(nm[:, one], mx[:, one], -1.0, None, ALU.mult)
                            vec.scalar_tensor_tensor(low[:, 0, one], mx[:, one], -1.0, u.shift, ALU.mult,
                                                     ALU.subtract).then_inc(first, 1)
                        elif kind == "stick":
                            wait(dve, sc_full, n + 1)
                            vec.tensor_tensor(buf(lg, n), scores(n), u.mask, ALU.add).then_inc(first, 1)
                        else:
                            wait(dve, sc_full, n + 1)
                            if kind == "decayed":
                                link(vec.scalar_tensor_tensor(buf(lg, n), scores(n), scale, u.row, ALU.mult, ALU.add))
                                link(vec.tensor_tensor_reduce(buf(lg, n), buf(lg, n), u.mask, 1.0, -3e38, ALU.add, ALU.max,
                                                              mx[:, one]))
                            elif u.mask is not None:
                                link(vec.tensor_tensor_reduce(buf(lg, n), scores(n), u.mask, 1.0, -3e38, ALU.add, ALU.max,
                                                              mx[:, one]))
                            else:
                                link(vec.tensor_reduce(mx[:, one], scores(n), AX_X, ALU.max))
                            vec.tensor_scalar(nm[:, one], mx[:, one], -scale if kind == "softmax" else -1.0, None,
                                              ALU.mult).then_inc(first, 1)
                    m = n - 1
                    if late and 0 <= m < U:
                        wait(dve, mid, m + 1)
                        if kind == "mlstm":
                            wait(dve, sc_full, m + 1)
                            wait(dve, t_full, m - 1)
                            vec.scalar_tensor_tensor(buf(pr, m), scores(m), scale, buf(tmp, m), ALU.mult, ALU.mult,
                                                     accum_out=den[:, m:m + 1]).then_inc(w_ready, 1)
                        else:
                            link(vec.scalar_tensor_tensor(buf(sp_, m), buf(lg, m), 0.0, buf(tmp, m), ALU.max, ALU.add))
                            w_ = units[m].hi
                            s = sp_[:, m % 2, 0:w_]
                            link(vec.tensor_tensor_scan(s[:, ::-1], s[:, ::-1], s[:, ::-1], 0.0, ALU.add, ALU.bypass))
                            vec.tensor_tensor(buf(lg, m), buf(lg, m), s, ALU.subtract).then_inc(second, 1)
                    m = n - 1 - late
                    if kind == "stick" and 0 <= m < U:
                        wait(dve, t_full, m + 1)
                        wait(dve, o_full, m - 1)
                        w_ = units[m].hi
                        vec.tensor_copy(prT[:, m % 2, 0:w_], ps[:, 2 + m % 2, 0:w_]).then_inc(wt_ready, 1)
                    m = n - 2 - late
                    if 0 <= m < U:
                        u = units[m]
                        one = slice(m, m + 1)
                        o = ps[:, 4 + m % 2, 0:dv]
                        wait(dve, o_full, m + 1)
                        if kind == "mlstm":
                            link(vec.scalar_tensor_tensor(mx[:, one], den[:, one], -1.0, den[:, one], ALU.mult, ALU.max))
                            link(vec.tensor_tensor(den[:, one], mx[:, one], low[:, 1, one], ALU.max))
                        dst = out(u.head, u.tile)
                        if kind != "stick":
                            link(vec.reciprocal(mx[:, one], den[:, one]))
                        if kind == "stick":
                            vec.tensor_copy(dst, o).then_inc(o_done, 1)
                        elif u.add:
                            wait(dve, o_done, m)
                            vec.scalar_tensor_tensor(dst, o, mx[:, one], dst, ALU.mult, ALU.add).then_inc(o_done, 1)
                        else:
                            vec.tensor_scalar(dst, o, mx[:, one], None, ALU.mult).then_inc(o_done, 1)
                if branches is not None:
                    branches.dve_steps(dve, branches.share(steps, steps))


def constants(nc, st, ps):
    k = {"ps": ps}
    for n, shape, dt in (("ident", [P, P], F32), ("ones", [P, P], F32), ("before", [P, P], F32), ("upto", [P, P], F32),
                         ("after", [P, P], F32), ("mask_le", [P, 2 * S - P], F32), ("mask_lt", [P, 2 * S - P], F32),
                         ("mask_ge", [P, 2 * S - P], F32),
                         ("iota_e", [P, NE], F32), ("group_of", [P, NE], F32), ("choice", [P, 2, TT], F32), ("second", [P, 1], F32)):
        k[n] = st.sb(n, shape, dt)
    made = st.sem("const_made")
    with nc.Block() as block:
        @block.gpsimd
        def _(pool):
            g = nc.gpsimd
            for n in ("ones", "before", "upto", "after"):
                g.memset(k[n][:], 1.0)
            for n in ("ident", "mask_le", "mask_lt", "mask_ge", "second"):
                g.memset(k[n][:], 0.0)
            g.iota(k["iota_e"][:], [[1, NE]], 0, 0, allow_small_or_imprecise_dtypes=True)
            g.iota(k["group_of"][:].rearrange("p (g e) -> p g e", g=NG), [[1, NG], [0, EPG]], 0, 0,
                   allow_small_or_imprecise_dtypes=True)
            g.iota(k["choice"][:], [[S, 2], [P, TT]], 0, 1, allow_small_or_imprecise_dtypes=True).then_inc(made, 1)
            pool.wait_ge(made, 1)
            g.affine_select(k["second"][:], k["second"][:], [[0, 1]], ALU.is_ge, 1.0, SLOTS - 1, -1)
            g.affine_select(k["ident"][:], k["ident"][:], [[-1, P]], ALU.not_equal, 1.0, 0, 1)
            g.affine_select(k["before"][:], k["before"][:], [[1, P]], ALU.is_gt, 0.0, 0, -1)
            g.affine_select(k["upto"][:], k["upto"][:], [[1, P]], ALU.is_ge, 0.0, 0, -1)
            g.affine_select(k["after"][:], k["after"][:], [[-1, P]], ALU.is_ge, 0.0, 0, 1)
            n, off = 2 * S - P, S - P
            g.affine_select(k["mask_le"][:], k["mask_le"][:], [[-1, n]], ALU.is_ge, -BIG, off, 1)
            g.affine_select(k["mask_lt"][:], k["mask_lt"][:], [[-1, n]], ALU.is_gt, -BIG, off, 1)
            g.affine_select(k["mask_ge"][:], k["mask_ge"][:], [[1, n]], ALU.is_ge, -BIG, -off, -1).then_inc(made, 1)
    return k


def moe(nc, name, k, x, hT, h_rows, gain, w_rg, b_rg, w_re, b_re, w_gate, w_up, w_down, alpha=1.0):
    FF = w_gate.shape[2]
    NF = FF // P
    OWN = 2 if FF == 512 else 5
    RING = OWN + 1
    TURNS, TAIL = NE // RING, NE % RING
    EARLY = 5 * 512 // FF
    DEPTH = 2
    HALF = FF // 2
    HF = HALF // P
    ident, ps = k["ident"], k["ps"]
    rows_dram = nc.dram_tensor(f"{name}_dram_rows", [S, D], F32).ap()
    y_dram = nc.dram_tensor(f"{name}_dram_y", [4 * S, D // 2], F32).ap()
    spare_dram = nc.dram_tensor(f"{name}_dram_spare", [1, SLOTS], F32).ap()
    token_dram = nc.dram_tensor(f"{name}_dram_token", [ROWS, 1], F32).ap()

    with Stage(nc, name) as st:
        wg_own = st.sb("wg", [P, OWN, DC, FF])
        wu_own = st.sb("wu", [P, OWN, DC, FF])
        wd_all = st.sb("wd", [P, RING, NF, D])
        if FF == 512:
            borrowed = [h_rows.rearrange("p t (c f) -> p (t c) f", f=FF), hT[:]]
        else:
            half = DC // 2
            borrowed = [hT[:, n * half:(n + 1) * half].rearrange("p c (q f) -> p (c q) f", f=FF) for n in range(2)]
        wg = [wg_own[:, s] for s in range(OWN)] + borrowed[0:1]
        wu = [wu_own[:, s] for s in range(OWN)] + borrowed[1:2]
        wd = [wd_all[:, s] for s in range(RING)]
        router = st.sb("router", [P, DC, NG + NE])
        bias = st.sb("bias", [P, NG + NE])
        logitsT = st.sb("logitsT", [NG + NE, S])
        logits = st.sb("logits", [P, TT, NG + NE])
        gpad = st.sb("gpad", [P, TT, 8])
        gmax = st.sb("gmax", [P, TT, 8])
        gidx = st.sb("gidx", [P, TT, 8], U32)
        gidxf = st.sb("gidxf", [P, TT, 1])
        gmask = st.sb("gmask", [P, TT, NE])
        away = st.sb("away", [P, TT, NE])
        masked = st.sb("masked", [P, TT, NE])
        emax = st.sb("emax", [P, TT, 8])
        eidx = st.sb("eidx", [P, TT, 8], U32)
        eidxf = st.sb("eidxf", [P, TT, 2])
        hot = st.sb("hot", [P, 2, TT, NE])
        both = st.sb("both", [P, TT, NE])
        diff = st.sb("diff", [P, 5 * TT])
        expd = st.sb("expd", [P, 5 * TT])
        gsum = st.sb("gsum", [P, TT])
        weight = st.sb("weight", [P, 2, TT])
        nblk = st.sb("nblk", [P, 8, NE])
        ends = st.sb("ends", [P, 3, NE])
        slot = st.sb("slot", [P, TT, NE])
        picked = st.sb("picked", [P, 2, TT, NE])
        slotf = st.sb("slotf", [P, 2, TT])
        sloti = st.sb("sloti", [P, 2, TT], U32)
        table = st.sb("table", [1, 2, NE], I32)
        zero = st.sb("zero", [TABLE, SLOTS])
        tokrow = st.sb("tokrow", [TABLE, 2, SLOTS])
        part = st.sb("part", [P, 3, TABLE])
        tokcol = st.sb("tokcol", [SLOTS, TABLE], U32)
        choicecol = st.sb("choicecol", [P, TABLE], U32)
        choicecur = st.sb("choicecur", [P, 1], U32)
        tokcur = st.sb("tokcur", [SLOTS, 1], U32)
        gathered = st.sb("gathered", [SLOTS, D])
        xT = st.sb("xT", [P, DC, SLOTS])
        silu = st.sb("silu", [P, 2, HALF])
        hid = st.sb("hid", [P, 2, HALF])
        hidT = st.sb("hidT", [P, NF, SLOTS])
        y = st.sb("y", [P, D // 2])
        aside = st.sb("aside", [1, 1])

        w_sem = [[st.sem(f"{m}_landed{s}") for m in ("gate", "up", "down")] for s in range(RING)]
        router_landed = st.sem("router_landed")
        rows_stored = st.sem("rows_stored")
        zero_ready = st.sem("zero_ready")
        zero_stored = st.sem("zero_stored")
        logits_ready = st.sem("logits_ready")
        logitsT_ready = st.sem("logitsT_ready")
        logitsT_copied = st.sem("logitsT_copied")
        chain = st.sem("dve_chain")
        diff_ready = st.sem("diff_ready")
        exp_ready = st.sem("exp_ready")
        hot_ready = st.sem("hot_ready")
        rank_ready = st.sem("rank_ready")
        table_ready = st.sem("table_ready")
        token_scattered = st.sem("token_scattered")
        tokrow_landed = st.sem("tokrow_landed")
        tokT_ready = st.sem("tokT_ready")
        tokcol_ready = st.sem("tokcol_ready")
        tokcur_ready = st.sem("tokcur_ready")
        choicecur_ready = st.sem("choicecur_ready")
        rows_gathered = st.sem("rows_gathered")
        turned = st.sem("turned")
        xT_ready = st.sem("xT_ready")
        gu_ready = st.sem("gate_up_ready")
        silu_ready = st.sem("silu_ready")
        hid_ready = st.sem("hid_ready")
        hid_turned = st.sem("hid_turned")
        hidT_ready = st.sem("hidT_ready")
        y_ready = st.sem("y_ready")
        y_copied = st.sem("y_copied")
        y_stored = st.sem("y_stored")
        back_landed = [st.sem(f"back_landed{n}") for n in range(2 * TT)]
        back_used = st.sem("back_used")

        wg_dram = w_gate.rearrange("e (c p) f -> e p c f", p=P)
        wu_dram = w_up.rearrange("e (c p) f -> e p c f", p=P)
        wd_dram = w_down.rearrange("e (c p) d -> e p c d", p=P)
        ps_turn = ps[:, 0, :]
        ps_gu = [ps[:, 1 + q, 0:HALF] for q in range(2)]
        ps_hid = [ps[:, 3 + q, 0:HF * SLOTS] for q in range(2)]
        ps_y = ps[:, 5, :]
        ps_tok = ps[:, 6, 0:TABLE]

        def back(j):
            n = 512 // FF
            return wg_own[:, j * n:(j + 1) * n].rearrange("p r c f -> p (r c f)").rearrange("p (t d) -> p t d", t=TT)

        def blocks_of(eng, e):
            return eng.value_load(table[0:1, 0, bass.ds(e, 1)], min_val=1, max_val=S // SLOTS)

        with nc.Block() as block:
            @block.sync
            def _(sp):
                def load(e, s, m):
                    w, dram = ((wg, wg_dram), (wu, wu_dram), (wd, wd_dram))[m]
                    sp.dma_start(w[s], dram[bass.ds(e, 1)].rearrange("e p c f -> p (e c) f")).then_inc(w_sem[s][m], 16)

                sp.dma_start(router[:, :, 0:NG], w_rg.rearrange("(c p) n -> p c n", p=P)).then_inc(router_landed, 16)
                sp.dma_start(router[:, :, NG:], w_re.rearrange("(c p) n -> p c n", p=P)).then_inc(router_landed, 16)
                sp.dma_start(bias[:, 0:NG], b_rg.partition_broadcast(P)).then_inc(router_landed, 16)
                sp.dma_start(bias[:, NG:], b_re.partition_broadcast(P)).then_inc(router_landed, 16)
                sp.wait_ge(zero_ready, 1)
                sp.dma_start(token_dram.rearrange("(b s) one -> b (s one)", s=SLOTS), zero[:]).then_inc(zero_stored, 16)
                sp.dma_start(rows_dram.rearrange("(t p) d -> p t d", p=P), h_rows).then_inc(rows_stored, 16)
                first = [(s, m) for s in range(RING) for m in range(3)]
                for s, m in first[:EARLY]:
                    load(s, s, m)
                sp.wait_ge(token_scattered, 16 * 2 * TT)
                for q in range(2):
                    sp.dma_start(tokrow[:, q], token_dram.rearrange("(b s) one -> b (s one)", s=SLOTS)).then_inc(tokrow_landed, 16)
                for n in range(EARLY, len(first)):
                    done_s, done_m = first[n - DEPTH]
                    sp.wait_ge(w_sem[done_s][done_m], 16)
                    if n == 3 * OWN:
                        sp.wait_ge(logitsT_ready, 1)
                        sp.wait_ge(rows_stored, 16)
                    load(first[n][0], *first[n])
                sp.wait_ge(table_ready, 2)

                def refill(turn_, s):
                    e = turn_ * RING + s
                    end = sp.value_load(table[0:1, 1, bass.ds(e, 1)], min_val=1, max_val=MAX_BLOCKS)
                    prev, landed = (s - 1) % RING, (turn_ + (1 if s == 0 else 2)) * 16
                    sp.wait_ge(gu_ready, end * 2)
                    sp.wait_ge(w_sem[prev][1], landed)
                    load(e + RING, s, 0)
                    sp.wait_ge(w_sem[prev][2], landed)
                    load(e + RING, s, 1)
                    sp.wait_ge(y_ready, end)
                    sp.wait_ge(w_sem[s][0], (turn_ + 2) * 16)
                    load(e + RING, s, 2)

                with sp.Fori(0, TURNS - 1) as turn_:
                    for s in range(RING):
                        refill(turn_, s)
                for s in range(TAIL):
                    refill(TURNS - 1, s)
                total = sp.value_load(table[0:1, 1, NE - 1:NE], min_val=1, max_val=MAX_BLOCKS)
                sp.wait_ge(y_stored, total * 16 + 16)
                for j in range(2):
                    for t in range(TT):
                        a = 2 * S * j + 2 * P * t
                        sp.dma_start(back(j)[:, t, :], y_dram[a:a + 2 * P].rearrange("(p h) d -> p (h d)", p=P)
                                     ).then_inc(back_landed[j * TT + t], 16)

            @block.tensor
            def _(pe):
                pe.wait_ge(router_landed, 64)
                for c in range(DC):
                    last = nc.tensor.matmul(ps[0:NG + NE, 6, :], router[:, c, :], hT[:, c, :], start=c == 0, stop=c == DC - 1)
                last.then_inc(logitsT_ready, 1)
                pe.wait_ge(logitsT_copied, 1)
                for t in range(TT):
                    last = nc.tensor.transpose(ps[:, t, 0:NG + NE], logitsT[:, t * P:(t + 1) * P], ident[0:NG + NE, 0:NG + NE])
                last.then_inc(logits_ready, 1)
                pe.wait_ge(hot_ready, 1)
                rank = ps[:, 4, :].rearrange("p (t e) -> p t e", e=NE)
                nc.tensor.matmul(rank[:, 0:TT, :], k["before"][:], both[:], start=True, stop=False)
                for u in range(1, TT):
                    nc.tensor.matmul(rank[:, u:TT, :], k["ones"][:], both[:, 0:TT - u, :], start=False, stop=u == TT - 1)
                for t in range(TT):
                    last = nc.tensor.matmul(ps[:, 5, 0:NE], k["ones"][:], both[:, t, :], start=t == 0, stop=t == TT - 1)
                last.then_inc(rank_ready, 1)
                pe.wait_ge(tokrow_landed, 32)
                nb = TABLE
                nc.tensor.transpose(ps_tok, tokrow[:].rearrange("b q s -> b (q s)"), ident[0:nb, 0:nb]).then_inc(tokT_ready, 1)
                pe.wait_ge(table_ready, 2)

                def turn():
                    nc.tensor.matmul(ps_turn[:, 0:SLOTS], gathered[:, 0:P], ident[0:SLOTS, 0:SLOTS], start=True, stop=True)
                    for c in range(1, DC):
                        last = nc.tensor.transpose(ps_turn[:, c * SLOTS:(c + 1) * SLOTS], gathered[:, c * P:(c + 1) * P],
                                                   ident[0:SLOTS, 0:SLOTS])
                    last.then_inc(turned, 1)

                pe.wait_ge(rows_gathered, 16)
                turn()
                done = pe.alloc_register(f"{name}_done")
                pe.reg_mov(done, 0)

                def expert(turn_, s):
                    for m in range(3):
                        pe.wait_ge(w_sem[s][m], (turn_ + 1) * 16)
                    with pe.Fori(0, blocks_of(pe, turn_ * RING + s)):
                        g = pe.snap(done)
                        pe.wait_ge(xT_ready, g + 1)
                        for q in range(2):
                            span = slice(q * HALF, (q + 1) * HALF)
                            for c in range(DC):
                                nc.tensor.matmul(ps_gu[q][0:SLOTS], xT[:, c, :], wg[s][:, c, span],
                                                 start=c == 0, stop=c == DC - 1)
                                last = nc.tensor.matmul(ps_gu[q][SLOTS:P], xT[:, c, :], wu[s][:, c, span],
                                                        start=c == 0, stop=c == DC - 1)
                            last.then_inc(gu_ready, 1)
                        pe.wait_ge(rows_gathered, (g + 2) * 16)
                        turn()
                        for q in range(2):
                            pe.wait_ge(hid_ready, g * 2 + (q + 1))
                            for f in range(HF):
                                last = nc.tensor.matmul(ps_hid[q][:, f * SLOTS:(f + 1) * SLOTS],
                                                        hid[SLOTS:P, q, f * P:(f + 1) * P], ident[SLOTS:P, SLOTS:P],
                                                        start=True, stop=True)
                            last.then_inc(hid_turned, 1)
                        pe.wait_ge(y_copied, g + 1)
                        for f in range(NF):
                            if f % HF == 0:
                                pe.wait_ge(hidT_ready, g * 2 + (f // HF + 1))
                            for h in range(2):
                                last = nc.tensor.matmul(ps_y[h * SLOTS:(h + 1) * SLOTS], hidT[:, f, :],
                                                        wd[s][:, f, h * 512:(h + 1) * 512],
                                                        start=f == 0, stop=f == NF - 1)
                        last.then_inc(y_ready, 1)
                        pe.reg_add(done, done, 1)

                with pe.Fori(0, TURNS) as turn_:
                    for s in range(RING):
                        expert(turn_, s)
                for s in range(TAIL):
                    expert(TURNS, s)

            @block.scalar
            def _(act):
                act.sem_inc(y_copied, 1)
                act.wait_ge(logitsT_ready, 1)
                nc.scalar.copy(logitsT[:], ps[0:NG + NE, 6, :]).then_inc(logitsT_copied, 1)
                act.wait_ge(diff_ready, 1)
                nc.scalar.activation(expd[:], diff[:], ACT.Exp).then_inc(exp_ready, 1)
                act.wait_ge(table_ready, 2)
                done = act.alloc_register(f"{name}_done")
                act.reg_mov(done, 0)
                with act.Fori(0, NE) as e:
                    with act.Fori(0, blocks_of(act, e)):
                        g = act.snap(done)
                        for q in range(2):
                            act.wait_ge(gu_ready, g * 2 + (q + 1))
                            nc.scalar.activation(silu[SLOTS:P, q], ps_gu[q][0:SLOTS], ACT.Silu).then_inc(silu_ready, 1)
                        for q in range(2):
                            act.wait_ge(hid_turned, g * 2 + (q + 1))
                            nc.scalar.copy(hidT[:, q * HF:(q + 1) * HF].rearrange("p f s -> p (f s)"), ps_hid[q]
                                           ).then_inc(hidT_ready, 1)
                        act.wait_ge(y_ready, g + 1)
                        act.wait_ge(y_stored, (g + 1) * 16)
                        nc.scalar.copy(y[:], ps_y).then_inc(y_copied, 1)
                        act.reg_add(done, done, 1)

            @block.vector
            def _(dve):
                link = Chain(dve, chain)
                vec = nc.vector
                vec.memset(zero[:], float(2 * S)).then_inc(zero_ready, 1)
                link(vec.memset(gpad[:], -BIG * 1e8))
                dve.wait_ge(router_landed, 64)
                dve.wait_ge(logits_ready, 1)
                link(vec.tensor_tensor(logits[:], ps[:, 0:TT, 0:NG + NE],
                                       bias[:].unsqueeze(1).to_broadcast([P, TT, NG + NE]), ALU.add))
                link(vec.tensor_copy(gpad[:, :, 0:NG], logits[:, :, 0:NG]))
                for t in range(TT):
                    link(vec.max(gmax[:, t, :], gpad[:, t, :]))
                    link(vec.max_index(gidx[:, t, :], gmax[:, t, :], gpad[:, t, :]))
                link(vec.tensor_copy(gidxf[:], gidx[:, :, 0:1]))
                link(vec.tensor_tensor(gmask[:], k["group_of"][:].unsqueeze(1).to_broadcast([P, TT, NE]),
                                       gidxf[:].to_broadcast([P, TT, NE]), ALU.is_equal))
                link(vec.tensor_scalar(away[:], gmask[:], -1.0, BIG, ALU.add, ALU.mult))
                link(vec.tensor_tensor(masked[:], logits[:, :, NG:], gmask[:], ALU.mult))
                link(vec.tensor_tensor(masked[:], masked[:], away[:], ALU.add))
                for t in range(TT):
                    link(vec.max(emax[:, t, :], masked[:, t, :]))
                    link(vec.max_index(eidx[:, t, :], emax[:, t, :], masked[:, t, :]))
                link(vec.tensor_copy(eidxf[:], eidx[:, :, 0:2]))
                for j in range(2):
                    link(vec.tensor_tensor(hot[:, j], k["iota_e"][:].unsqueeze(1).to_broadcast([P, TT, NE]),
                                           eidxf[:, :, j:j + 1].to_broadcast([P, TT, NE]), ALU.is_equal))
                vec.tensor_tensor(both[:], hot[:, 0], hot[:, 1], ALU.add).then_inc(hot_ready, 1)
                vec.tensor_tensor(diff[:, 0:TT * NG].rearrange("p (t g) -> p t g", t=TT), logits[:, :, 0:NG],
                                  gmax[:, :, 0:1].to_broadcast([P, TT, NG]), ALU.subtract)
                link(vec.tensor_tensor(diff[:, TT * NG:], emax[:, :, 1], emax[:, :, 0], ALU.subtract))
                vec.tensor_copy(gpad[:, 0, 0:1], diff[:, 0:1]).then_inc(diff_ready, 1)
                dve.wait_ge(exp_ready, 1)
                link(vec.tensor_reduce(gsum[:], expd[:, 0:TT * NG].rearrange("p (t g) -> p t g", t=TT), AX_X, ALU.add))
                link(vec.scalar_tensor_tensor(gsum[:], expd[:, TT * NG:], 1.0, gsum[:], ALU.add, ALU.mult))
                link(vec.reciprocal(weight[:, 0], gsum[:]))
                link(vec.tensor_tensor(weight[:, 1], weight[:, 0], expd[:, TT * NG:], ALU.mult))
                dve.wait_ge(rank_ready, 1)
                counts = ps[:, 5, 0:NE]
                link(vec.tensor_scalar(nblk[:, 0], counts, float(SLOTS), 1.0, ALU.is_gt, ALU.add))
                for j in range(2, S // SLOTS):
                    link(vec.scalar_tensor_tensor(nblk[:, j - 1], counts, float(SLOTS * j), nblk[:, j - 2], ALU.is_gt, ALU.add))
                blocks = nblk[:, S // SLOTS - 2]
                link(vec.tensor_tensor_scan(ends[:, 0], blocks, blocks, 0.0, ALU.add, ALU.bypass))
                vec.tensor_copy(table[0:1, 0], blocks[0:1]).then_inc(table_ready, 1)
                vec.tensor_copy(table[0:1, 1], ends[0:1, 0]).then_inc(table_ready, 1)
                link(vec.tensor_tensor(ends[:, 1], ends[:, 0], blocks, ALU.subtract))
                link(vec.tensor_scalar(ends[:, 2], ends[:, 1], float(SLOTS), None, ALU.mult))
                link(vec.tensor_tensor(slot[:], ps[:, 4, 0:TT * NE].rearrange("p (t e) -> p t e", e=NE),
                                       ends[:, 2:3].to_broadcast([P, TT, NE]), ALU.add))
                for j in range(2):
                    link(vec.tensor_tensor(picked[:, j], slot[:], hot[:, j], ALU.mult))
                for j in range(2):
                    link(vec.tensor_reduce(slotf[:, j], picked[:, j], AX_X, ALU.add))
                vec.tensor_copy(sloti[:], slotf[:]).then_inc(table_ready, 1)
                dve.wait_ge(tokT_ready, 1)
                link(vec.tensor_scalar(part[:, 0], ps_tok, 1.0, None, ALU.mult))
                link(vec.tensor_scalar(part[:, 1], part[:, 0], float(S), float(-S), ALU.is_ge, ALU.mult))
                link(vec.tensor_tensor(part[:, 2], part[:, 0], part[:, 1], ALU.add))
                vec.tensor_scalar(choicecol[:], part[:, 0], 2.0, k["second"][:], ALU.mult, ALU.add).then_inc(tokcol_ready, 1)
                vec.tensor_scalar(tokcol[:], part[0:SLOTS, 2], float(S - 1), None, ALU.min).then_inc(tokcol_ready, 1)

                def turn_copy(n):
                    dve.wait_ge(turned, n)
                    view = ps_turn.rearrange("p (c s) -> p c s", c=DC)
                    if gain is None:
                        vec.tensor_copy(xT[:], view).then_inc(xT_ready, 1)
                    else:
                        vec.tensor_tensor(xT[:], view, cols(gain, SLOTS), ALU.mult).then_inc(xT_ready, 1)

                turn_copy(1)
                done = dve.alloc_register(f"{name}_done")
                dve.reg_mov(done, 0)
                with dve.Fori(0, NE) as e:
                    with dve.Fori(0, blocks_of(dve, e)):
                        g = dve.snap(done)
                        for q in range(2):
                            dve.wait_ge(silu_ready, g * 2 + (q + 1))
                            vec.tensor_tensor(hid[SLOTS:P, q], silu[SLOTS:P, q], ps_gu[q][SLOTS:P], ALU.mult).then_inc(hid_ready, 1)
                        turn_copy(g + 2)
                        dve.reg_add(done, done, 1)
                dve.wait_ge(rows_stored, 16)
                if alpha != 1.0:
                    link(vec.tensor_scalar(x[:], x[:], alpha, None, ALU.mult))
                for j in range(2):
                    for t in range(TT):
                        dve.wait_ge(back_landed[j * TT + t], 16)
                        if j:
                            dve.wait_ge(back_used, t + 1)
                        vec.scalar_tensor_tensor(x[:, t, :], back(j)[:, t, :], weight[:, j, t:t + 1], x[:, t, :],
                                                 ALU.mult, ALU.add).then_inc(back_used, 1)

            @block.gpsimd
            def _(pool):
                def step_aside():
                    nc.gpsimd.tensor_tensor(aside[:], ident[0:1, 0:1], ident[0:1, 0:1], ALU.mult)

                pool.wait_ge(zero_stored, 16)
                pool.wait_ge(rows_stored, 16)
                pool.wait_ge(table_ready, 3)
                for t in range(TT):
                    for j in range(2):
                        nc.gpsimd.indirect_dma_start(token_dram, bass.IndirectOffsetOnAxis(sloti[:, j, t:t + 1], 0),
                                                     k["choice"][:, j, t:t + 1], None).then_inc(token_scattered, 16)
                pool.wait_ge(tokcol_ready, 2)

                def gather(n):
                    nc.gpsimd.tensor_copy(tokcur[:], tokcol[:, bass.ds(n, 1)]).then_inc(tokcur_ready, 1)
                    pool.wait_ge(tokcur_ready, n + 1)
                    step_aside()
                    nc.gpsimd.indirect_dma_start(gathered[:], None, rows_dram,
                                                 bass.IndirectOffsetOnAxis(tokcur[:], 0)).then_inc(rows_gathered, 16)

                nc.gpsimd.dma_start(spare_dram, ident[0:1, 0:SLOTS]).then_inc(y_stored, 16)
                gather(0)
                pool.wait_ge(turned, 1)
                gather(1)
                done = pool.alloc_register(f"{name}_done")
                pool.reg_mov(done, 0)
                with pool.Fori(0, NE) as e:
                    with pool.Fori(0, blocks_of(pool, e)):
                        g = pool.snap(done)
                        pool.wait_ge(turned, g + 2)
                        gather(g + 2)
                        pool.wait_ge(y_copied, g + 2)
                        nc.gpsimd.tensor_copy(choicecur[:], choicecol[:, bass.ds(g, 1)]).then_inc(choicecur_ready, 1)
                        pool.wait_ge(choicecur_ready, g + 1)
                        step_aside()
                        nc.gpsimd.indirect_dma_start(y_dram, bass.IndirectOffsetOnAxis(choicecur[:], 0), y[:], None,
                                                     bounds_check=4 * S - 1, oob_is_err=False).then_inc(y_stored, 16)
                        pool.reg_add(done, done, 1)


class Columns:

    def __init__(self, sizes):
        self.at, n = {}, 0
        for name, width in sizes:
            self.at[name] = (n, n + width)
            n += width
        self.width = n


COLS = Columns([("g_mix", 8), ("g_xattn", 8), ("g_mem", 8), ("g_moe", 8), ("conv_w", 40), ("conv_b", 8), ("b_s", 4)]
               + [(f"{n}{l}", w) for l in range(2) for n, w in (("b_gate", 32), ("q_norm", 2), ("kv_norm", 1), ("conv_w2", 62),
                                                               ("conv_b2", 2), ("ln_g2", 2), ("ln_b2", 2))])
ROWS_ = Columns([("gate_b", 16), ("g_head", 512), ("ln_v_g", 512), ("ln_v_b", 512), ("g_final", 1024), ("inv_freq", 16)]
                + [(f"{n}{l}", w) for l in range(2) for n, w in (("b_forget", 4), ("ln1_g", 1024), ("ln1_b", 1024),
                                                                ("ln2_g", 1024), ("ln2_b", 1024))])


def load(nc, name, pairs):
    with Stage(nc, name) as st:
        landed = st.sem("landed")
        with nc.Block() as block:
            @block.sync
            def _(sp):
                for dst, src in pairs:
                    sp.dma_start(dst, src).then_inc(landed, 16)
                sp.wait_ge(landed, 16 * len(pairs))


def running_log_sigmoid(nc, name, k, f, nf, after_from, b):
    ps = k["ps"]
    with Stage(nc, name) as st:
        a = st.sb("abs", [P, TT, nf])
        e = st.sb("exp", [P, TT, nf])
        l1 = st.sb("ln", [P, TT, nf])
        ls = st.sb("ls", [P, TT, nf])
        forward = ps[:, 0, 0:TT * after_from].rearrange("p (t j) -> p t j", t=TT)
        backward = ps[:, 1, 0:TT * max(nf - after_from, 1)].rearrange("p (t j) -> p t j", t=TT)
        achain, ln_ready, ls_ready, summed = (st.sem(n) for n in ("act_chain", "ln_ready", "ls_ready", "summed"))
        with nc.Block() as block:
            @block.scalar
            def _(act):
                link = Chain(act, achain)
                act.preload_act_table_set("natural_log_exp_and_others")
                link(nc.scalar.activation(a[:], f, ACT.Abs))
                link(nc.scalar.activation(e[:], a[:], ACT.Exp, scale=-1.0))
                nc.scalar.activation(l1[:], e[:], ACT.Ln, bias=1.0).then_inc(ln_ready, 1)

            @block.vector
            def _(dve):
                dve.wait_ge(ln_ready, 1)
                nc.vector.scalar_tensor_tensor(ls[:], f, 0.0, l1[:], ALU.min, ALU.subtract).then_inc(ls_ready, 1)
                dve.wait_ge(summed, 1)
                nc.vector.tensor_copy(b[:, :, 0:after_from], forward)
                if after_from < nf:
                    nc.vector.tensor_copy(b[:, :, after_from:nf], backward)

            @block.tensor
            def _(pe):
                pe.wait_ge(ls_ready, 1)
                nc.tensor.matmul(forward, k["upto"][:], ls[:, :, 0:after_from], start=True, stop=False)
                for u in range(1, TT):
                    last = nc.tensor.matmul(forward[:, u:TT], k["ones"][:], ls[:, 0:TT - u, 0:after_from],
                                            start=False, stop=u == TT - 1)
                if after_from < nf:
                    nc.tensor.matmul(backward, k["after"][:], ls[:, :, after_from:nf], start=True, stop=False)
                    for u in range(1, TT):
                        last = nc.tensor.matmul(backward[:, 0:TT - u], k["ones"][:], ls[:, u:TT, after_from:nf],
                                                start=False, stop=u == TT - 1)
                last.then_inc(summed, 1)


def spread_rows(nc, name, k, r, n, rows):
    ps = k["ps"]
    with Stage(nc, name) as st:
        full = st.sem("bank_full")
        emptied = [st.sem("emptied_by_act"), st.sem("emptied_by_dve")]
        with nc.Block() as block:
            @block.tensor
            def _(pe):
                for j in range(n):
                    for t in range(TT):
                        last = nc.tensor.matmul(ps[:, j, t * P:(t + 1) * P], r[:, t, j:j + 1].to_broadcast([P, P]),
                                                k["ident"][:], start=True, stop=True)
                    last.then_inc(full, 1)

            @block.scalar
            def _(act):
                for j in range(0, n, 2):
                    act.wait_ge(full, j + 1)
                    nc.scalar.activation(rows[:, j, :], ps[:, j, :], ACT.Identity)

            @block.vector
            def _(dve):
                for j in range(1, n, 2):
                    dve.wait_ge(full, j + 1)
                    nc.vector.tensor_copy(rows[:, j, :], ps[:, j, :])


def mixer_one(nc, k, x, col, i):
    ps, vec, sca = k["ps"], nc.vector, nc.scalar
    H, DH = 4, P
    with Stage(nc, "mix") as sx:
        hT = sx.sb("hT", [P, 2, DC, S], F32R)
        o = sx.sb("o", [P, TT, 512])
        gu = sx.sb("gu", [P, TT, 512])
        gv = sx.sb("gv", [P, TT, 512])
        y = sx.sb("y", [P, TT, D])
        with Stage(nc, "mixa") as sa:
            raw = sa.sb("raw", [P, 8, S + 4])
            qk = sa.sb("qk", [P, 8, S])
            v = sa.sb("v", [P, TT, 512])
            gates = sa.sb("gates", [P, TT, 16])
            rms_rows(nc, "mixn", [(lambda t: x[:, t, :], lambda t: y[:, t, :], TT, D)], 1e-6, k["mixer_loads"])
            w = i["w_in"][0]
            spans = [(a, a + WIDTH) for a in range(0, 1536, WIDTH)] + [(1536, 1800), (1800, 2064)]
            spans += [(a, a + WIDTH) for a in range(2064, 3088, WIDTH)]
            chunks = [chunk_of(w, a, b) for a, b in spans]
            items = []
            func = lambda out, f: lambda eng, src: eng.activation(out, src, f)
            for c in range(4):
                for j in range(2):
                    items.append(by_feature(c, hT, j * P, "act" if j % 2 else "dve", plain(nc, raw[:, 2 * c + j, 2:2 + S])))
            for c in range(2):
                cs = slice(c * WIDTH, (c + 1) * WIDTH)
                for t in range(TT):
                    items.append(by_token(4 + c, hT, t, 0, WIDTH, "dve", plain(nc, v[:, t, cs])))
            def output_gates(t, a):
                def out(eng, src):
                    if a:
                        eng.copy(gates[:, t, :], src[:, 248:264])
                    return eng.activation(o[:, t, a:min(a + 264, 512)], src[:, 0:min(264, 512 - a)], ACT.Sigmoid)
                return out

            for c in range(2):
                for t in range(TT):
                    items.append(by_token(6 + c, hT, t, 0, 264, "act", output_gates(t, 264 * c)))
            for c in range(4):
                cs = slice(c % 2 * WIDTH, (c % 2 + 1) * WIDTH)
                for t in range(TT):
                    items.append(by_token(8 + c, hT, t, 0, WIDTH, "act", func((gu if c < 2 else gv)[:, t, cs],
                                                                              ACT.Gelu_apprx_tanh)))
            acc = y[:].rearrange("p t (h s) -> p (t h) s", s=S)
            padded, tapped = sa.sem("padded"), sa.sem("tapped")

            def taps(dve, c, emptied):
                if c == 0:
                    vec.memset(raw[:, :, 0:2], 0.0)
                    vec.memset(raw[:, :, 2 + S:], 0.0).then_inc(padded, 1)
                if 1 <= c <= 4:
                    dve.wait_ge(padded, 1)
                    dve.wait_ge(emptied["dve"], c)
                    dve.wait_ge(emptied["act"], c)
                    for j in range(5):
                        for q in (2 * c - 2, 2 * c - 1):
                            wj = col("conv_w")[:, 8 * j + q:8 * j + q + 1]
                            src = raw[:, q, j:j + S]
                            if j == 0:
                                vec.tensor_scalar(acc[:, q, :], src, wj, None, ALU.mult).then_inc(tapped, 1)
                            else:
                                dve.wait_ge(tapped, 10 * (c - 1) + 2 * (j - 1) + q % 2 + 1)
                                vec.scalar_tensor_tensor(acc[:, q, :], src, wj, acc[:, q, :], ALU.mult,
                                                         ALU.add).then_inc(tapped, 1)

            dense(nc, "mixw", k, chunks, items, raw_ring=2, side=taps,
                  before=TurnSplit(nc, k, TT, lambda t, c: y[:, t, c * P:(c + 1) * P], hT, DC, col("g_mix")))
            with nc.Block() as block:
                @block.scalar
                def _(act):
                    for c in range(8):
                        sca.activation(qk[:, c, :], acc[:, c, :], ACT.Silu, bias=col("conv_b")[:, c:c + 1])

                @block.vector
                def _(dve):
                    vec.tensor_tensor(gates[:], gates[:], k["rows"]["gate_b"].unsqueeze(1).to_broadcast([P, TT, 16]), ALU.add)
            hs = raw[:, 0:4, 0:512]
            with Stage(nc, "mixm") as sm:
                f = sm.sb("f", [P, TT, 8])
                b = sm.sb("b", [P, TT, 8])
                r = sm.sb("r", [P, TT, 8])
                rows = sm.sb("rows", [P, 8, S])
                copied = sm.sem("copied")
                with nc.Block() as block:
                    @block.vector
                    def _(dve):
                        g4 = gates[:].rearrange("p t (q h) -> p t q h", h=4)
                        vec.tensor_copy(f[:].rearrange("p t (q h) -> p t q h", h=4), g4[:, :, 1::2, :]).then_inc(copied, 1)
                        dve.wait_ge(copied, 1)
                running_log_sigmoid(nc, "mixs", k, f[:], 8, 4, b[:])
                with nc.Block() as block:
                    @block.vector
                    def _(dve):
                        g4 = gates[:].rearrange("p t (q h) -> p t q h", h=4)
                        vec.tensor_tensor(r[:].rearrange("p t (q h) -> p t q h", h=4), g4[:, :, 0::2, :],
                                          b[:].rearrange("p t (q h) -> p t q h", h=4), ALU.subtract)
                spread_rows(nc, "mixr", k, r, 8, rows)
                units = []
                for h in range(H):
                    for t in range(TT):
                        n = (h * TT + t) * 2
                        hi = (t + 1) * P
                        off = S - P - t * P
                        units.append(Unit(h, t, 0, hi, n, k["mask_le"][:, off:off + hi], rows[:, h, 0:hi], b[:, t, h:h + 1]))
                        lo = t * P
                        units.append(Unit(h, t, lo, S, n + 1, k["mask_ge"][:, S - P:S - P + S - lo], rows[:, 4 + h, lo:],
                                          b[:, t, 4 + h:5 + h], add=True))
                attention(nc, "mixh", k, "mlstm", units, lambda h, t: qk[:, h, t * P:(t + 1) * P],
                          lambda h, lo, hi: qk[:, 4 + h, lo:hi], lambda h, c: v[:, c, h * P:(h + 1) * P],
                          lambda h, t: hs[:, t, h * P:(h + 1) * P], P, DH ** -0.5)
            with Stage(nc, "mixg") as st:
                junk = st.sb("junk", [P, P])
                ss = st.sb("ss", [P, 4, TT, H])
                squared, mean_ready, root_ready, chain, act_chain = (
                    st.sem(n) for n in ("squared", "mean_ready", "root_ready", "dve_chain", "act_chain"))
                with nc.Block() as block:
                    @block.scalar
                    def _(act):
                        link = Chain(act, act_chain)
                        for t in range(TT):
                            for h in range(H):
                                link(sca.activation(junk[:], hs[:, t, h * P:(h + 1) * P], ACT.Square,
                                                    accum_out=ss[:, 0, t, h:h + 1]))
                        act.sem_inc(squared, 1)
                        act.wait_ge(mean_ready, 1)
                        sca.activation(ss[:, 2], ss[:, 1], ACT.Sqrt).then_inc(root_ready, 1)

                    @block.vector
                    def _(dve):
                        link = Chain(dve, chain)
                        for t in range(TT):
                            last = vec.tensor_tensor(o[:, t, :], o[:, t, :], k["rows"]["g_head"], ALU.mult)
                        link(last)
                        dve.wait_ge(squared, 1)
                        vec.tensor_scalar(ss[:, 1], ss[:, 0], 1.0 / P, 1e-6, ALU.mult, ALU.add).then_inc(mean_ready, 1)
                        dve.wait_ge(root_ready, 1)
                        link(vec.reciprocal(ss[:, 3], ss[:, 2]))
                        for t in range(TT):
                            for h in range(H):
                                cs = slice(h * P, (h + 1) * P)
                                vec.scalar_tensor_tensor(y[:, t, cs], hs[:, t, cs], ss[:, 3, t, h:h + 1], o[:, t, cs],
                                                         ALU.mult, ALU.mult)
        ln_rows(nc, "mixl", lambda t: gv[:, t, :], lambda t: gv[:, t, :], TT, 512, 1e-5,
                k["ln_v"])
        with Stage(nc, "mixp") as st:
            full = st.sem("bank_full")
            with nc.Block() as block:
                @block.tensor
                def _(pe):
                    for t in range(TT):
                        for g in range(4):
                            last = nc.tensor.matmul(ps[:, t, g * P:(g + 1) * P], k["w_sT"][:, g, :],
                                                    gv[:, t, g * P:(g + 1) * P], start=True, stop=True)
                        last.then_inc(full, 1)

                @block.vector
                def _(dve):
                    for t in range(TT):
                        dve.wait_ge(full, t + 1)
                        for g in range(4):
                            cs = slice(g * P, (g + 1) * P)
                            vec.scalar_tensor_tensor(y[:, t, 512 + g * P:512 + (g + 1) * P], ps[:, t, cs],
                                                     col("b_s")[:, g:g + 1], gu[:, t, cs], ALU.add, ALU.mult)
        project_onto(nc, "mixo", k, hT, i["w_out"][0], x, 1.0,
                     TurnSplit(nc, k, TT, lambda t, c: y[:, t, c * P:(c + 1) * P], hT, DC))


def project_onto(nc, name, k, hT, w, x, alpha, before):
    chunks = [chunk_of(w, a, a + WIDTH) for a in range(0, D, WIDTH)]
    items = []
    for c in range(D // WIDTH):
        for t in range(TT):
            xs = x[:, t, c * WIDTH:(c + 1) * WIDTH]
            items.append(by_token(c, hT, t, 0, WIDTH, "dve", lambda eng, src, xs=xs: eng.scalar_tensor_tensor(
                xs, xs, alpha, src, ALU.mult, ALU.add)))
    dense(nc, name, k, chunks, items, before=before)


def cross_attention(nc, k, x, col, i):
    MT = i["mem"].shape[1] // P
    M = MT * P
    with Stage(nc, "xa") as sx:
        h = sx.sb("h", [P, TT, D])
        qT = sx.sb("qT", [P, DC, S])
        kT = sx.sb("kT", [P, DC, M])
        v = sx.sb("v", [P, MT, D])
        hT = sx.sb("hT", [P, 2, DC, S], F32R)
        mT = sx.sb("mT", [P, 2, DC, M], F32R)
        m = sx.sb("m", [P, MT, D])
        rms_rows(nc, "xan", [(lambda t: x[:, t, :], lambda t: h[:, t, :], TT, D)], 1e-6,
                 [(m[:], i["mem"][0].rearrange("(t p) d -> p t d", p=P))])
        rms_rows(nc, "xam", [(lambda t: m[:, t, :], lambda t: m[:, t, :], MT, D)], 1e-6)
        turn_split(nc, "xat", k, MT, lambda t, c: m[:, t, c * P:(c + 1) * P], mT, DC, col("g_mem"))
        wq, wkv = i["w_q_x"][0], i["w_kv_x"][0]
        chunks = [chunk_of(wq, a, a + WIDTH) for a in range(0, D, WIDTH)]
        chunks += [chunk_of(wkv, a, a + WIDTH) for a in range(0, 2 * D, WIDTH)]
        items = []
        eng = lambda n: "act" if n % 2 else "dve"
        for c in range(4):
            for j in range(2):
                items.append(by_feature(c, hT, j * P, eng(j), plain(nc, qT[:, 2 * c + j, :])))
        for c in range(4):
            for j in range(2):
                items.append(by_feature(4 + c, mT, j * P, eng(j), plain(nc, kT[:, 2 * c + j, :]), n=M))
        for c in range(4):
            for t in range(MT):
                items.append(by_token(8 + c, mT, t, 0, WIDTH, eng(t), plain(nc, v[:, t, c * WIDTH:(c + 1) * WIDTH])))
        dense(nc, "xaw", k, chunks, items,
              before=TurnSplit(nc, k, TT, lambda t, c: h[:, t, c * P:(c + 1) * P], hT, DC, col("g_xattn")))
        units = [Unit(hd, t, 0, M, hd * TT + t) for hd in range(4) for t in range(TT)]
        attention(nc, "xaa", k, "softmax", units,
                  lambda hd, t: [qT[:, 2 * hd + j, t * P:(t + 1) * P] for j in range(2)],
                  lambda hd, lo, hi: [kT[:, 2 * hd + j, lo:hi] for j in range(2)],
                  lambda hd, c: v[:, c, hd * 256:(hd + 1) * 256], lambda hd, t: h[:, t, hd * 256:(hd + 1) * 256],
                  256, 256 ** -0.5)
        project_onto(nc, "xao", k, hT, i["w_o_x"][0], x, 1.0,
                     TurnSplit(nc, k, TT, lambda t, c: h[:, t, c * P:(c + 1) * P], hT, DC))


def rope_tables(nc, k, positions, cs):
    vec, sca = nc.vector, nc.scalar
    two_pi = 2 * np.pi
    c1 = float(np.float32(round(two_pi * 256) / 256))
    c2 = float(np.float32(round((two_pi - c1) * 2 ** 20) / 2 ** 20))
    c3 = float(np.float32(two_pi - c1 - c2))
    shift = 12582912.0
    with Stage(nc, "rope") as st:
        pi = st.sb("pi", [P, TT], I32)
        pf = st.sb("pf", [P, TT])
        ang = st.sb("ang", [P, 4, TT, 16])
        landed, chain, ready, sined = (st.sem(n) for n in ("landed", "dve_chain", "ready", "sined"))
        with nc.Block() as block:
            @block.sync
            def _(sp):
                sp.dma_start(pi[:], positions).then_inc(landed, 16)

            @block.vector
            def _(dve):
                link = Chain(dve, chain)
                dve.wait_ge(landed, 16)
                link(vec.tensor_copy(pf[:], pi[:]))
                link(vec.tensor_tensor(ang[:, 0], pf[:].unsqueeze(2).to_broadcast([P, TT, 16]),
                                       k["rows"]["inv_freq"].unsqueeze(1).to_broadcast([P, TT, 16]), ALU.mult))
                link(vec.tensor_scalar(ang[:, 1], ang[:, 0], float(1 / two_pi), shift, ALU.mult, ALU.add))
                link(vec.tensor_scalar(ang[:, 1], ang[:, 1], -shift, None, ALU.add))
                for c in (c1, c2, c3):
                    link(vec.scalar_tensor_tensor(ang[:, 0], ang[:, 1], -c, ang[:, 0], ALU.mult, ALU.add))
                link(vec.tensor_scalar(ang[:, 0], ang[:, 0], float(np.float32(3.141592)), float(np.float32(-3.141592)),
                                       ALU.min, ALU.max))
                link(vec.scalar_tensor_tensor(ang[:, 2], ang[:, 0], -1.0, ang[:, 0], ALU.mult, ALU.min))
                vec.tensor_scalar(ang[:, 3], ang[:, 2], float(np.pi / 2), None, ALU.add).then_inc(ready, 1)

            @block.scalar
            def _(act):
                act.wait_ge(ready, 1)
                sca.activation(cs[:, 0], ang[:, 3], ACT.Sin)
                sca.activation(cs[:, 1], ang[:, 0], ACT.Sin)


def token_mixer(nc, name, k, x, col, i, l):
    ps, vec, sca = k["ps"], nc.vector, nc.scalar
    alpha = (2.0 * 2) ** 0.25
    H = 4
    with Stage(nc, name) as sx:
        ys = sx.sb("ys", [P, TT, 256])
        hT = sx.sb("hT", [P, 2, DC, S], F32R)
        merged = sx.sb("merged", [P, DC, S])
        with Stage(nc, name + "a") as sa:
            za = sa.sb("za", [P, TT, 416])
            sbqk = sa.sb("sbqk", [P, 4, S])
            sbv = sa.sb("sbv", [P, TT, 256])
            fxqk = sa.sb("fxqk", [P, 4, S])
            fxv = sa.sb("fxv", [P, TT, 256])
            fxf = sa.sb("fxf", [P, TT, 4])
            with Stage(nc, name + "v") as sc:
                ca = sc.sb("ca", [P, 2, S + 30])
                cg = sc.sb("cg", [P, 2, S])
                acc = sc.sb("acc", [P, 2, S])
                ready, tapped = sc.sem("conv_ready"), sc.sem("tapped")
                w = i["w_in_2"][l]
                spans = ((1184, 1440), (1440, 1696), (0, 256), (256, 416), (416, 672), (672, 928), (928, 1184),
                         (1696, 1952), (1952, 2208), (2208, 2468))
                chunks = [chunk_of(w, a, b) for a, b in spans]
                eng = lambda n: "act" if n % 2 else "dve"
                items = []
                for j in range(2):
                    items.append(by_feature(0, hT, j * P, "dve", plain(nc, ca[:, j, 30:])))
                for j in range(2):
                    items.append(by_feature(1, hT, j * P, "act", lambda e, src, j=j: e.activation(cg[:, j, :], src, ACT.Sigmoid)))
                for t in range(TT):
                    items.append(by_token(2, hT, t, 0, 256, eng(t), plain(nc, za[:, t, 0:256])))
                for t in range(TT):
                    items.append(by_token(3, hT, t, 0, 160, eng(t), plain(nc, za[:, t, 256:416])))
                for j in range(2):
                    items.append(by_feature(4, hT, j * P, eng(j), lambda e, src, j=j: e.tensor_scalar(
                        sbqk[:, j, :], src, 64 ** -0.5, None, ALU.mult) if e is nc.vector else e.activation(
                        sbqk[:, j, :], src, ACT.Identity, scale=64 ** -0.5)))
                for j in range(2):
                    items.append(by_feature(5, hT, j * P, eng(j), plain(nc, sbqk[:, 2 + j, :])))
                for t in range(TT):
                    items.append(by_token(6, hT, t, 0, 256, eng(t), plain(nc, sbv[:, t, :])))
                for c in range(2):
                    for j in range(2):
                        items.append(by_feature(7 + c, hT, j * P, eng(j), plain(nc, fxqk[:, 2 * c + j, :])))

                def values_and_forget(t):
                    def out(e, src):
                        e.tensor_copy(fxv[:, t, :], src[:, 0:256])
                        return e.tensor_tensor(fxf[:, t, :], src[:, 256:260], k["rows"][f"b_forget{l}"], ALU.add)
                    return out

                for t in range(TT):
                    items.append(by_token(9, hT, t, 0, 260, "dve", values_and_forget(t)))

                def taps(dve, c, emptied):
                    if c == 0:
                        vec.memset(ca[:, :, 0:30], 0.0)
                    if c < 2:
                        return
                    if c == 2:
                        dve.wait_ge(emptied["dve"], 2)
                        dve.wait_ge(emptied["act"], 2)
                        vec.tensor_tensor(ca[:, :, 30:], ca[:, :, 30:], cg[:], ALU.mult).then_inc(ready, 1)
                        dve.wait_ge(ready, 1)
                    for j in range((c - 2) * 4, min(31, (c - 1) * 4)):
                        for q in range(2):
                            wj = col(f"conv_w2{l}")[:, 2 * j + q:2 * j + q + 1]
                            src = ca[:, q, j:j + S]
                            if j == 0:
                                vec.tensor_scalar(acc[:, q, :], src, wj, col(f"conv_b2{l}")[:, q:q + 1], ALU.mult,
                                                  ALU.add).then_inc(tapped, 1)
                            else:
                                dve.wait_ge(tapped, 2 * (j - 1) + q + 1)
                                vec.scalar_tensor_tensor(acc[:, q, :], src, wj, acc[:, q, :], ALU.mult,
                                                         ALU.add).then_inc(tapped, 1)

                dense(nc, name + "w", k, chunks, items, side=taps,
                      before=TurnSplit(nc, k, TT, lambda t, c: x[:, t, c * P:(c + 1) * P], hT, DC))

                with Stage(nc, name + "c") as st:
                    cn = st.sb("cn", [P, TT, 256])
                    full = st.sem("bank_full")
                    with nc.Block() as block:
                        @block.tensor
                        def _(pe):
                            for t in range(TT):
                                for c in range(2):
                                    last = nc.tensor.transpose(ps[:, t, c * P:(c + 1) * P], acc[:, c, t * P:(t + 1) * P], k["ident"][:])
                            last.then_inc(full, 1)

                        @block.vector
                        def _(dve):
                            dve.wait_ge(full, 1)
                            vec.tensor_copy(cn[:], ps[:, 0:TT, 0:256])
                    ln_rows(nc, name + "cl", lambda t: cn[:, t, :], lambda t: ys[:, t, :], TT, 256, 1e-5)
            branches = GatedBranches(nc, name + "g", k, sa, hT, merged, w[:, 2468:], i["w_branch_2"][l],
                                     k["half_b_gate"][:, l * 32:(l + 1) * 32], k["minus_b_gate"][:, l * DC:(l + 1) * DC])
            branches.turn_conv(name + "ct", ys, col(f"ln_g2{l}"), col(f"ln_b2{l}"))

            with Stage(nc, name + "m") as sm:
                v = sm.sb("v", [P, TT, H, 64])
                qkT = sm.sb("qkT", [96, 2 * H, S])
                with Stage(nc, name + "n") as sn:
                    cT = sn.sb("cT", [P, 3, S])
                    wuq = sn.sb("wuq", [P, 2, 384])
                    wukv = sn.sb("wukv", [P, 512])
                    spare = merged[:].rearrange("p c s -> p (c s)")
                    n_f, n_rot = TT * H * 96, 4 * TT * H * 16
                    qf = spare[:, 0:n_f].rearrange("p (t h d) -> p t h d", t=TT, h=H)
                    kf = spare[:, n_f:2 * n_f].rearrange("p (t h d) -> p t h d", t=TT, h=H)
                    rot = spare[:, 2 * n_f:2 * n_f + n_rot].rearrange("p (q t h d) -> p q t h d", q=4, t=TT, h=H)
                    rms_rows(nc, name + "mq", [(lambda t: za[:, t, 0:256], lambda t: za[:, t, 0:256], TT, 256),
                                               (lambda t: za[:, t, 256:384], lambda t: za[:, t, 256:384], TT, 128)], 1e-5,
                             [(wuq[:], i["mla_w_uq_2"][l].rearrange("(c p) n -> p c n", p=P)),
                              (wukv[:], i["mla_w_ukv_2"][l])])
                    turn(nc, name + "mt", k, TT, lambda t, c: za[:, t, c * P:(c + 1) * P],
                         [plain(nc, cT[:, c, :], (col(f"q_norm{l}")[:, c:c + 1] if c < 2 else col(f"kv_norm{l}"))) for c in range(3)])
                    with Stage(nc, name + "mu") as st:
                        full, q_out, chain = st.sem("bank_full"), st.sem("q_out"), st.sem("dve_chain")
                        with nc.Block() as block:
                            @block.tensor
                            def _(pe):
                                for t in range(TT):
                                    for c in range(2):
                                        last = nc.tensor.matmul(ps[:, t, 0:384], cT[:, c, t * P:(t + 1) * P], wuq[:, c, :],
                                                                start=c == 0, stop=c == 1)
                                    last.then_inc(full, 1)
                                for t in range(TT):
                                    nc.tensor.matmul(ps[:, 4 + t, :], cT[:, 2, t * P:(t + 1) * P], wukv[:],
                                                     start=True, stop=True).then_inc(full, 1)

                            @block.scalar
                            def _(act):
                                act.wait_ge(full, TT)
                                for t in range(TT):
                                    last = sca.activation(qf[:, t], ps[:, t, 0:384].rearrange("p (h d) -> p h d", h=H), ACT.Identity)
                                last.then_inc(q_out, 1)
                                for t in range(TT):
                                    act.wait_ge(full, TT + t + 1)
                                    kv = ps[:, 4 + t, :].rearrange("p (h d) -> p h d", h=H)
                                    sca.activation(kf[:, t, :, 0:64], kv[:, :, 0:64], ACT.Identity)
                                    sca.activation(v[:, t], kv[:, :, 64:], ACT.Identity)

                            @block.vector
                            def _(dve):
                                link = Chain(dve, chain)

                                def rotate(src, heads, write):
                                    x1, x2 = src(0), src(16)
                                    cs = [k["cs"][:, j].unsqueeze(2).to_broadcast([P, TT, heads, 16]) if heads > 1 else k["cs"][:, j]
                                          for j in range(2)]
                                    r = [rot[:, j] if heads > 1 else rot[:, j, :, 0, :] for j in range(4)]
                                    vec.tensor_tensor(r[0], x1, cs[0], ALU.mult)
                                    vec.tensor_tensor(r[1], x2, cs[1], ALU.mult)
                                    vec.tensor_tensor(r[2], x2, cs[0], ALU.mult)
                                    link(vec.tensor_tensor(r[3], x1, cs[1], ALU.mult))
                                    write(r)

                                def write_k(r):
                                    for h in range(H):
                                        vec.tensor_tensor(kf[:, :, h, 64:80], r[0], r[1], ALU.subtract)
                                        last = vec.tensor_tensor(kf[:, :, h, 80:96], r[2], r[3], ALU.add)
                                    link(last)

                                def write_q(r):
                                    vec.tensor_tensor(qf[:, :, :, 64:80], r[0], r[1], ALU.subtract)
                                    vec.tensor_tensor(qf[:, :, :, 80:96], r[2], r[3], ALU.add)

                                rotate(lambda a: za[:, :, 384 + a:400 + a], 1, write_k)
                                dve.wait_ge(q_out, 1)
                                rotate(lambda a: qf[:, :, :, 64 + a:80 + a], H, write_q)
                    with Stage(nc, name + "mv") as st:
                        full = st.sem("bank_full")
                        with nc.Block() as block:
                            @block.tensor
                            def _(pe):
                                for j in range(2 * H):
                                    src = (qf if j < H else kf)
                                    for t in range(TT):
                                        last = nc.tensor.transpose(ps[0:96, j, t * P:(t + 1) * P], src[:, t, j % H, :], k["ident"][:])
                                    last.then_inc(full, 1)

                            @block.scalar
                            def _(act):
                                for j in range(0, 2 * H, 2):
                                    act.wait_ge(full, j + 1)
                                    sca.activation(qkT[:, j, :], ps[0:96, j, :], ACT.Identity)

                            @block.vector
                            def _(dve):
                                for j in range(1, 2 * H, 2):
                                    dve.wait_ge(full, j + 1)
                                    vec.tensor_copy(qkT[:, j, :], ps[0:96, j, :])
                attention(nc, name + "ma", k, "softmax", causal_units(k["mask_le"]),
                          lambda h, t: qkT[:, h, t * P:(t + 1) * P], lambda h, lo, hi: qkT[:, H + h, lo:hi],
                          lambda h, c: v[:, c, h, :], lambda h, t: ys[:, t, h * 64:(h + 1) * 64], 64, 96 ** -0.5, branches)

            branches.turn_branch(name + "mx", ys)

            def half(buf, j0):
                return lambda h, lo, hi: buf[64 * (h % 2):64 * (h % 2) + 64, j0 + h // 2, lo:hi]

            attention(nc, name + "sa", k, "stick", causal_units(k["mask_lt"]),
                      lambda h, t: half(sbqk, 0)(h, t * P, (t + 1) * P), half(sbqk, 2),
                      lambda h, c: sbv[:, c, h * 64:(h + 1) * 64], lambda h, t: ys[:, t, h * 64:(h + 1) * 64],
                      64, 1.0, branches)
            branches.turn_branch(name + "sx", ys)
            with Stage(nc, name + "f") as sf:
                b = sf.sb("b", [P, TT, 4])
                r = sf.sb("r", [P, TT, 4])
                rows = sf.sb("rows", [P, 4, S])
                running_log_sigmoid(nc, name + "fs", k, fxf[:], 4, 4, b[:])
                with nc.Block() as block:
                    @block.vector
                    def _(dve):
                        vec.tensor_scalar(r[:], b[:], -1.0, None, ALU.mult)
                spread_rows(nc, name + "fr", k, r, 4, rows)
                attention(nc, name + "fa", k, "decayed", causal_units(k["mask_le"], lambda h: rows[:, h, :]),
                          lambda h, t: half(fxqk, 0)(h, t * P, (t + 1) * P), half(fxqk, 2),
                          lambda h, c: fxv[:, c, h * 64:(h + 1) * 64], lambda h, t: ys[:, t, h * 64:(h + 1) * 64],
                          64, 64 ** -0.5, branches)
            branches.turn_branch(name + "fx", ys)
            branches.finish()
        project_onto(nc, name + "o", k, hT, i["w_o_2"][l], x, alpha, Split(nc, merged, hT, 0.5))


class GatedBranches:

    ORDER = (2, 0, 1, 3)
    RAW, SPLIT = 3, 2

    def __init__(self, nc, name, k, st, hT, merged, w_gates, w_branch, half_b, minus_b):
        self.nc, self.name, self.k, self.hT, self.merged = nc, name, k, hT, merged
        self.half_b, self.minus_b = half_b, minus_b
        self.units = 4 * DC
        self.w_gates = w_gates.rearrange("(c p) n -> p c n", p=P)
        self.w_branch = w_branch.rearrange("n (c p) d -> n p c d", p=P)
        self.raw = st.sb(name + "_raw", [P, self.RAW, DC + 2, P])
        self.w = st.sb(name + "_w", [P, self.SPLIT, 2, DC + 2, P], F32R)
        self.yT = st.sb(name + "_yT", [P, 2, 2, S], F32R)
        self.sg = st.sb(name + "_sg", [P, 2, S])
        self.gp = st.sb(name + "_gp", [P, S])
        self.landed = [st.sem(f"{name}_landed{n}") for n in range(self.RAW)]
        (self.high_ready, self.low_ready, self.gate_full, self.proj_full, self.gate_ready, self.dve_chain,
         self.merged_ready) = (st.sem(f"{name}_{n}") for n in
                               ("high_ready", "low_ready", "gate_full", "proj_full", "gate_ready", "dve_chain", "merged_ready"))
        self.next = {"pe": 0, "act": 0, "dve": 0, "high": 0, "low": 0}
        self.target = 0
        self.chained = self.act_chained = 0
        self.by_log = range(DC, 2 * DC)
        self.act_chain = st.sem(name + "_act_chain")

    def share(self, step, steps):
        return 3 * self.target + min(24, max(0, int((step + 1) * 24 / steps)))

    def load(self, sp, u):
        b, a = self.ORDER[u // DC], u % DC * P
        slot = u % self.RAW
        if u >= self.RAW:
            sp.wait_ge(self.low_ready, u - self.RAW + 1)
        sp.dma_start(self.raw[:, slot, 0:DC], self.w_gates[:, :, b * D + a:b * D + a + P]).then_inc(self.landed[slot], 16)
        sp.dma_start(self.raw[:, slot, DC:], self.w_branch[b, :, :, a:a + P]).then_inc(self.landed[slot], 16)

    def load_first(self, sp):
        for u in range(self.RAW):
            self.load(sp, u)

    def load_on(self, sp):
        for u in range(self.target + self.RAW, min(self.target + self.RAW + 8, self.units)):
            self.load(sp, u)

    def pe_steps(self, pe, until):
        ps, nc = self.k["ps"], self.nc
        for piece in range(self.next["pe"], until):
            u, part = piece // 3, piece % 3
            w = self.w[:, u % self.SPLIT]
            if part == 0:
                pe.wait_ge(self.low_ready, u + 1)
                if u:
                    pe.wait_ge(self.gate_ready, u)
            if part < 2:
                for q in range(part * DC // 2, (part + 1) * DC // 2):
                    for p, r in PARTS:
                        last = nc.tensor.matmul(ps[:, 6, :], w[:, p, q, :], self.hT[:, r, q, :],
                                                start=q == 0 and p == r, stop=q == DC - 1 and p == LO)
                if part == 1:
                    last.then_inc(self.gate_full, 1)
                continue
            if u:
                pe.wait_ge(self.merged_ready, u)
            for q in range(2):
                for p, r in PARTS:
                    last = nc.tensor.matmul(ps[:, 7, :], w[:, p, DC + q, :], self.yT[:, r, q, :],
                                            start=q == 0 and p == r, stop=q == 1 and p == LO)
            last.then_inc(self.proj_full, 1)
        self.next["pe"] = max(until, self.next["pe"])

    def high(self, act, u):
        act.wait_ge(self.landed[u % self.RAW], 32 * (u // self.RAW + 1))
        if u >= self.SPLIT:
            act.wait_ge(self.proj_full, u - self.SPLIT + 1)
        self.nc.scalar.copy(self.w[:, u % self.SPLIT, HI], self.raw[:, u % self.RAW]).then_inc(self.high_ready, 1)

    def low(self, dve, u):
        dve.wait_ge(self.high_ready, u + 1)
        self.nc.vector.tensor_tensor(self.w[:, u % self.SPLIT, LO], self.raw[:, u % self.RAW],
                                     self.w[:, u % self.SPLIT, HI], ALU.subtract).then_inc(self.low_ready, 1)

    def splits(self, engine, which, pieces):
        for u in range(self.next[which], min(pieces // 3 + self.SPLIT, self.units)):
            (self.high if which == "high" else self.low)(engine, u)
            self.next[which] = u + 1

    def act_steps(self, act, pieces):
        until = (pieces + 1) // 3
        for u in range(self.next["act"], until):
            g = self.ORDER[u // 8] * DC + u % 8
            act.wait_ge(self.gate_full, u + 1)
            if u >= 2:
                act.wait_ge(self.merged_ready, u - 1)
            sg, z, sca = self.sg[:, u % 2, :], self.k["ps"][:, 6, :], self.nc.scalar
            if u in self.by_log:
                for out, src, func, kw in ((sg, z, ACT.Exp, dict(scale=-1.0, bias=self.minus_b[:, u % DC:u % DC + 1])),
                                           (sg, sg, ACT.Ln, dict(bias=1.0))):
                    self.act_chained += 1
                    sca.activation(out, src, func, **kw).then_inc(self.act_chain, 1)
                    act.wait_ge(self.act_chain, self.act_chained)
                sca.activation(sg, sg, ACT.Exp, scale=-1.0).then_inc(self.gate_ready, 1)
            else:
                sca.activation(sg, z, ACT.Tanh, scale=0.5, bias=self.half_b[:, g:g + 1]).then_inc(self.gate_ready, 1)
        self.next["act"] = max(until, self.next["act"])

    def dve_steps(self, dve, pieces):
        until = pieces // 3
        vec = self.nc.vector

        def link(instruction):
            self.chained += 1
            instruction.then_inc(self.dve_chain, 1)
            dve.wait_ge(self.dve_chain, self.chained)

        for u in range(self.next["dve"], until):
            sg, dst = self.sg[:, u % 2, :], self.merged[:, u % 8, :]
            form = (2.0, self.k["ps"][:, 7, :], ALU.mult, ALU.mult) if u in self.by_log else (
                1.0, self.k["ps"][:, 7, :], ALU.add, ALU.mult)
            dve.wait_ge(self.gate_ready, u + 1)
            dve.wait_ge(self.proj_full, u + 1)
            if u < 8:
                vec.scalar_tensor_tensor(dst, sg, *form).then_inc(self.merged_ready, 1)
            else:
                link(vec.scalar_tensor_tensor(self.gp[:], sg, *form))
                vec.tensor_tensor(dst, dst, self.gp[:], ALU.add).then_inc(self.merged_ready, 1)
        self.next["dve"] = max(until, self.next["dve"])

    def begin(self):
        self.target = self.next["pe"] // 3

    def turn_conv(self, name, ys, gain, bias):
        nc, ps = self.nc, self.k["ps"]
        with Stage(nc, name) as st:
            silu = st.sb("silu", [P, 2, S])
            full, silu_ready, high_ready = st.sem("bank_full"), st.sem("silu_ready"), st.sem("high_ready")
            with nc.Block() as block:
                @block.sync
                def _(sp):
                    self.load_first(sp)

                @block.tensor
                def _(pe):
                    for c in range(2):
                        for t in range(TT):
                            last = nc.tensor.transpose(ps[:, c, t * P:(t + 1) * P], ys[:, t, c * P:(c + 1) * P],
                                                       self.k["ident"][:])
                        last.then_inc(full, 1)

                @block.scalar
                def _(act):
                    for c in range(2):
                        act.wait_ge(full, c + 1)
                        nc.scalar.activation(silu[:, c, :], ps[:, c, :], ACT.Silu, scale=gain[:, c:c + 1],
                                             bias=bias[:, c:c + 1]).then_inc(silu_ready, 1)
                    act.wait_ge(silu_ready, 2)
                    nc.scalar.copy(self.yT[:, HI], silu[:]).then_inc(high_ready, 1)

                @block.vector
                def _(dve):
                    dve.wait_ge(high_ready, 1)
                    nc.vector.tensor_tensor(self.yT[:, LO], silu[:], self.yT[:, HI], ALU.subtract)

    def turn_branch(self, name, ys):
        turn_split(self.nc, name, self.k, TT, lambda t, c: ys[:, t, c * P:(c + 1) * P], self.yT, 2)

    def finish(self):
        self.begin()
        with self.nc.Block() as block:
            @block.sync
            def _(sp):
                self.load_on(sp)

            @block.tensor
            def _(pe):
                self.pe_steps(pe, 3 * self.units)

            @block.scalar
            def _(act):
                for u in range(self.target, self.units):
                    self.splits(act, "high", 3 * u)
                    self.act_steps(act, 3 * u + 3)

            @block.vector
            def _(dve):
                for u in range(self.target, self.units):
                    self.splits(dve, "low", 3 * u)
                    self.dve_steps(dve, 3 * u + 3)


def program(nc, i, out, dump=None):
    with ExitStack() as ctx:
        ps = ctx.enter_context(nc.psum_tensor("ps", [P, 8, 512], F32))
        with Stage(nc, "all") as st:
            x = st.sb("x", [P, TT, D])
            k = constants(nc, st, ps)
            columns = st.sb("columns", [P, COLS.width])
            small = st.sb("small", [P, 16 + 16 + 8])
            cs = st.sb("cs", [P, 2, TT, 16])
            k["cs"] = cs
            k["rows"] = {"gate_b": small[:, 0:16], "inv_freq": small[:, 16:32], "b_forget0": small[:, 32:36],
                         "b_forget1": small[:, 36:40]}
            col = lambda n: columns[:, COLS.at[n][0]:COLS.at[n][1]]

            def row(n):
                a, b = ROWS_.at[n]
                return i["rows"][a:b].partition_broadcast(P)

            def gain_row(n):
                a, b = ROWS_.at[n]
                return i["rows"][a:b]

            load(nc, "ld", [(x[:], i["x"][0].rearrange("(t p) d -> p t d", p=P)), (columns[:], i["columns"])]
                 + [(k["rows"][n], row(n)) for n in k["rows"]])
            k["half_b_gate"] = st.sb("half_b_gate", [P, 64])
            k["minus_b_gate"] = st.sb("minus_b_gate", [P, 2 * DC])
            with nc.Block() as block:
                @block.vector
                def _(dve):
                    for l in range(2):
                        for n, w, factor in (("half_b_gate", 32, 0.5), ("minus_b_gate", DC, -1.0)):
                            nc.vector.tensor_scalar(k[n][:, l * w:(l + 1) * w], col(f"b_gate{l}")[:, 0:w], factor, None,
                                                    ALU.mult)
            rope_tables(nc, k, i["positions"], cs)
            with Stage(nc, "m1") as s1:
                w_sT = s1.sb("w_sT", [P, 4, P])
                g_head = s1.sb("g_head", [P, 512])
                ln_v = s1.sb("ln_v", [P, 2, 512])
                k["mixer_loads"] = [(w_sT[:], i["w_sT"]), (g_head[:], row("g_head")), (ln_v[:, 0], row("ln_v_g")),
                                    (ln_v[:, 1], row("ln_v_b"))]
                k["w_sT"], k["ln_v"] = w_sT, ln_v
                k["rows"]["g_head"] = g_head[:]
                mixer_one(nc, k, x, col, i)
            dump and dump("mix", x)
            cross_attention(nc, k, x, col, i)
            dump and dump("xa", x)
            with Stage(nc, "m3") as s3:
                h = s3.sb("h", [P, TT, D])
                hT = s3.sb("hT", [P, DC, S])
                rms_rows(nc, "m3n", [(lambda t: x[:, t, :], lambda t: h[:, t, :], TT, D)], 1e-6)
                turn(nc, "m3t", k, TT, lambda t, c: h[:, t, c * P:(c + 1) * P],
                     [plain(nc, hT[:, c, :], col("g_moe")[:, c:c + 1]) for c in range(DC)])
                moe(nc, "e0", k, x, hT, h[:], col("g_moe"), i["w_rg"][0], i["b_rg"][0], i["w_re"][0], i["b_re"][0],
                    i["w_gate"][0], i["w_up"][0], i["w_down"][0])
            final_norm(nc, "m4", x, gain_row("g_final"), 1e-6)
            dump and dump("first", x)
            for l in range(2):
                token_mixer(nc, f"t{l}", k, x, col, i, l)
                dump and dump(f"tm{l}", x)
                with Stage(nc, f"r{l}") as sr:
                    hT = sr.sb("hT", [P, DC, S])
                    post_norm(nc, f"ln{l}1", k, x, gain_row(f"ln1_g{l}"), gain_row(f"ln1_b{l}"), 1e-5, hT)
                    dump and dump(f"ln{l}1", x)
                    moe(nc, f"e{l + 1}", k, x, hT, x[:], None, i["w_router_group_2"][l], i["b_router_group_2"][l],
                        i["w_router_expert_2"][l], i["b_router_expert_2"][l], i["w_exp_gate_2"][l],
                        i["w_exp_up_2"][l], i["w_exp_down_2"][l], (2.0 * 2) ** 0.25)
                post_norm(nc, f"ln{l}2", k, x, gain_row(f"ln2_g{l}"), gain_row(f"ln2_b{l}"), 1e-5)
                dump and dump(f"ln{l}2", x)
            with Stage(nc, "end") as se:
                stored = se.sem("stored")
                with nc.Block() as block:
                    @block.sync
                    def _(sp):
                        sp.dma_start(out[0].rearrange("(t p) d -> p t d", p=P), x[:]).then_inc(stored, 16)
                        sp.wait_ge(stored, 16)


def columns_of(inputs):
    def cols_(v):
        return v.reshape(-1, P).T

    parts = {"g_mix": cols_(inputs["g_mix"]), "g_xattn": cols_(inputs["g_xattn"]), "g_mem": cols_(inputs["g_mem"]),
             "g_moe": cols_(inputs["g_moe"]), "conv_w": cols_(inputs["conv_w"]), "conv_b": cols_(inputs["conv_b"]),
             "b_s": inputs["b_s"][0].T}
    for l in range(2):
        for n, src in (("b_gate", "b_gate_2"), ("q_norm", "mla_q_norm_2"), ("kv_norm", "mla_kv_norm_2"),
                       ("conv_w2", "conv_w_2"), ("conv_b2", "conv_b_2"), ("ln_g2", "conv_ln_g_2"), ("ln_b2", "conv_ln_b_2")):
            parts[f"{n}{l}"] = cols_(inputs[src][l])
    return np.ascontiguousarray(np.concatenate([parts[n] for n in COLS.at], axis=1))


def rows_of(inputs):
    parts = {"gate_b": inputs["gate_b"][0], "g_head": inputs["g_head"][0], "ln_v_g": inputs["ln_v_g"][0],
             "ln_v_b": inputs["ln_v_b"][0], "g_final": inputs["g_final"],
             "inv_freq": (np.float32(10000.0) ** (-np.arange(16, dtype=np.float32) / np.float32(16))).astype(np.float32)}
    for l in range(2):
        for n, src in (("b_forget", "b_forget_2"), ("ln1_g", "ln1_g_2"), ("ln1_b", "ln1_b_2"), ("ln2_g", "ln2_g_2"),
                       ("ln2_b", "ln2_b_2")):
            parts[f"{n}{l}"] = inputs[src][l]
    return np.ascontiguousarray(np.concatenate([parts[n] for n in ROWS_.at]))


_DIRECT = ["x", "mem", "w_in", "w_out", "w_q_x", "w_kv_x", "w_o_x", "w_rg", "b_rg", "w_re", "b_re", "w_gate", "w_up",
           "w_down", "w_in_2", "mla_w_uq_2", "mla_w_ukv_2", "w_branch_2", "w_o_2", "w_router_group_2", "b_router_group_2",
           "w_router_expert_2", "b_router_expert_2", "w_exp_gate_2", "w_exp_up_2", "w_exp_down_2"]


def laid_out(inputs):
    arrays = {n: np.ascontiguousarray(inputs[n]) for n in _DIRECT}
    arrays["columns"] = columns_of(inputs)
    arrays["rows"] = rows_of(inputs)
    arrays["w_sT"] = np.ascontiguousarray(inputs["w_s"][0].transpose(2, 0, 1))
    arrays["positions"] = np.ascontiguousarray(inputs["positions_2"].reshape(TT, P).T)
    return arrays


def kernel(**inputs):
    from concourse import bacc
    from concourse.bass_utils import run_bass_kernel_spmd

    nc = bacc.Bacc("TRN2", target_bir_lowering=False, num_devices=1)
    inputs = {n: np.asarray(a) for n, a in inputs.items()}
    arrays, aps = {}, {}
    for n, a in laid_out(inputs).items():
        arrays[f"in_{n}"] = a
        aps[n] = nc.dram_tensor(f"in_{n}", a.shape, mybir.dt.from_np(a.dtype), kind="ExternalInput").ap()
    out = nc.dram_tensor("out_0", (1, S, D), F32, kind="ExternalOutput").ap()
    program(nc, aps, out)
    return run_bass_kernel_spmd(nc, [arrays], core_ids=[0]).results[0]["out_0"]
```
